# Optimizing a Trainium2 kernel written in Bass

```python
import jax, jax.numpy as jnp
from jax import lax
import numpy as np

D_MODEL = 1024
BATCH = 1
SEQ = 512
DEPTH = 2

N_MIXERS = 2
N_POOL_LAYERS = (DEPTH + N_MIXERS - 1) // N_MIXERS
N_MLA_LAYERS = DEPTH // N_MIXERS
EXPAND = 2
POOL_WIDTH = EXPAND * D_MODEL
POOL_WINDOWS = (2, 4, 8, 16)
N_POOL_GROUPS = len(POOL_WINDOWS)
POOL_GROUP = POOL_WIDTH // N_POOL_GROUPS
N_HEADS = 16
QK_NOPE_DIM = 128
QK_ROPE_DIM = 64
QK_HEAD_DIM = QK_NOPE_DIM + QK_ROPE_DIM
V_HEAD_DIM = 128
Q_LORA_RANK = 384
KV_LORA_RANK = 256
MLA_WIDTH = N_HEADS * V_HEAD_DIM
MLA_IN_WIDTH = Q_LORA_RANK + KV_LORA_RANK + QK_ROPE_DIM + MLA_WIDTH
ROPE_THETA = 10000.0
Q_BLOCK = 128
EPS = 1e-6


def rmsnorm(x, g):
    xf = x.astype(jnp.float32)
    inv = lax.rsqrt(jnp.mean(xf * xf, axis=-1, keepdims=True) + EPS)
    return (xf * inv).astype(x.dtype) * g

def causal_window_mean(u, w):
    S = u.shape[1]
    cs = jnp.cumsum(u.astype(jnp.float32), axis=1)
    shifted = jnp.pad(cs, ((0, 0), (w, 0), (0, 0)))[:, :S]
    count = jnp.minimum(jnp.arange(1, S + 1), w).astype(jnp.float32)
    return ((cs - shifted) / count[None, :, None]).astype(u.dtype)

def pool_layer(x, norm_g, w_in, w_group, scale, w_out):
    B, S, _ = x.shape
    h = rmsnorm(x, norm_g)
    uz = h @ w_in
    u, z = uz[..., :POOL_WIDTH], uz[..., POOL_WIDTH:]
    ug = u.reshape(B, S, N_POOL_GROUPS, POOL_GROUP)
    pooled = jnp.stack([causal_window_mean(ug[:, :, g], w)
                        for g, w in enumerate(POOL_WINDOWS)], axis=2) - ug
    mixed = jnp.einsum('bsgc,gcd->bsgd', pooled, w_group).reshape(B, S, POOL_WIDTH) * scale
    y = mixed * jax.nn.silu(z)
    return x + y @ w_out

def rope_tables(positions, dtype):
    inv_freq = 1.0 / (ROPE_THETA ** (jnp.arange(0, QK_ROPE_DIM, 2, dtype=jnp.float32) / QK_ROPE_DIM))
    ang = positions.astype(jnp.float32)[..., None] * inv_freq
    return jnp.cos(ang).astype(dtype), jnp.sin(ang).astype(dtype)

def apply_rope(t, cos, sin):
    half = QK_ROPE_DIM // 2
    t1, t2 = t[..., :half], t[..., half:]
    return jnp.concatenate([t1 * cos - t2 * sin, t2 * cos + t1 * sin], axis=-1)

def causal_mla_attention(q_nope, q_rope, k_nope, k_rope, v):
    B, S, H, _ = q_nope.shape
    nb = S // Q_BLOCK
    scale = QK_HEAD_DIM ** -0.5
    key_pos = jnp.arange(S)

    def to_blocks(t):
        return t.reshape(B, nb, Q_BLOCK, *t.shape[2:]).swapaxes(0, 1)

    def one_block(args):
        qn, qr, start = args
        s = (jnp.einsum('bqhd,bkhd->bhqk', qn, k_nope)
             + jnp.einsum('bqhr,bkr->bhqk', qr, k_rope)).astype(jnp.float32) * scale
        q_pos = start + jnp.arange(Q_BLOCK)
        mask = q_pos[:, None] >= key_pos[None, :]
        s = jnp.where(mask, s, jnp.finfo(jnp.float32).min)
        p = jax.nn.softmax(s, axis=-1).astype(v.dtype)
        return jnp.einsum('bhqk,bkhd->bqhd', p, v)

    starts = jnp.arange(nb, dtype=jnp.int32) * Q_BLOCK
    out = lax.map(one_block, (to_blocks(q_nope), to_blocks(q_rope), starts))
    return out.swapaxes(0, 1).reshape(B, S, H, V_HEAD_DIM)

def mla_layer(x, cos, sin, norm_g, w_in, q_norm_g, w_q_b, kv_norm_g, w_kv_b, w_out):
    B, S, _ = x.shape
    h = rmsnorm(x, norm_g)
    proj = h @ w_in
    o1 = Q_LORA_RANK
    o2 = o1 + KV_LORA_RANK
    o3 = o2 + QK_ROPE_DIM
    q_lat, kv_lat, k_rope, z = proj[..., :o1], proj[..., o1:o2], proj[..., o2:o3], proj[..., o3:]
    q = (rmsnorm(q_lat, q_norm_g) @ w_q_b).reshape(B, S, N_HEADS, QK_HEAD_DIM)
    q_nope, q_rope = q[..., :QK_NOPE_DIM], q[..., QK_NOPE_DIM:]
    kv = (rmsnorm(kv_lat, kv_norm_g) @ w_kv_b).reshape(B, S, N_HEADS, QK_NOPE_DIM + V_HEAD_DIM)
    k_nope, v = kv[..., :QK_NOPE_DIM], kv[..., QK_NOPE_DIM:]
    q_rope = apply_rope(q_rope, cos[:, :, None, :], sin[:, :, None, :])
    k_rope = apply_rope(k_rope, cos, sin)
    o = causal_mla_attention(q_nope, q_rope, k_nope, k_rope, v)
    y = o.reshape(B, S, MLA_WIDTH) * jax.nn.silu(z)
    return x + y @ w_out

def first_inputs(seed: int = 0) -> dict:
    key = jax.random.key(seed)
    ks = jax.random.split(key, 16)
    nrm = jax.random.normal
    Lp, Lm = N_POOL_LAYERS, N_MLA_LAYERS
    x = nrm(ks[0], (BATCH, SEQ, D_MODEL), jnp.float32)
    positions = jnp.broadcast_to(jnp.arange(SEQ, dtype=jnp.int32)[None, :], (BATCH, SEQ))
    return {
        "x": x,
        "positions": positions,
        "pool_norm": 1.0 + 0.02 * nrm(ks[1], (Lp, D_MODEL), jnp.float32),
        "pool_w_in": nrm(ks[2], (Lp, D_MODEL, 2 * POOL_WIDTH), jnp.float32) * D_MODEL ** -0.5,
        "pool_w_group": nrm(ks[3], (Lp, N_POOL_GROUPS, POOL_GROUP, POOL_GROUP), jnp.float32) * POOL_GROUP ** -0.5,
        "pool_scale": 1.0 + 0.02 * nrm(ks[4], (Lp, POOL_WIDTH), jnp.float32),
        "pool_w_out": nrm(ks[5], (Lp, POOL_WIDTH, D_MODEL), jnp.float32) * POOL_WIDTH ** -0.5,
        "mla_norm": 1.0 + 0.02 * nrm(ks[6], (Lm, D_MODEL), jnp.float32),
        "mla_w_in": nrm(ks[7], (Lm, D_MODEL, MLA_IN_WIDTH), jnp.float32) * D_MODEL ** -0.5,
        "mla_q_norm": 1.0 + 0.02 * nrm(ks[8], (Lm, Q_LORA_RANK), jnp.float32),
        "mla_w_q_b": nrm(ks[9], (Lm, Q_LORA_RANK, N_HEADS * QK_HEAD_DIM), jnp.float32) * Q_LORA_RANK ** -0.5,
        "mla_kv_norm": 1.0 + 0.02 * nrm(ks[10], (Lm, KV_LORA_RANK), jnp.float32),
        "mla_w_kv_b": nrm(ks[11], (Lm, KV_LORA_RANK, N_HEADS * (QK_NOPE_DIM + V_HEAD_DIM)), jnp.float32) * KV_LORA_RANK ** -0.5,
        "mla_w_out": nrm(ks[12], (Lm, MLA_WIDTH, D_MODEL), jnp.float32) * MLA_WIDTH ** -0.5,
        "final_norm": 1.0 + 0.02 * nrm(ks[13], (D_MODEL,), jnp.float32),
    }

def first_block(x, positions, pool_norm, pool_w_in, pool_w_group, pool_scale, pool_w_out,
              mla_norm, mla_w_in, mla_q_norm, mla_w_q_b, mla_kv_norm, mla_w_kv_b, mla_w_out,
              final_norm):
    cos, sin = rope_tables(positions, x.dtype)
    for i in range(DEPTH):
        j = i // N_MIXERS
        if i % N_MIXERS == 0:
            x = pool_layer(x, pool_norm[j], pool_w_in[j], pool_w_group[j], pool_scale[j], pool_w_out[j])
        else:
            x = mla_layer(x, cos, sin, mla_norm[j], mla_w_in[j], mla_q_norm[j], mla_w_q_b[j],
                          mla_kv_norm[j], mla_w_kv_b[j], mla_w_out[j])
    return rmsnorm(x, final_norm)


DEPTH_2 = 1

CHUNK = 64
SGU_CHUNK = 128
HEAD_DIM = 64
D_ATTN = D_MODEL // 2
N_ATTN_HEADS = D_ATTN // HEAD_DIM
D_SGU = D_MODEL // 2
SGU_GROUP_DIM = 64
N_SGU_GROUPS = D_SGU // SGU_GROUP_DIM
D_MIX = D_ATTN + D_SGU
D_IN = 3 * D_ATTN + N_ATTN_HEADS + 2 * D_SGU
D_FF = -(-8 * D_MODEL // (3 * 256)) * 256


def rms_norm(x, g):
    xf = x.astype(jnp.float32)
    y = xf * lax.rsqrt(jnp.mean(xf * xf, axis=-1, keepdims=True) + EPS)
    return (y * g.astype(jnp.float32)).astype(x.dtype)

def layer_norm(x, g, b):
    xf = x.astype(jnp.float32)
    mu = jnp.mean(xf, axis=-1, keepdims=True)
    xc = xf - mu
    y = xc * lax.rsqrt(jnp.mean(xc * xc, axis=-1, keepdims=True) + EPS)
    return (y * g.astype(jnp.float32) + b.astype(jnp.float32)).astype(x.dtype)

def forgetting_attention(q, k, v, log_f):
    B, S, H, Dh = q.shape
    nb = S // Q_BLOCK
    c_bhs = jnp.cumsum(log_f, axis=1).transpose(0, 2, 1)
    q_blocks = q.reshape(B, nb, Q_BLOCK, H, Dh).transpose(1, 0, 2, 3, 4)
    cq_blocks = c_bhs.reshape(B, H, nb, Q_BLOCK).transpose(2, 0, 1, 3)
    starts = jnp.arange(nb, dtype=jnp.int32) * Q_BLOCK
    key_pos = jnp.arange(S, dtype=jnp.int32)
    scale = Dh ** -0.5

    def one_block(args):
        qb, cqb, start = args
        s = jnp.einsum('bqhd,bkhd->bhqk', qb, k).astype(jnp.float32) * scale
        s = s + cqb[..., :, None] - c_bhs[..., None, :]
        q_pos = start + jnp.arange(Q_BLOCK, dtype=jnp.int32)
        causal = key_pos[None, :] <= q_pos[:, None]
        s = jnp.where(causal, s, -jnp.inf)
        p = jax.nn.softmax(s, axis=-1).astype(v.dtype)
        return jnp.einsum('bhqk,bkhd->bqhd', p, v)

    out = lax.map(one_block, (q_blocks, cq_blocks, starts))
    return out.transpose(1, 0, 2, 3, 4).reshape(B, S, H * Dh)

def spatial_gating(z, ln_g, ln_b, w_s, b_s):
    B, S, _ = z.shape
    zu, zv = jnp.split(z, 2, axis=-1)
    zv = layer_norm(zv, ln_g, ln_b)
    nc = S // SGU_CHUNK
    zv = zv.reshape(B, nc, SGU_CHUNK, N_SGU_GROUPS, SGU_GROUP_DIM)
    pos = jnp.arange(SGU_CHUNK, dtype=jnp.int32) // CHUNK
    mask = (pos[None, :] <= pos[:, None]).astype(w_s.dtype)
    w = w_s * mask[None]
    mixed = jnp.einsum('gij,bcjgd->bcigd', w, zv) + b_s.T[None, None, :, :, None]
    return zu * mixed.reshape(B, S, D_SGU)

def second_inputs(seed: int = 0) -> dict:
    key = jax.random.key(seed)
    ks = jax.random.split(key, 14)
    f32 = jnp.float32
    nrm = lambda k, shape, s: jax.random.normal(k, shape, f32) * s
    head_bias = jnp.linspace(1.0, 5.0, N_ATTN_HEADS, dtype=f32)
    return {
        'x': jax.random.normal(ks[0], (BATCH, SEQ, D_MODEL), f32),
        'mix_norm_g': 1.0 + nrm(ks[1], (DEPTH_2, D_MODEL), 0.05),
        'w_in': nrm(ks[2], (DEPTH_2, D_MODEL, D_IN), D_MODEL ** -0.5),
        'b_f': head_bias[None, :] + nrm(ks[3], (DEPTH_2, N_ATTN_HEADS), 0.1),
        'sgu_ln_g': 1.0 + nrm(ks[4], (DEPTH_2, D_SGU), 0.05),
        'sgu_ln_b': nrm(ks[5], (DEPTH_2, D_SGU), 0.02),
        'w_s': nrm(ks[6], (DEPTH_2, N_SGU_GROUPS, SGU_CHUNK, SGU_CHUNK), 0.5 * SGU_CHUNK ** -0.5),
        'b_s': 1.0 + nrm(ks[7], (DEPTH_2, N_SGU_GROUPS, SGU_CHUNK), 0.1),
        'out_norm_g': 1.0 + nrm(ks[8], (DEPTH_2, D_MIX), 0.05),
        'w_out': nrm(ks[9], (DEPTH_2, D_MIX, D_MODEL), D_MIX ** -0.5),
        'ffn_norm_g': 1.0 + nrm(ks[10], (DEPTH_2, D_MODEL), 0.05),
        'w_gate_up': nrm(ks[11], (DEPTH_2, D_MODEL, 2 * D_FF), D_MODEL ** -0.5),
        'w_down': nrm(ks[12], (DEPTH_2, D_FF, D_MODEL), D_FF ** -0.5),
        'final_norm_g': 1.0 + nrm(ks[13], (D_MODEL,), 0.05),
    }

def second_block(x, mix_norm_g, w_in, b_f, sgu_ln_g, sgu_ln_b, w_s, b_s, out_norm_g, w_out,
              ffn_norm_g, w_gate_up, w_down, final_norm_g):
    B, S, _ = x.shape
    for l in range(DEPTH_2):
        xn = rms_norm(x, mix_norm_g[l])
        h = xn @ w_in[l]
        q, k, v, f_logit, z = jnp.split(
            h, [D_ATTN, 2 * D_ATTN, 3 * D_ATTN, 3 * D_ATTN + N_ATTN_HEADS], axis=-1)
        q = q.reshape(B, S, N_ATTN_HEADS, HEAD_DIM)
        k = k.reshape(B, S, N_ATTN_HEADS, HEAD_DIM)
        v = v.reshape(B, S, N_ATTN_HEADS, HEAD_DIM)
        log_f = jax.nn.log_sigmoid(f_logit.astype(jnp.float32) + b_f[l].astype(jnp.float32))
        attn = forgetting_attention(q, k, v, log_f)
        sgu = spatial_gating(jax.nn.gelu(z, approximate=False),
                             sgu_ln_g[l], sgu_ln_b[l], w_s[l], b_s[l])
        merged = jnp.concatenate(
            [rms_norm(attn, out_norm_g[l, :D_ATTN]), rms_norm(sgu, out_norm_g[l, D_ATTN:])], axis=-1)
        x = x + merged @ w_out[l]
        xn = rms_norm(x, ffn_norm_g[l])
        gate, up = jnp.split(xn @ w_gate_up[l], 2, axis=-1)
        x = x + (jax.nn.silu(gate) * up) @ w_down[l]
    return rms_norm(x, final_norm_g)


def setup_inputs(seed=0):
    out = dict(first_inputs(seed))
    for name, value in second_inputs(seed + 1).items():
        if name != "x":
            out[name + "_2"] = value
    return out


def reference(
    x, positions, pool_norm, pool_w_in, pool_w_group, pool_scale, pool_w_out, mla_norm,
    mla_w_in, mla_q_norm, mla_w_q_b, mla_kv_norm, mla_w_kv_b, mla_w_out, final_norm,
    mix_norm_g_2, w_in_2, b_f_2, sgu_ln_g_2, sgu_ln_b_2, w_s_2, b_s_2, out_norm_g_2, w_out_2,
    ffn_norm_g_2, w_gate_up_2, w_down_2, final_norm_g_2,
):
    x = first_block(
        x, positions, pool_norm, pool_w_in, pool_w_group, pool_scale, pool_w_out, mla_norm,
        mla_w_in, mla_q_norm, mla_w_q_b, mla_kv_norm, mla_w_kv_b, mla_w_out, final_norm,
    )
    return second_block(
        x, mix_norm_g_2, w_in_2, b_f_2, sgu_ln_g_2, sgu_ln_b_2, w_s_2, b_s_2, out_norm_g_2,
        w_out_2, ffn_norm_g_2, w_gate_up_2, w_down_2, final_norm_g_2,
    )


_drawn_inputs = setup_inputs


def setup_inputs(seed=0):
    import zlib

    import numpy as np

    out = dict(_drawn_inputs(seed))
    spreads = {}
    factors = {'pool_norm': 3.101,
     'pool_scale': 4.881,
     'mla_norm': 8.0,
     'mla_q_norm': 8.0,
     'mla_kv_norm': 8.0,
     'sgu_ln_g_2': 5.489,
     'sgu_ln_b_2': 32.084}
    for name, (base, spread) in spreads.items():
        noise = np.random.default_rng([zlib.crc32(name.encode()), seed]).standard_normal(out[name].shape)
        drawn = base * np.exp(spread * noise) if base else spread * noise
        out[name] = __import__('jax').numpy.asarray(drawn.astype(out[name].dtype))
    for name, factor in factors.items():
        out[name] = (out[name] * factor).astype(out[name].dtype)
    return out
```

```python
from contextlib import ExitStack

import numpy as np

import concourse.bass as bass
from concourse import mybir

P = 128
S = 512
NB = S // P
D = 1024
DC = D // P
POOL_W = 2048
WINDOWS = (2, 4, 8, 16)
PAD = max(WINDOWS)
PC = POOL_W // P
PG = PC // len(WINDOWS)
HEADS, NOPE, ROPE, VD = 16, 128, 64, 128
HALF = ROPE // 2
QC, KC = 384 // P, 256 // P
LC = QC + KC
MLA_SCALE = float(NOPE + ROPE) ** -0.5
GH = P // HALF
GROUPS = HEADS // GH
FOX_HEADS, FOX_D = 8, 64
FOX_PAIRS = FOX_HEADS // 2
D_ATTN = FOX_HEADS * FOX_D
SGU_G, SGU_D = 8, 64
D_SGU = SGU_G * SGU_D
AC = D_ATTN // P
SC = D_SGU // P
SGU_HALF = 64
FF = 2816
FC = FF // P
EPS = 1e-6
MASKED = -1e30
ROW = [P * b * (b + 1) // 2 for b in range(NB + 1)]
COLUMN = [sum(S - P * c for c in range(b)) for b in range(NB + 1)]
SCORE_BANK = (0, 0, 1, 2)
SCORE_AT = (0, P, 0, 0)
TWO_PI = 6.283185307179586
TWO_PI_PARTS = (6.28125, 0.0019340515136718750, 1.2556659146e-06)
ROUNDER = 12582912.0

COLUMN_SIZES = (("pool_norm", DC), ("pool_scale", PC), ("mla_norm", DC), ("q_norm", QC), ("kv_norm", KC),
                ("final_norm", DC), ("mix_norm", DC), ("out_norm", DC), ("ffn_norm", DC),
                ("final_norm_2", DC), ("b_s", SGU_G), ("inv_freq", 1), ("rope_sign", 1))
COLUMNS = {name: sum(n for _, n in COLUMN_SIZES[:i]) for i, (name, _) in enumerate(COLUMN_SIZES)}
N_COLUMNS = sum(n for _, n in COLUMN_SIZES)

TILE_SIZES = (("pool_u", PC), ("pool_z", PC), ("pool_group", PC * PG // 8), ("pool_out", PC), ("mla_in", LC + 2 + PC),
              ("heads", 5 * GROUPS), ("mla_out", PC), ("mix_qk", 8), ("mix_v", 4), ("mix_z", 8),
              ("mix_out", DC), ("ffn_up", 2 * FC), ("ffn_down", FC))
TILE = {name: sum(n for _, n in TILE_SIZES[:i]) for i, (name, _) in enumerate(TILE_SIZES)}
N_TILES = sum(n for _, n in TILE_SIZES)
RING = 4
RAW = 2
AHEAD = RING - 1


def sweep(engine, n, tail=0):
    turns = (n - tail) // RING
    for j in range(min(RING, n)):
        yield 0, j
    done = min(RING, n)
    if turns > 2:
        with engine.Fori(1, turns) as turn:
            for j in range(RING):
                yield turn, j
        done = turns * RING
    for unit in range(done, n):
        yield 0, unit


def starts(turn, j, n):
    return isinstance(turn, int) and j < n


class NormSemaphores:
    def __init__(self, sem, stage):
        self.x_ready = sem(f"{stage}_x_ready") if stage != "pool" else None
        self.xg_hi = sem(f"{stage}_xg_hi") if stage != "final" else None
        self.xg_lo = sem(f"{stage}_xg_lo") if stage != "final" else None
        self.squared = sem(f"{stage}_squared")
        self.summed = sem(f"{stage}_summed")
        self.mean = sem(f"{stage}_mean")
        self.prepared = sem(f"{stage}_prepared")
        self.inv = sem(f"{stage}_inv")


class HeadSemaphores:
    def __init__(self, sem, kind):
        self.scores = sem(f"{kind}_scores")
        self.peaks = sem(f"{kind}_peaks")
        self.exped = sem(f"{kind}_exped")
        self.transposed = sem(f"{kind}_transposed")
        self.prob_t_hi = sem(f"{kind}_prob_t_hi")
        self.prob_t_lo = sem(f"{kind}_prob_t_lo")
        self.weighted = sem(f"{kind}_weighted")
        self.out = sem(f"{kind}_out")


def build(nc, x_in, stream, columns, counts_in, positions, rows_in, w_s, w_f, spill, out):
    f32, f32r, i32 = mybir.dt.float32, mybir.dt.float32r, mybir.dt.int32
    ACT = mybir.ActivationFunctionType
    ALU = mybir.AluOpType
    X = mybir.AxisListType.X
    ctx = ExitStack()
    with ctx:
        def sem(name):
            return ctx.enter_context(nc.semaphore(name))

        def sb(name, shape, dtype=f32):
            return ctx.enter_context(nc.sbuf_tensor(name, shape, dtype))

        def place(kib, name, shape, dtype=f32):
            with ExitStack() as s:
                if kib:
                    s.enter_context(nc.sbuf_tensor(f"below_{name}", [P, int(kib * 256)], f32))
                return s.enter_context(nc.sbuf_tensor(name, shape, dtype))

        def plain(ap):
            return ap.bitcast(f32)

        raw = sb("raw", [P, RAW, 1024])
        w_hi = sb("w_hi", [P, RING, 1024], f32r)
        w_lo = sb("w_lo", [P, RING, 1024], f32r)
        cols = sb("cols", [P, N_COLUMNS])
        counts = sb("counts", [P, PAD])
        gain12 = sb("gain12", [P, DC])
        ident = sb("ident", [P, P])
        ident_r = sb("ident_r", [P, P], f32r)
        mask = sb("mask", [P, P])
        mask_r = sb("mask_r", [P, P], f32r)
        upper = sb("upper", [P, P])
        ones = sb("ones", [P, P])
        inv = sb("inv", [P, S])
        mean_sq = sb("mean_sq", [P, S])
        peak = sb("peak", [P, 2, NB])
        neg_peak = sb("neg_peak", [P, 2, NB])
        row_sum = sb("row_sum", [P, 2, NB])
        inv_sum = sb("inv_sum", [P, 2, NB])
        inv_t = sb("inv_t", [P, NB])
        w_f_raw = sb("w_f_raw", [P, DC * FOX_HEADS])
        w_f_hi = sb("w_f_hi", [P, DC * FOX_HEADS], f32r)
        w_f_lo = sb("w_f_lo", [P, DC * FOX_HEADS], f32r)
        b_f = sb("b_f", [P, FOX_HEADS])
        gate = sb("gate", [P, NB, FOX_HEADS])
        gate_abs = sb("gate_abs", [P, NB, FOX_HEADS])
        log_f = sb("log_f", [P, NB, FOX_HEADS])
        stats = sb("stats", [P, NB, 6])
        moments = sb("moments", [P, NB, 2])
        rstd = sb("rstd", [P, NB])
        branch_sq = sb("branch_sq", [P, 2, NB])
        branch_inv = sb("branch_inv", [P, 2, NB])

        x = place(0, "x", [P, DC, S])
        z = place(16, "z", [P, PC, S])
        pool_xg_hi, pool_xg_lo = (place(48 + 16 * i, f"pool_xg_{i}", [P, DC, S], f32r) for i in range(2))
        pooled_hi, pooled_lo = (place(80 + 32 * i, f"pooled_{i}", [P, PC, S], f32r) for i in range(2))
        pool_sq, pool_sqsum = place(144, "pool_sq", [P, 2, S]), place(148, "pool_sqsum", [P, S])
        u_pad = place(144, "u_pad", [P, 2, PAD + S])
        sum_a, sum_b = place(148.25, "sum_a", [P, PAD + S]), place(150.5, "sum_b", [P, PAD + S])
        pooled = place(152.75, "pooled", [P, 2, S])
        y_hi, y_lo = (place(80 + 8 * i, f"y_{i}", [P, RING, S], f32r) for i in range(2))
        lat_hi, lat_lo = (place(48 + 10 * i, f"lat_{i}", [P, LC, S], f32r) for i in range(2))
        rope_k_hi, rope_k_lo = (place(68 + 2 * i, f"rope_k_{i}", [P, S], f32r) for i in range(2))
        cos, sin = place(72, "cos", [P, S]), place(74, "sin", [P, S])
        rope_a, rope_b = place(76, "rope_a", [P, S]), place(78, "rope_b", [P, S])
        lat = place(96, "lat", [P, LC, S])
        mla_xg_hi, mla_xg_lo = (place(106 + 16 * i, f"mla_xg_{i}", [P, DC, S], f32r) for i in range(2))
        mla_sq, mla_sqsum = place(138, "mla_sq", [P, 2, S]), place(142, "mla_sqsum", [P, S])
        pos_i, angle = place(144, "pos_i", [P, S], i32), place(146, "angle", [P, S])
        turns_of, reduced = place(148, "turns_of", [P, S]), place(150, "reduced", [P, S])
        lat_sq, lat_sqsum = place(144, "lat_sq", [P, LC, S]), place(154, "lat_sqsum", [P, 2, S])
        v_hi, v_lo = (place(8 * i, f"v_{i}", [P, NB, S], f32r) for i in range(2))
        k_hi, k_lo = (place(76 + 8 * i, f"k_{i}", [P, GH, S], f32r) for i in range(2))
        q_hi, q_lo = (place(92 + 8 * i, f"q_{i}", [P, GH, S], f32r) for i in range(2))
        rope_q = place(108, "rope_q", [P, 2, GH, S], f32r)
        prob = place(124, "prob", [P, ROW[NB]])
        prob_t_hi, prob_t_lo = (place(129 + 5 * i, f"prob_t_{i}", [P, COLUMN[NB]], f32r) for i in range(2))
        turned_1, turned_2 = place(139, "turned_1", [P, S]), place(141, "turned_2", [P, S])
        rope_t = place(143, "rope_t", [P, S])
        turned_hi, turned_lo = (place(145 + 4 * i, f"turned_hl_{i}", [P, 2, S], f32r) for i in range(2))
        fq_hi, fq_lo = (place(16 + 8 * i, f"fq_{i}", [P, FOX_PAIRS, S], f32r) for i in range(2))
        fk_hi, fk_lo = (place(32 + 8 * i, f"fk_{i}", [P, FOX_PAIRS, S], f32r) for i in range(2))
        fv_hi, fv_lo = (place(48 + 8 * i, f"fv_{i}", [P, NB, D_ATTN], f32r) for i in range(2))
        decay_q = place(64, "decay_q", [P, 2, S], f32r)
        decay_k = place(68, "decay_k", [P, 2, S], f32r)
        ln_g, ln_b = place(72, "ln_g", [P, D_SGU]), place(74, "ln_b", [P, D_SGU])
        inv_1 = place(78, "inv_1", [P, S])
        zu, zv = place(80, "zu", [P, NB, D_SGU]), place(88, "zv", [P, NB, D_SGU])
        mix_xg_hi, mix_xg_lo = (place(96 + 16 * i, f"mix_xg_{i}", [P, DC, S], f32r) for i in range(2))
        mix_sq, mix_sqsum = place(128, "mix_sq", [P, 2, 2, S]), place(136, "mix_sqsum", [P, 2, S])
        ws_raw = place(140, "ws_raw", [P, SGU_G * P])
        zvn_hi, zvn_lo = (place(128 + 8 * i, f"zvn_{i}", [P, NB, D_SGU], f32r) for i in range(2))
        ws_hi, ws_lo = (place(144 + 4 * i, f"ws_{i}", [P, SGU_G * P], f32r) for i in range(2))
        qk_t = place(152, "qk_t", [P, 2, S])
        c_parts = place(128, "c_parts", [FOX_HEADS, 4, S], f32r)
        f_prob = place(96, "f_prob", [P, ROW[NB]])
        f_prob_t_hi, f_prob_t_lo = (place(101 + 5 * i, f"f_prob_t_{i}", [P, COLUMN[NB]], f32r) for i in range(2))
        attn = place(111, "attn", [P, NB, D_ATTN])
        junk = place(119, "junk", [P, S])
        merged_hi, merged_lo = (place(121 + 16 * i, f"merged_{i}", [P, DC, S], f32r) for i in range(2))
        ffn_xg_hi, ffn_xg_lo = (place(16 + 16 * i, f"ffn_xg_{i}", [P, DC, S], f32r) for i in range(2))
        ffn_sq, ffn_sqsum = place(48, "ffn_sq", [P, 2, S]), place(52, "ffn_sqsum", [P, S])
        act_hi, act_lo = (place(54 + 44 * i, f"act_{i}", [P, FC, S], f32r) for i in range(2))
        gated, up = place(142, "gated", [P, 2, S]), place(146, "up", [P, 2, S])
        fin_sq, fin_sqsum = place(16, "fin_sq", [P, 2, S]), place(20, "fin_sqsum", [P, S])

        bank = [ctx.enter_context(nc.psum_tensor(f"bank{b}", [P, S], f32)) for b in range(8)]
        MEAN_BANK = 7

        def col(name, k=0):
            at = COLUMNS[name] + k
            return cols[:, at:at + 1]

        tile_loaded = [sem(f"tile_loaded_{i}") for i in range(RAW)]
        tile_hi, tile_lo, tile_used = sem("tile_hi"), sem("tile_lo"), sem("tile_used")
        cols_in, small_in, ln_in = sem("cols_in"), sem("small_in"), sem("ln_in")
        patterns, made = sem("patterns"), sem("made")
        x_loaded = [sem(f"x_loaded_{i}") for i in range(4)]
        norm = {n: NormSemaphores(sem, n) for n in ("pool", "mla", "mix", "ffn", "final")}
        steps = sem("dve_steps")
        asteps = sem("act_steps")
        in_evac, pooled_ready = sem("in_evac"), sem("pooled_ready")
        pooled_hi_done, pooled_lo_done = sem("pooled_hi_done"), sem("pooled_lo_done")
        z_silu = sem("z_silu")
        half_tile = sem("half_tile")
        y_ready = sem("y_ready")
        y_hi_done, y_lo_done = sem("y_hi_done"), sem("y_lo_done")
        Y_BEFORE = {"pool_out": 0, "mla_out": PC}
        bank_done = {n: sem(f"{n}_bank_done") for n in ("pool_out", "mla_out", "mix_out", "ffn_down")}
        pos_in, angle_ready, table_done = sem("pos_in"), sem("angle_ready"), sem("table_done")
        mla_evac, lat_squared, lat_summed = sem("mla_evac"), sem("lat_squared"), sem("lat_summed")
        lat_mean, lat_prepared, lat_inv = sem("lat_mean"), sem("lat_prepared"), sem("lat_inv")
        lat_ready, lat_hi_done, lat_lo_done = sem("lat_ready"), sem("lat_hi_done"), sem("lat_lo_done")
        rope_k_ready, rope_k_hi_done, rope_k_lo_done = sem("rope_k_ready"), sem("rope_k_hi_done"), sem("rope_k_lo_done")
        mz_silu = sem("mz_silu")
        x_spilled, x_back = sem("x_spilled"), sem("x_back")
        unit_done, unit_hi, unit_evac = sem("unit_done"), sem("unit_hi"), sem("unit_evac")
        turned, turned_hi_done, turned_lo_done, rope_q_in = sem("turned"), sem("turned_hi_done"), sem("turned_lo_done"), sem("rope_q_in")

        mla, fox = HeadSemaphores(sem, "mla_head"), HeadSemaphores(sem, "fox_head")
        probs = sem("mla_head_probs")
        qk_ready, qk_hi, qk_lo = sem("qk_ready"), sem("qk_hi"), sem("qk_lo")
        inv_t_sum, inv_t_ready = sem("inv_t_sum"), sem("inv_t_ready")
        token_summed, fv_hi_done, fv_lo_done = sem("token_summed"), sem("fv_hi_done"), sem("fv_lo_done")
        f_summed, gate_abs_ready, gate_log, log_f_ready = sem("f_summed"), sem("gate_abs_ready"), sem("gate_log"), sem("log_f_ready")
        c_summed, c_hi_done, c_ready, decay_in = sem("c_summed"), sem("c_hi_done"), sem("c_ready"), sem("decay_in")
        inv_both, decay_ones = sem("inv_both"), sem("decay_ones")
        z_gelu = sem("z_gelu")
        ln_prepared, ln_rstd, zvn_ready, zvn_hi_done, zvn_lo_done = (sem(n) for n in ("ln_prepared", "ln_rstd", "zvn_ready", "zvn_hi_done", "zvn_lo_done"))
        ws_in, ws_cut, ws_hi_done, ws_lo_done = sem("ws_in"), sem("ws_cut"), sem("ws_hi_done"), sem("ws_lo_done")
        sgu_mixed, sgu_gated = sem("sgu_mixed"), sem("sgu_gated")
        branch_squared, branch_prepared, branch_inv_done, branch_scaled = (sem(n) for n in ("branch_squared", "branch_prepared", "branch_inv_done", "branch_scaled"))
        branch_t, merged_hi_done, merged_lo_done = sem("branch_t"), sem("merged_hi_done"), sem("merged_lo_done")
        ffn_evac, gate_silu, act_ready, act_hi_done, act_lo_done = (sem(n) for n in ("ffn_evac", "gate_silu", "act_ready", "act_hi_done", "act_lo_done"))
        out_ready, stored = sem("out_ready"), sem("stored")

        UNITS = []
        for g in range(GROUPS):
            for j in range(GH):
                UNITS += [("k", g, j), ("q", g, j)]
                if j < 2:
                    UNITS += [("rope", g, j)]
            UNITS += [("v", g, b) for b in range(NB)]
        UNIT = {u: i for i, u in enumerate(UNITS)}

        def ends_tile(u):
            kind, g, j = u
            return kind == "rope" or (kind == "q" and j >= 2) or (kind == "v" and j == NB - 1)

        def unit_tile(u):
            kind, g, j = u
            return TILE["heads"] + 5 * g + (GH if kind == "v" else j)

        def wait_unit(engine, u):
            if ends_tile(u):
                engine.wait_ge(tile_used, unit_tile(u) + 1)
            else:
                engine.wait_ge(unit_done, sum(not ends_tile(o) for o in UNITS[:UNIT[u] + 1]))

        def hi_units(u):
            return sum(o[0] != "rope" for o in UNITS[:UNIT[u] + 1])

        block = ctx.enter_context(nc.Block())

        @block.sync
        def _(sp):
            for i in range(4):
                sp.dma_start(x[:, 2 * i:2 * i + 2, :], x_in[:, 2 * i:2 * i + 2, :]).then_inc(x_loaded[i], 16)
                if i == 0:
                    sp.dma_start(raw[:, 0, :], stream[0]).then_inc(tile_loaded[0], 16)
                if i == 3:
                    sp.dma_start(raw[:, 1, :], stream[1]).then_inc(tile_loaded[1], 16)
            for turn, j in sweep(sp, N_TILES):
                if not starts(turn, j, RAW):
                    sp.wait_ge(tile_lo, turn * RING + (j - RAW + 1))
                    sp.dma_start(raw[:, j % RAW, :], stream[turn * RING + j]).then_inc(tile_loaded[j % RAW], 16)

        @block.gpsimd
        def _(pool):
            pool.memset(ident[:], 0.0).then_inc(patterns, 1)
            pool.memset(mask[:], 0.0).then_inc(patterns, 1)
            pool.memset(upper[:], 1.0).then_inc(patterns, 1)
            pool.wait_ge(patterns, 3)
            pool.affine_select(out=ident[:], in_=ident[:], compare_op=ALU.not_equal, fill=1.0, base=0,
                               pattern=[[-1, P]], channel_multiplier=1).then_inc(patterns, 1)
            pool.affine_select(out=mask[:], in_=mask[:], compare_op=ALU.is_ge, fill=MASKED, base=0,
                               pattern=[[-1, P]], channel_multiplier=1).then_inc(patterns, 1)
            pool.affine_select(out=upper[:], in_=upper[:], compare_op=ALU.is_ge, fill=0.0, base=0,
                               pattern=[[1, P]], channel_multiplier=-1).then_inc(patterns, 1)
            for turn, j in sweep(pool, N_TILES):
                pool.wait_ge(tile_hi, turn * RING + (j + 1))
                pool.tensor_tensor(w_lo[:, j % RING, :], raw[:, j % RAW, :], plain(w_hi[:, j % RING, :]),
                                   ALU.subtract).then_inc(tile_lo, 1)

        @block.scalar
        def _(act):
            own = [0]

            def settle(instruction):
                own[0] += 1
                instruction.then_inc(asteps, 1)
                act.wait_ge(asteps, own[0])

            def split_tile(stage, turn, j):
                t = TILE[stage] + j + AHEAD
                if isinstance(turn, int) and t >= N_TILES:
                    return
                act.wait_ge(tile_loaded[t % RAW], turn * (16 * RING // RAW) + 16 * (t // RAW + 1))
                if not starts(turn, t, RING):
                    act.wait_ge(tile_used, turn * RING + (t - RING + 1))
                act.activation(w_hi[:, t % RING, :], raw[:, t % RAW, :], ACT.Copy).then_inc(tile_hi, 1)

            def norm_in(n, xg, sq, sqsum, gain, loaded=None):
                for k in range(DC):
                    if loaded:
                        act.wait_ge(loaded[k // 2], 16)
                    else:
                        act.wait_ge(n.x_ready, k + 1)
                    act.activation(xg[:, k, :], x[:, k, :], ACT.Copy, scale=gain(k)).then_inc(n.xg_hi, 1)
                    if k >= 3:
                        act.wait_ge(n.summed, k - 2)
                    act.activation(sq[:, k % 2, :] if k else sqsum[:], x[:, k, :], ACT.Square).then_inc(n.squared, 1)

            def norm_root(n):
                act.wait_ge(n.prepared, 1)
                act.activation(inv[:], mean_sq[:], ACT.Sqrt).then_inc(n.inv, 1)

            act.dma_start(cols[:], columns).then_inc(cols_in, 16)
            act.dma_start(counts[:], counts_in).then_inc(small_in, 16)
            act.dma_start(w_f_raw[:], w_f).then_inc(small_in, 16)
            act.dma_start(b_f[:], rows_in[:, 0:FOX_HEADS]).then_inc(small_in, 16)
            act.wait_ge(cols_in, 16)
            split_tile("pool_u", 0, -3)
            norm_in(norm["pool"], pool_xg_hi, pool_sq, pool_sqsum, lambda k: col("pool_norm", k), x_loaded)
            split_tile("pool_u", 0, -2)
            split_tile("pool_u", 0, -1)
            for n in range(PC):
                split_tile("pool_u", 0, n)
                if n == 0:
                    norm_root(norm["pool"])
                else:
                    act.wait_ge(pooled_ready, n)
                    act.activation(pooled_hi[:, n - 1, :], pooled[:, (n - 1) % 2, :], ACT.Copy).then_inc(pooled_hi_done, 1)
            for n in range(PC):
                split_tile("pool_z", 0, n)
                if n == 0:
                    act.wait_ge(pooled_ready, PC)
                    act.activation(pooled_hi[:, PC - 1, :], pooled[:, (PC - 1) % 2, :], ACT.Copy).then_inc(pooled_hi_done, 1)
                else:
                    act.wait_ge(in_evac, PC + n)
                    act.activation(z[:, n - 1, :], z[:, n - 1, :], ACT.Silu).then_inc(z_silu, 1)
            act.wait_ge(in_evac, 2 * PC)
            act.activation(z[:, PC - 1, :], z[:, PC - 1, :], ACT.Silu).then_inc(z_silu, 1)
            for n in range(PC * PG // 8):
                split_tile("pool_group", 0, n)

            def out_split(stage, ready, before):
                def chunk_hi(turn, k):
                    act.wait_ge(ready, turn * RING + (k + 1))
                    if not starts(turn, k, RING):
                        act.wait_ge(tile_used, turn * RING + (TILE[stage] + k - RING + 1))
                    index = turn * RING + k
                    act.activation(y_hi[:, k % RING, :], z[:, index, :], ACT.Copy).then_inc(y_hi_done, 1)

                before()
                for k in range(AHEAD):
                    chunk_hi(0, k)
                for turn, j in sweep(act, PC, tail=AHEAD):
                    split_tile(stage, turn, j)
                    if not isinstance(turn, int) or j + AHEAD < PC:
                        chunk_hi(turn, j + AHEAD)
                    if stage == "pool_out" and isinstance(turn, int) and j == 3:
                        for i, table in enumerate((sin, cos)):
                            act.wait_ge(angle_ready, i + 1)
                            act.activation(table[:], reduced[:], ACT.Sin).then_inc(table_done, 1)

            def before_pool_out():
                act.wait_ge(tile_used, TILE["pool_out"])
                act.dma_start(pos_i[:], positions).then_inc(pos_in, 16)

            out_split("pool_out", y_ready, before_pool_out)

            norm_in(norm["mla"], mla_xg_hi, mla_sq, mla_sqsum, lambda k: col("mla_norm", k))
            act.dma_start(spill, x[:]).then_inc(x_spilled, 16)
            for u in range(LC + 2 + PC):
                split_tile("mla_in", 0, u)
                if u == 0:
                    norm_root(norm["mla"])
                if 1 <= u <= LC:
                    act.wait_ge(mla_evac, u)
                    act.activation(lat_sq[:, u - 1, :], lat[:, u - 1, :], ACT.Square).then_inc(lat_squared, 1)
                if u == LC + 2:
                    for i in range(2):
                        act.wait_ge(lat_prepared, i + 1)
                        act.activation(lat_sqsum[:, i, :], lat_sqsum[:, i, :], ACT.Sqrt).then_inc(lat_inv, 1)
                    act.wait_ge(rope_k_ready, 1)
                    act.activation(rope_k_hi[:], rope_a[:], ACT.Copy).then_inc(rope_k_hi_done, 1)
                if u == LC + 4:
                    for i in range(LC):
                        act.wait_ge(lat_ready, i + 1)
                        act.activation(lat_hi[:, i, :], lat[:, i, :], ACT.Copy).then_inc(lat_hi_done, 1)
                if u > LC + 2:
                    n = u - LC - 3
                    act.wait_ge(mla_evac, LC + 2 + n + 1)
                    act.activation(z[:, n, :], z[:, n, :], ACT.Silu).then_inc(mz_silu, 1)
            act.wait_ge(mla_evac, LC + 2 + PC)
            act.activation(z[:, PC - 1, :], z[:, PC - 1, :], ACT.Silu).then_inc(mz_silu, 1)

            def unit_high(u):
                kind, g, j = u
                if kind == "v":
                    if u == ("v", 0, 0):
                        act.wait_ge(x_spilled, 16)
                    target = v_hi
                else:
                    target = k_hi if kind == "k" else q_hi
                wait_unit(act, u)
                act.activation(target[:, j, :], bank[6 + UNIT[u] % 2][:], ACT.Copy).then_inc(unit_hi, 1)

            def prepare(g, j):
                split_tile("heads", 0, 5 * g + j)
                unit_high(("k", g, j))
                unit_high(("q", g, j))

            def turn_split(g):
                act.wait_ge(turned, 2 * g + 2)
                if g:
                    act.wait_ge(rope_q_in, 256 * g)
                for i, t in enumerate((turned_1, turned_2)):
                    act.activation(turned_hi[:, i, :], t[:], ACT.Copy).then_inc(turned_hi_done, 1)

            def rope_rows(g):
                act.wait_ge(turned_lo_done, 2 * g + 2)
                for part, source in enumerate((turned_hi, turned_lo)):
                    for i in range(2):
                        at = HALF * (2 * part + i)
                        for h in range(GH):
                            act.dma_start(plain(rope_q[at:at + HALF, g % 2, h, :]),
                                          plain(source[HALF * h:HALF * h + HALF, i, :])).then_inc(rope_q_in, 16)

            def values_high(g):
                split_tile("heads", 0, 5 * g + GH)
                for b in range(NB):
                    unit_high(("v", g, b))

            def exps(s, h, target, scale):
                for b in range(NB):
                    act.wait_ge(s.peaks, 3 * h + SCORE_BANK[b] + 1)
                    if b == 0 and h:
                        act.wait_ge(s.transposed, NB * h)
                    n = P * (b + 1)
                    act.activation(target[:, ROW[b]:ROW[b + 1]], bank[SCORE_BANK[b]][:, SCORE_AT[b]:SCORE_AT[b] + n],
                                   ACT.Exp, bias=neg_peak[:, h % 2, b:b + 1], scale=scale,
                                   accum_out=row_sum[:, h % 2, b:b + 1]).then_inc(s.exped, 1)

            def transposed_high(s, h, target):
                if h:
                    act.wait_ge(s.weighted, h)
                for b in range(NB):
                    act.wait_ge(s.transposed, NB * h + b + 1)
                    act.activation(target[:, COLUMN[b]:COLUMN[b + 1]], bank[3 + b % 2][:, 0:S - P * b],
                                   ACT.Copy).then_inc(s.prob_t_hi, 1)

            for j in range(GH):
                prepare(0, j)
                if j == 2:
                    turn_split(0)
            rope_rows(0)
            values_high(0)
            exps(mla, 0, prob, MLA_SCALE)
            for h in range(HEADS):
                g, j = h // GH + 1, h % GH
                if g < GROUPS and j == 2:
                    rope_rows(g)
                transposed_high(mla, h, prob_t_hi)
                if h + 1 < HEADS:
                    exps(mla, h + 1, prob, MLA_SCALE)
                if g < GROUPS:
                    prepare(g, j)
                    if j == 1:
                        turn_split(g)
                    if j == GH - 1:
                        values_high(g)

            def before_mla_out():
                act.wait_ge(mla.weighted, HEADS)
                act.dma_start(x[:], spill).then_inc(x_back, 16)

            out_split("mla_out", mla.out, before_mla_out)

            n = norm["mix"]
            act.dma_start(ln_g[:], rows_in[:, FOX_HEADS:FOX_HEADS + D_SGU]).then_inc(ln_in, 16)
            act.dma_start(ln_b[:], rows_in[:, FOX_HEADS + D_SGU:]).then_inc(ln_in, 16)
            for k in range(DC):
                act.wait_ge(n.x_ready, k + 1)
                act.activation(mix_xg_hi[:, k, :], x[:, k, :], ACT.Copy, scale=gain12[:, k:k + 1]).then_inc(n.xg_hi, 1)
                if k >= 3:
                    act.wait_ge(n.summed, 2 * (k - 2))
                act.activation(mix_sq[:, k % 2, 0, :] if k else mix_sqsum[:, 0, :], x[:, k, :], ACT.Square).then_inc(n.squared, 1)
                act.activation(mix_sq[:, k % 2, 1, :] if k else mix_sqsum[:, 1, :], x[:, k, :], ACT.Square,
                               scale=col("final_norm", k)).then_inc(n.squared, 1)
            act.wait_ge(n.summed, 2 * (DC - 1))
            act.dma_start(ws_raw[:], w_s).then_inc(ws_in, 16)
            for u in range(8):
                split_tile("mix_qk", 0, u)
                if u == 0:
                    act.wait_ge(n.prepared, 1)
                    act.activation(inv_1[:], mean_sq[:], ACT.Sqrt).then_inc(n.inv, 1)
                    act.wait_ge(n.prepared, 2)
                    act.activation(inv[:], mean_sq[:], ACT.Sqrt).then_inc(n.inv, 1)
                else:
                    act.wait_ge(qk_ready, u)
                    target = fq_hi if u <= 4 else fk_hi
                    act.activation(target[:, (u - 1) % 4, :], qk_t[:, (u - 1) % 2, :], ACT.Copy).then_inc(qk_hi, 1)
            act.wait_ge(qk_ready, 8)
            act.activation(fk_hi[:, 3, :], qk_t[:, 1, :], ACT.Copy).then_inc(qk_hi, 1)
            for u in range(4):
                split_tile("mix_v", 0, u)
            act.wait_ge(ws_cut, 1)
            act.activation(ws_hi[:], ws_raw[:], ACT.Copy).then_inc(ws_hi_done, 1)
            act.wait_ge(inv_t_ready, 1)
            for b in range(NB):
                if b == NB - 1:
                    act.wait_ge(tile_used, TILE["mix_z"])
                else:
                    act.wait_ge(token_summed, b + 1)
                act.activation(fv_hi[:, b, :], bank[b][:], ACT.Copy, scale=inv_t[:, b:b + 1]).then_inc(fv_hi_done, 1)
            act.wait_ge(gate_abs_ready, 1)
            settle(act.activation(gate_abs[:], gate_abs[:], ACT.Exp, scale=-1.0))
            act.activation(gate_abs[:], gate_abs[:], ACT.Ln, bias=1.0).then_inc(gate_log, 1)
            for u in range(8):
                split_tile("mix_z", 0, u)
                if u == 4:
                    act.wait_ge(c_summed, 1)
                    act.activation(c_parts[:, 0, :], bank[6][0:FOX_HEADS, :], ACT.Copy).then_inc(c_hi_done, 1)
                if u == 6:
                    act.wait_ge(decay_ones, 1)
                    act.wait_ge(c_ready, 1)
                    for s in range(2):
                        for part in range(2):
                            act.dma_start(plain(decay_q[part:P:32, s, :]), plain(c_parts[4 * s:4 * s + 4, part, :])).then_inc(decay_in, 16)
                            act.dma_start(plain(decay_k[2 + part:P:32, s, :]), plain(c_parts[4 * s:4 * s + 4, 2 + part, :])).then_inc(decay_in, 16)
                if u in (4, 7):
                    group = (u - 4) // 3
                    for b in range(NB):
                        if b == NB - 1:
                            act.wait_ge(tile_used, TILE["mix_z"] + 4 * group + 4)
                        else:
                            act.wait_ge(token_summed, 3 * (group + 1) + b + 1)
                        act.activation((zu, zv)[group][:, b, :], bank[4 * group + b][:], ACT.Gelu,
                                       scale=inv_t[:, b:b + 1]).then_inc(z_gelu, 1)
            act.wait_ge(decay_in, 8 * 16)
            act.wait_ge(ln_prepared, 1)
            act.activation(rstd[:], rstd[:], ACT.Sqrt).then_inc(ln_rstd, 1)
            for b in range(NB):
                act.wait_ge(zvn_ready, b + 1)
                act.activation(zvn_hi[:, b, :], zv[:, b, :], ACT.Copy).then_inc(zvn_hi_done, 1)

            exps(fox, 0, f_prob, 1.0)
            for h in range(FOX_HEADS):
                transposed_high(fox, h, f_prob_t_hi)
                if h + 1 < FOX_HEADS:
                    exps(fox, h + 1, f_prob, 1.0)
            for i, source in enumerate((zu, attn)):
                if i == 0:
                    act.wait_ge(sgu_gated, SGU_G)
                else:
                    act.wait_ge(fox.out, FOX_HEADS)
                for b in range(NB):
                    if NB * i + b:
                        act.wait_ge(branch_squared, NB * i + b)
                    act.activation(junk[:], source[:, b, :], ACT.Square,
                                   accum_out=branch_sq[:, i, b:b + 1]).then_inc(branch_squared, 1)
                act.wait_ge(branch_prepared, i + 1)
                act.activation(branch_inv[:, i, :], branch_inv[:, i, :], ACT.Sqrt).then_inc(branch_inv_done, 1)
                for c in range(AC):
                    act.wait_ge(branch_t, AC * i + c + 1)
                    at = c + (AC if i == 0 else 0)
                    act.activation(merged_hi[:, at, :], bank[6 + c % 2][:], ACT.Copy,
                                   scale=col("out_norm", at)).then_inc(merged_hi_done, 1)
            for k in range(DC):
                split_tile("mix_out", 0, k)

            norm_in(norm["ffn"], ffn_xg_hi, ffn_sq, ffn_sqsum, lambda k: col("ffn_norm", k))

            def act_high(turn, n):
                index = turn * 2 + n
                act.wait_ge(act_ready, index + 1)
                act.activation(act_hi[:, index, :], up[:, n % 2, :], ACT.Copy).then_inc(act_hi_done, 1)

            for turn, j in sweep(act, 2 * FC):
                split_tile("ffn_up", turn, j)
                if starts(turn, j, 1):
                    norm_root(norm["ffn"])
                if j % 2 == 0:
                    act.wait_ge(ffn_evac, turn * RING + (j + 1))
                    act.activation(gated[:, j // 2 % 2, :], gated[:, j // 2 % 2, :], ACT.Silu).then_inc(gate_silu, 1)
                elif not starts(turn, j, 2):
                    act_high(turn, j // 2 - 1)
            act_high(0, FC - 1)
            for k in range(FC):
                split_tile("ffn_down", 0, k)
            n = norm["final"]
            for k in range(DC):
                act.wait_ge(n.x_ready, k + 1)
                if k >= 3:
                    act.wait_ge(n.summed, k - 2)
                act.activation(fin_sq[:, k % 2, :] if k else fin_sqsum[:], x[:, k, :], ACT.Square).then_inc(n.squared, 1)
            norm_root(n)
            for k in range(DC):
                act.wait_ge(out_ready, k + 1)
                act.dma_start(out[:, k, :], x[:, k, :]).then_inc(stored, 16)
            act.wait_ge(stored, 16 * DC)
            act.wait_ge(x_spilled, 16)

        @block.vector
        def _(dve):
            own = [0]

            def settle(instruction):
                own[0] += 1
                instruction.then_inc(steps, 1)
                dve.wait_ge(steps, own[0])

            def norm_chunk(n, k, xg_hi, xg_lo, gain, pairs):
                dve.wait_ge(n.xg_hi, k + 1)
                dve.scalar_tensor_tensor(xg_lo[:, k, :], x[:, k, :], gain(k), plain(xg_hi[:, k, :]),
                                         ALU.mult, ALU.subtract).then_inc(n.xg_lo, 1)
                if k:
                    dve.wait_ge(n.squared, len(pairs) * (k + 1))
                    if k >= 2:
                        dve.wait_ge(n.summed, len(pairs) * (k - 1))
                    for total, square in pairs:
                        dve.tensor_tensor(total, total, square(k), ALU.add).then_inc(n.summed, 1)

            def norm_mean(n, b, source_scale=1.0 / D):
                dve.wait_ge(n.mean, 1)
                settle(dve.tensor_scalar(mean_sq[:], b[:], source_scale, EPS, ALU.mult, ALU.add))
                dve.reciprocal(mean_sq[:], mean_sq[:]).then_inc(n.prepared, 1)

            def take_bank(stage, n, k):
                if k < DC - 1:
                    dve.wait_ge(bank_done[stage], k + 1)
                else:
                    dve.wait_ge(tile_used, TILE[stage] + dict(TILE_SIZES)[stage])
                dve.tensor_tensor(x[:, k, :], bank[k][:], x[:, k, :], ALU.add).then_inc(n.x_ready, 1)

            def residual(stage, name, xg_hi, xg_lo, sq, sqsum, gain):
                n = norm[name]
                for k in range(DC + 1):
                    if k < DC:
                        take_bank(stage, n, k)
                    if k:
                        norm_chunk(n, k - 1, xg_hi, xg_lo, gain, [(sqsum[:], lambda c: sq[:, c % 2, :])])

            def out_low(stage):
                for turn, j in sweep(dve, PC):
                    dve.wait_ge(y_hi_done, turn * RING + (Y_BEFORE[stage] + j + 1))
                    index = turn * RING + j
                    dve.tensor_tensor(y_lo[:, j % RING, :], z[:, index, :], plain(y_hi[:, j % RING, :]),
                                      ALU.subtract).then_inc(y_lo_done, 1)
                    if stage == "pool_out" and isinstance(turn, int) and j == 3:
                        rope_angles()

            def rope_angles():
                dve.wait_ge(pos_in, 16)
                settle(dve.tensor_copy(angle[:], pos_i[:]))
                settle(dve.tensor_scalar(angle[:], angle[:], col("inv_freq"), None, ALU.mult))
                for i, ahead in enumerate((0.0, 0.25)):
                    settle(dve.tensor_scalar(turns_of[:], angle[:], 1.0 / TWO_PI, ahead, ALU.mult, ALU.add))
                    settle(dve.tensor_scalar(turns_of[:], turns_of[:], ROUNDER, None, ALU.add))
                    settle(dve.tensor_scalar(turns_of[:], turns_of[:], ROUNDER, None, ALU.subtract))
                    if i:
                        dve.wait_ge(table_done, 1)
                    settle(dve.scalar_tensor_tensor(reduced[:], turns_of[:], -TWO_PI_PARTS[0], angle[:], ALU.mult, ALU.add))
                    for part in TWO_PI_PARTS[1:]:
                        settle(dve.scalar_tensor_tensor(reduced[:], turns_of[:], -part, reduced[:], ALU.mult, ALU.add))
                    if i:
                        settle(dve.tensor_scalar(reduced[:], reduced[:], TWO_PI / 4, None, ALU.add))
                    dve.tensor_scalar(reduced[:], reduced[:], 3.1415925, -3.1415925, ALU.min, ALU.max).then_inc(angle_ready, 1)

            dve.memset(ones[:], 1.0).then_inc(made, 1)
            dve.wait_ge(patterns, 6)
            dve.tensor_copy(ident_r[:], ident[:]).then_inc(made, 1)
            dve.tensor_copy(mask_r[:], mask[:]).then_inc(made, 1)
            dve.wait_ge(cols_in, 16)
            n = norm["pool"]
            for k in range(DC):
                norm_chunk(n, k, pool_xg_hi, pool_xg_lo, lambda c: col("pool_norm", c),
                           [(pool_sqsum[:], lambda c: pool_sq[:, c % 2, :])])
            norm_mean(n, bank[MEAN_BANK])
            dve.wait_ge(small_in, 48)
            dve.tensor_tensor(gain12[:], cols[:, COLUMNS["final_norm"]:COLUMNS["final_norm"] + DC],
                              cols[:, COLUMNS["mix_norm"]:COLUMNS["mix_norm"] + DC], ALU.mult).then_inc(made, 1)
            settle(dve.tensor_copy(w_f_hi[:], w_f_raw[:]))
            dve.tensor_tensor(w_f_lo[:], w_f_raw[:], plain(w_f_hi[:]), ALU.subtract).then_inc(made, 1)
            for i in range(2):
                settle(dve.memset(u_pad[:, i, 0:PAD], 0.0))
            dve.wait_ge(n.inv, 1)

            def pooled_low(c):
                dve.wait_ge(pooled_hi_done, c + 1)
                dve.tensor_tensor(pooled_lo[:, c, :], pooled[:, c % 2, :], plain(pooled_hi[:, c, :]),
                                  ALU.subtract).then_inc(pooled_lo_done, 1)

            for c in range(PC):
                window = WINDOWS[c // PG]
                u = u_pad[:, c % 2, :]
                dve.wait_ge(tile_used, TILE["pool_u"] + c + 1)
                dve.tensor_tensor(u[:, PAD:], bank[c % 4][:], inv[:], ALU.mult).then_inc(in_evac, 1)
                dve.wait_ge(in_evac, c + 1)
                total, reach, spare = u, 1, (sum_a, sum_b)
                while reach < window:
                    target = spare[0]
                    settle(dve.tensor_tensor(target[:, 2 * reach:], total[:, 2 * reach:], total[:, reach:PAD + S - reach], ALU.add))
                    total, reach, spare = target, 2 * reach, spare[::-1]
                if c >= 2:
                    pooled_low(c - 2)
                    dve.wait_ge(pooled_lo_done, c - 1)
                dst = pooled[:, c % 2, :]
                edge = window - 1
                other = spare[0]
                dve.scalar_tensor_tensor(dst[:, edge:], total[:, PAD + edge:], 1.0 / window, u[:, PAD + edge:],
                                         ALU.mult, ALU.subtract)
                settle(dve.tensor_tensor(other[:, 0:edge], total[:, PAD:PAD + edge], counts[:, 0:edge], ALU.mult))
                dve.tensor_tensor(dst[:, 0:edge], other[:, 0:edge], u[:, PAD:PAD + edge], ALU.subtract).then_inc(pooled_ready, 1)
            for c in range(PC):
                dve.wait_ge(tile_used, TILE["pool_z"] + c + 1)
                dve.tensor_tensor(z[:, c, :], bank[c % 4][:], inv[:], ALU.mult).then_inc(in_evac, 1)
                if c < 2:
                    pooled_low(PC - 2 + c)
            for c in range(PC):
                if c % 2:
                    dve.wait_ge(tile_used, TILE["pool_group"] + c // 2 + 1)
                else:
                    dve.wait_ge(half_tile, c // 2 + 1)
                dve.wait_ge(z_silu, c + 1)
                dve.scalar_tensor_tensor(z[:, c, :], bank[c % 4][:], col("pool_scale", c), z[:, c, :],
                                         ALU.mult, ALU.mult).then_inc(y_ready, 1)
            out_low("pool_out")
            residual("pool_out", "mla", mla_xg_hi, mla_xg_lo, mla_sq, mla_sqsum, lambda k: col("mla_norm", k))
            norm_mean(norm["mla"], bank[MEAN_BANK])
            dve.wait_ge(norm["mla"].inv, 1)

            for u in range(LC + 2 + PC):
                dve.wait_ge(tile_used, TILE["mla_in"] + u + 1)
                source = bank[u % 4][:]
                if u < LC:
                    dve.tensor_tensor(lat[:, u, :], source, inv[:], ALU.mult).then_inc(mla_evac, 1)
                elif u == LC:
                    dve.wait_ge(table_done, 2)
                    dve.tensor_tensor(rope_a[:], source, cos[:], ALU.mult).then_inc(mla_evac, 1)
                elif u == LC + 1:
                    dve.scalar_tensor_tensor(rope_b[:], source, col("rope_sign"), sin[:], ALU.mult, ALU.mult).then_inc(mla_evac, 1)
                    dve.wait_ge(mla_evac, LC + 2)
                    settle(dve.tensor_tensor(rope_a[:], rope_a[:], rope_b[:], ALU.add))
                    dve.tensor_tensor(rope_a[:], rope_a[:], inv[:], ALU.mult).then_inc(rope_k_ready, 1)
                    for i, (first, last) in enumerate(((0, QC), (QC, LC))):
                        dve.wait_ge(lat_squared, last)
                        for c in range(first + 1, last):
                            t = dve.tensor_tensor(lat_sqsum[:, i, :], lat_sq[:, c, :],
                                                  lat_sq[:, first, :] if c == first + 1 else lat_sqsum[:, i, :], ALU.add)
                            if c < last - 1:
                                settle(t)
                            else:
                                t.then_inc(lat_summed, 1)
                else:
                    dve.tensor_tensor(z[:, u - LC - 2, :], source, inv[:], ALU.mult).then_inc(mla_evac, 1)
                if u == LC + 2:
                    for i, width in enumerate((QC * P, KC * P)):
                        dve.wait_ge(lat_mean, i + 1)
                        settle(dve.tensor_scalar(lat_sqsum[:, i, :], bank[6 + i][:], 1.0 / width, EPS, ALU.mult, ALU.add))
                        dve.reciprocal(lat_sqsum[:, i, :], lat_sqsum[:, i, :]).then_inc(lat_prepared, 1)
                if u == LC + 3:
                    dve.wait_ge(lat_inv, 2)
                    for c in range(LC):
                        dve.scalar_tensor_tensor(lat[:, c, :], lat[:, c, :], col("q_norm", c), lat_sqsum[:, int(c >= QC), :],
                                                 ALU.mult, ALU.mult).then_inc(lat_ready, 1)
                    dve.wait_ge(rope_k_hi_done, 1)
                    dve.tensor_tensor(rope_k_lo[:], rope_a[:], plain(rope_k_hi[:]), ALU.subtract).then_inc(rope_k_lo_done, 1)
                if u == LC + 5:
                    for c in range(LC):
                        dve.wait_ge(lat_hi_done, c + 1)
                        dve.tensor_tensor(lat_lo[:, c, :], lat[:, c, :], plain(lat_hi[:, c, :]), ALU.subtract).then_inc(lat_lo_done, 1)

            def unit_low(u):
                kind, g, j = u
                hi, lo = {"k": (k_hi, k_lo), "q": (q_hi, q_lo), "v": (v_hi, v_lo)}[kind]
                dve.wait_ge(unit_hi, hi_units(u))
                dve.tensor_tensor(lo[:, j, :], bank[6 + UNIT[u] % 2][:], plain(hi[:, j, :]), ALU.subtract).then_inc(unit_evac, 1)

            def turn_half(g, j):
                u = ("rope", g, j)
                source = bank[6 + UNIT[u] % 2][:]
                wait_unit(dve, u)
                if j == 0:
                    if g:
                        dve.wait_ge(turned_lo_done, 2 * g)
                        dve.wait_ge(turned_hi_done, 2 * g)
                    settle(dve.tensor_tensor(turned_1[:], source, cos[:], ALU.mult))
                    dve.tensor_tensor(turned_2[:], source, sin[:], ALU.mult).then_inc(unit_evac, 1)
                else:
                    settle(dve.tensor_tensor(rope_t[:], source, sin[:], ALU.mult))
                    dve.tensor_tensor(turned_1[:], turned_1[:], rope_t[:], ALU.subtract).then_inc(turned, 1)
                    dve.wait_ge(turned, 2 * g + 1)
                    dve.tensor_tensor(rope_t[:], source, cos[:], ALU.mult).then_inc(unit_evac, 1)
                    dve.wait_ge(unit_evac, UNIT[u] + 1)
                    dve.tensor_tensor(turned_2[:], turned_2[:], rope_t[:], ALU.add).then_inc(turned, 1)

            def turned_low(g):
                for i, t in enumerate((turned_1, turned_2)):
                    dve.wait_ge(turned_hi_done, 2 * g + i + 1)
                    dve.tensor_tensor(turned_lo[:, i, :], t[:], plain(turned_hi[:, i, :]), ALU.subtract).then_inc(turned_lo_done, 1)

            def peaks(s, h, scale):
                for i, blocks in enumerate(((0, 1), (2,), (3,))):
                    dve.wait_ge(s.scores, 3 * h + i + 1)
                    for b in blocks:
                        t = dve.reduce_max(peak[:, h % 2, b:b + 1], bank[i][:, SCORE_AT[b]:SCORE_AT[b] + P * (b + 1)], X)
                    settle(t)
                    if h >= 2:
                        dve.wait_ge(s.exped, NB * (h - 1))
                    dve.tensor_scalar(neg_peak[:, h % 2, blocks[0]:blocks[-1] + 1], peak[:, h % 2, blocks[0]:blocks[-1] + 1],
                                      -scale, None, ALU.mult).then_inc(s.peaks, 1)

            def normalise(h):
                dve.wait_ge(mla.exped, NB * (h + 1))
                settle(dve.reciprocal(inv_sum[:, h % 2, :], row_sum[:, h % 2, :]))
                for b in range(NB):
                    dve.tensor_scalar(prob[:, ROW[b]:ROW[b + 1]], prob[:, ROW[b]:ROW[b + 1]], inv_sum[:, h % 2, b:b + 1],
                                      None, ALU.mult).then_inc(probs, 1)

            def transposed_low(s, h, hi, lo):
                for b in range(NB):
                    dve.wait_ge(s.prob_t_hi, NB * h + b + 1)
                    dve.tensor_tensor(lo[:, COLUMN[b]:COLUMN[b + 1]], bank[3 + b % 2][:, 0:S - P * b],
                                      plain(hi[:, COLUMN[b]:COLUMN[b + 1]]), ALU.subtract).then_inc(s.prob_t_lo, 1)

            def values_low(g):
                for b in range(NB):
                    unit_low(("v", g, b))

            for j in range(GH):
                unit_low(("k", 0, j))
                unit_low(("q", 0, j))
                if j < 2:
                    turn_half(0, j)
                if j == 2:
                    turned_low(0)
            values_low(0)
            peaks(mla, 0, MLA_SCALE)
            normalise(0)
            for h in range(HEADS):
                g, j = h // GH + 1, h % GH
                transposed_low(mla, h, prob_t_hi, prob_t_lo)
                if h + 1 < HEADS:
                    peaks(mla, h + 1, MLA_SCALE)
                dve.wait_ge(mla.weighted, h + 1)
                dve.wait_ge(mz_silu, h + 1)
                dve.tensor_tensor(z[:, h, :], bank[5][:], z[:, h, :], ALU.mult).then_inc(mla.out, 1)
                if g < GROUPS:
                    unit_low(("k", g, j))
                if h + 1 < HEADS:
                    normalise(h + 1)
                if g < GROUPS:
                    unit_low(("q", g, j))
                    if j < 2:
                        turn_half(g, j)
                    if j == 1:
                        turned_low(g)
                    if j == GH - 1:
                        values_low(g)
            out_low("mla_out")

            n = norm["mix"]
            dve.wait_ge(x_back, 16)
            pairs = [(mix_sqsum[:, i, :], lambda c, i=i: mix_sq[:, c % 2, i, :]) for i in range(2)]
            for k in range(DC + 1):
                if k < DC:
                    take_bank("mla_out", n, k)
                if k:
                    norm_chunk(n, k - 1, mix_xg_hi, mix_xg_lo, lambda c: gain12[:, c:c + 1], pairs)
            dve.wait_ge(n.mean, 1)
            settle(dve.tensor_scalar(mean_sq[:], bank[6][:], 1.0 / D, EPS, ALU.mult, ALU.add))
            dve.reciprocal(mean_sq[:], mean_sq[:]).then_inc(n.prepared, 1)
            dve.wait_ge(n.inv, 1)
            dve.wait_ge(n.mean, 2)
            settle(dve.tensor_tensor(mean_sq[:], bank[7][:], inv_1[:], ALU.mult))
            settle(dve.tensor_tensor(mean_sq[:], mean_sq[:], inv_1[:], ALU.mult))
            settle(dve.tensor_scalar(mean_sq[:], mean_sq[:], 1.0 / D, EPS, ALU.mult, ALU.add))
            dve.reciprocal(mean_sq[:], mean_sq[:]).then_inc(n.prepared, 1)
            dve.wait_ge(n.inv, 2)
            dve.tensor_tensor(inv[:], inv[:], inv_1[:], ALU.mult).then_inc(inv_both, 1)
            dve.wait_ge(inv_both, 1)

            def qk_low(u):
                hi, lo = (fq_hi, fq_lo) if u < 4 else (fk_hi, fk_lo)
                dve.wait_ge(qk_hi, u + 1)
                dve.tensor_tensor(lo[:, u % 4, :], qk_t[:, u % 2, :], plain(hi[:, u % 4, :]), ALU.subtract).then_inc(qk_lo, 1)

            for u in range(8):
                dve.wait_ge(tile_used, TILE["mix_qk"] + u + 1)
                if u >= 2:
                    qk_low(u - 2)
                    dve.wait_ge(qk_lo, u - 1)
                dve.scalar_tensor_tensor(qk_t[:, u % 2, :], bank[u % 4][:], FOX_D ** -0.5 if u < 4 else 1.0, inv[:],
                                         ALU.mult, ALU.mult).then_inc(qk_ready, 1)
                dve.scalar_tensor_tensor(x[:, u, :], x[:, u, :], col("final_norm", u), inv_1[:], ALU.mult, ALU.mult)
                if u == 0:
                    dve.wait_ge(inv_t_sum, 1)
                    dve.tensor_copy(inv_t[:], bank[5][:, 0:NB]).then_inc(inv_t_ready, 1)
                if u == 1:
                    dve.wait_ge(ws_in, 16)
                    w = ws_raw[:].rearrange("p (g i) -> p g i", g=SGU_G)
                    dve.memset(w[SGU_HALF:P, :, 0:SGU_HALF], 0.0).then_inc(ws_cut, 1)
                if u == 2:
                    dve.memset(plain(decay_q[:]), 1.0)
                    dve.memset(plain(decay_k[:]), 1.0).then_inc(decay_ones, 1)
            qk_low(6)
            qk_low(7)
            dve.wait_ge(inv_t_ready, 1)
            for b in range(NB):
                dve.wait_ge(fv_hi_done, b + 1)
                dve.scalar_tensor_tensor(fv_lo[:, b, :], bank[b][:], inv_t[:, b:b + 1], plain(fv_hi[:, b, :]),
                                         ALU.mult, ALU.subtract).then_inc(fv_lo_done, 1)
            dve.wait_ge(ws_hi_done, 1)
            dve.tensor_tensor(ws_lo[:], ws_raw[:], plain(ws_hi[:]), ALU.subtract).then_inc(ws_lo_done, 1)
            dve.wait_ge(f_summed, 1)
            for b in range(NB):
                t = dve.scalar_tensor_tensor(gate[:, b, :], bank[5][:, 8 * b:8 * b + 8], inv_t[:, b:b + 1], b_f[:],
                                             ALU.mult, ALU.add)
            settle(t)
            dve.scalar_tensor_tensor(gate_abs[:], gate[:], -1.0, gate[:], ALU.mult, ALU.max).then_inc(gate_abs_ready, 1)
            settle(dve.tensor_scalar(gate[:], gate[:], 0.0, None, ALU.min))
            dve.wait_ge(gate_log, 1)
            dve.tensor_tensor(log_f[:], gate[:], gate_abs[:], ALU.subtract).then_inc(log_f_ready, 1)
            dve.wait_ge(c_hi_done, 1)
            settle(dve.tensor_tensor(c_parts[:, 1, :], bank[6][0:FOX_HEADS, :], plain(c_parts[:, 0, :]), ALU.subtract))
            dve.tensor_scalar(c_parts[:, 2:4, :], plain(c_parts[:, 0:2, :]), -1.0, None, ALU.mult).then_inc(c_ready, 1)
            for b in range(NB):
                dve.wait_ge(z_gelu, NB + b + 1)
                settle(dve.bn_stats(stats[:, b, :], zv[:, b, :]))
                settle(dve.bn_aggr(moments[:, b, :], stats[:, b:b + 1, :]))
            settle(dve.tensor_scalar(rstd[:], moments[:, :, 1], EPS, None, ALU.add))
            dve.reciprocal(rstd[:], rstd[:]).then_inc(ln_prepared, 1)
            dve.wait_ge(ln_rstd, 1)
            dve.wait_ge(ln_in, 32)
            for b in range(NB):
                settle(dve.tensor_scalar(zv[:, b, :], zv[:, b, :], moments[:, b, 0:1], rstd[:, b:b + 1], ALU.subtract, ALU.mult))
                settle(dve.tensor_tensor(zv[:, b, :], zv[:, b, :], ln_g[:], ALU.mult))
                dve.tensor_tensor(zv[:, b, :], zv[:, b, :], ln_b[:], ALU.add).then_inc(zvn_ready, 1)
            for b in range(NB):
                dve.wait_ge(zvn_hi_done, b + 1)
                dve.tensor_tensor(zvn_lo[:, b, :], zv[:, b, :], plain(zvn_hi[:, b, :]), ALU.subtract).then_inc(zvn_lo_done, 1)

            peaks(fox, 0, 1.0)
            for h in range(FOX_HEADS):
                transposed_low(fox, h, f_prob_t_hi, f_prob_t_lo)
                if h + 1 < FOX_HEADS:
                    peaks(fox, h + 1, 1.0)
                dve.wait_ge(fox.exped, NB * (h + 1))
                settle(dve.reciprocal(inv_sum[:, h % 2, :], row_sum[:, h % 2, :]))
                dve.wait_ge(fox.weighted, h + 1)
                dve.tensor_tensor(attn[:, :, FOX_D * h:FOX_D * (h + 1)],
                                  bank[5][:, 0:NB * FOX_D].rearrange("p (b d) -> p b d", b=NB),
                                  inv_sum[:, h % 2, :].unsqueeze(2).to_broadcast([P, NB, FOX_D]), ALU.mult).then_inc(fox.out, 1)
                dve.wait_ge(sgu_mixed, h + 1)
                mine = zu[:, :, SGU_D * h:SGU_D * (h + 1)]
                dve.scalar_tensor_tensor(mine, bank[6 + h % 2][:, 0:NB * SGU_D].rearrange("p (b d) -> p b d", b=NB),
                                         col("b_s", h), mine, ALU.add, ALU.mult).then_inc(sgu_gated, 1)
            for i, source in enumerate((zu, attn)):
                dve.wait_ge(branch_squared, NB * (i + 1))
                settle(dve.tensor_scalar(branch_inv[:, i, :], branch_sq[:, i, :], 1.0 / D_ATTN, EPS, ALU.mult, ALU.add))
                dve.reciprocal(branch_inv[:, i, :], branch_inv[:, i, :]).then_inc(branch_prepared, 1)
                dve.wait_ge(branch_inv_done, i + 1)
                for b in range(NB):
                    dve.tensor_scalar(source[:, b, :], source[:, b, :], branch_inv[:, i, b:b + 1], None, ALU.mult).then_inc(branch_scaled, 1)
                for c in range(AC):
                    at = c + (AC if i == 0 else 0)
                    dve.wait_ge(merged_hi_done, AC * i + c + 1)
                    dve.scalar_tensor_tensor(merged_lo[:, at, :], bank[6 + c % 2][:], col("out_norm", at),
                                             plain(merged_hi[:, at, :]), ALU.mult, ALU.subtract).then_inc(merged_lo_done, 1)
            residual("mix_out", "ffn", ffn_xg_hi, ffn_xg_lo, ffn_sq, ffn_sqsum, lambda k: col("ffn_norm", k))

            norm_mean(norm["ffn"], bank[MEAN_BANK])
            dve.wait_ge(norm["ffn"].inv, 1)

            def act_low(turn, n):
                index = turn * 2 + n
                dve.wait_ge(act_hi_done, index + 1)
                dve.tensor_tensor(act_lo[:, index, :], up[:, n % 2, :], plain(act_hi[:, index, :]), ALU.subtract).then_inc(act_lo_done, 1)

            for turn, j in sweep(dve, 2 * FC):
                dve.wait_ge(tile_used, turn * RING + (TILE["ffn_up"] + j + 1))
                n = j // 2
                if j % 2 == 0:
                    dve.tensor_tensor(gated[:, n % 2, :], bank[j % 4][:], inv[:], ALU.mult).then_inc(ffn_evac, 1)
                    if not starts(turn, j, 4):
                        act_low(turn, n - 2)
                else:
                    if not starts(turn, j, 4):
                        dve.wait_ge(act_lo_done, turn * 2 + (n - 1))
                    dve.tensor_tensor(up[:, n % 2, :], bank[j % 4][:], inv[:], ALU.mult).then_inc(ffn_evac, 1)
                    dve.wait_ge(ffn_evac, turn * RING + (j + 1))
                    dve.wait_ge(gate_silu, turn * 2 + (n + 1))
                    dve.tensor_tensor(up[:, n % 2, :], up[:, n % 2, :], gated[:, n % 2, :], ALU.mult).then_inc(act_ready, 1)
            act_low(0, FC - 2)
            act_low(0, FC - 1)
            n = norm["final"]
            for k in range(DC):
                take_bank("ffn_down", n, k)
                if k:
                    dve.wait_ge(n.squared, k + 1)
                    if k >= 2:
                        dve.wait_ge(n.summed, k - 1)
                    dve.tensor_tensor(fin_sqsum[:], fin_sqsum[:], fin_sq[:, k % 2, :], ALU.add).then_inc(n.summed, 1)
            norm_mean(n, bank[0])
            dve.wait_ge(n.inv, 1)
            for k in range(DC):
                dve.scalar_tensor_tensor(x[:, k, :], x[:, k, :], col("final_norm_2", k), inv[:], ALU.mult, ALU.mult).then_inc(out_ready, 1)

        @block.tensor
        def _(pe):
            def three(target, a_hi, a_lo, b_hi, b_lo, start, stop):
                pe.matmul(target, a_hi, b_hi, start=start, stop=False)
                pe.matmul(target, a_hi, b_lo, start=False, stop=False)
                return pe.matmul(target, a_lo, b_hi, start=False, stop=stop)

            def wblock(t, i, width=P):
                return w_hi[:, t % RING, width * i:width * (i + 1)], w_lo[:, t % RING, width * i:width * (i + 1)]

            def wait_tile(turn, t):
                pe.wait_ge(tile_lo, turn * RING + (t + 1))

            def projection(stage, turn, j, b, xg_hi, xg_lo, xg_lo_done=None):
                t = TILE[stage] + j
                wait_tile(turn, t)
                for k in range(DC):
                    if xg_lo_done is not None:
                        pe.wait_ge(xg_lo_done, k + 1)
                    last = three(b[:], *wblock(t, k), xg_hi[:, k, :], xg_lo[:, k, :], k == 0, k == DC - 1)
                last.then_inc(tile_used, 1)

            def mean(sem_in, value, total, b, sem_out):
                pe.wait_ge(sem_in, value)
                pe.matmul(b[:], ones[:], total, start=True, stop=True).then_inc(sem_out, 1)

            def out_product(stage, chunks, chunk_lo, lo_sem, lo_value, tail=1, free=()):
                for turn, j in sweep(pe, chunks, tail=tail):
                    t = TILE[stage] + j
                    wait_tile(turn, t)
                    pe.wait_ge(lo_sem, lo_value(turn, j))
                    hi, lo = chunk_lo(turn, j)
                    first, final = starts(turn, j, 1), isinstance(turn, int) and j == chunks - 1
                    for n in range(DC):
                        if first:
                            for s_, v_ in free[n]:
                                pe.wait_ge(s_, v_)
                        last = three(bank[n][:], *wblock(t, n), hi, lo, first, final)
                        if final and n < DC - 1:
                            last.then_inc(bank_done[stage], 1)
                    last.then_inc(tile_used, 1)

            n = norm["pool"]
            for turn, j in sweep(pe, PC):
                if not starts(turn, j, 4):
                    pe.wait_ge(in_evac, turn * RING + (j - 3))
                projection("pool_u", turn, j, bank[j % 4], pool_xg_hi, pool_xg_lo, n.xg_lo if starts(turn, j, 1) else None)
                if starts(turn, j, 1):
                    pe.wait_ge(made, 1)
                    mean(n.summed, DC - 1, pool_sqsum[:], bank[MEAN_BANK], n.mean)
            for turn, j in sweep(pe, PC):
                pe.wait_ge(in_evac, turn * RING + (PC + j - 3))
                projection("pool_z", turn, j, bank[j % 4], pool_xg_hi, pool_xg_lo)
            for i in range(PC * PG // 8):
                t = TILE["pool_group"] + i
                wait_tile(0, t)
                group = i // 2
                pe.wait_ge(pooled_lo_done, PG * (group + 1))
                for half in range(2):
                    c = 2 * i + half
                    if c < 4:
                        pe.wait_ge(in_evac, 2 * PC - 4 + c + 1)
                    else:
                        pe.wait_ge(y_ready, c - 3)
                    for k in range(PG):
                        last = three(bank[c % 4][:], *wblock(t, PG * half + k), pooled_hi[:, PG * group + k, :],
                                     pooled_lo[:, PG * group + k, :], k == 0, k == PG - 1)
                    last.then_inc(tile_used if half else half_tile, 1)
            out_product("pool_out", PC, lambda turn, j: (y_hi[:, j % RING, :], y_lo[:, j % RING, :]),
                        y_lo_done, lambda turn, j: turn * RING + (j + 1),
                        free=[[(y_ready, PC - 4 + b + 1)] if b < 4 else [] for b in range(8)])

            n = norm["mla"]
            for u in range(LC + 2 + PC):
                if u >= 4:
                    pe.wait_ge(mla_evac, u - 3)
                projection("mla_in", 0, u, bank[u % 4], mla_xg_hi, mla_xg_lo, n.xg_lo if u == 0 else None)
                if u == 0:
                    mean(n.summed, DC - 1, mla_sqsum[:], bank[MEAN_BANK], n.mean)
                if u == LC + 2:
                    for i in range(2):
                        mean(lat_summed, i + 1, lat_sqsum[:, i, :], bank[6 + i], lat_mean)

            def unit(u):
                kind, g, j = u
                i = UNIT[u]
                if i >= 2:
                    pe.wait_ge(unit_evac, i - 1)
                t = unit_tile(u)
                wait_tile(0, t)
                b = bank[6 + i % 2]
                if kind == "v":
                    for c in range(KC):
                        hi, lo = wblock(t, c, S)
                        a = slice(P * j, P * (j + 1))
                        last = three(b[:], lat_hi[:, QC + c, a], lat_lo[:, QC + c, a], hi, lo, c == 0, c == KC - 1)
                else:
                    first, chunks, base = {"k": (QC, KC, 0), "q": (0, QC, KC), "rope": (0, QC, KC + QC)}[kind]
                    for c in range(chunks):
                        last = three(b[:], *wblock(t, base + c), lat_hi[:, first + c, :], lat_lo[:, first + c, :],
                                     c == 0, c == chunks - 1)
                last.then_inc(tile_used if ends_tile(u) else unit_done, 1)

            def causal_mask(target, b):
                return pe.matmul(target[:, P * b:P * (b + 1)], ident_r[:], mask_r[:], start=False, stop=True)

            def scores_mla(h):
                g, j = divmod(h, GH)
                pe.wait_ge(unit_evac, UNIT[("q", g, j)] + 1)
                if j == 0:
                    pe.wait_ge(rope_q_in, 256 * (g + 1))
                for b in range(NB):
                    i, at, n = SCORE_BANK[b], SCORE_AT[b], P * (b + 1)
                    if h and b != 1:
                        pe.wait_ge(mla.exped, NB * (h - 1) + (2, 3, 4)[i])
                    target = bank[i][:, at:at + n]
                    a = slice(P * b, P * (b + 1))
                    three(target, q_hi[:, j, a], q_lo[:, j, a], k_hi[:, j, 0:n], k_lo[:, j, 0:n], True, False)
                    pe.matmul(target, rope_q[:, g % 2, j, a], rope_k_hi[:, 0:n], start=False, stop=False)
                    pe.matmul(target, rope_q[:, g % 2, j, a], rope_k_lo[:, 0:n], start=False, stop=False)
                    last = causal_mask(target, b)
                    if b:
                        last.then_inc(mla.scores, 1)

            def transposes(s, h, source, ready, value):
                pe.wait_ge(ready, value)
                for b in range(NB):
                    if NB * h + b >= 2:
                        pe.wait_ge(s.prob_t_lo, NB * h + b - 1)
                    for q in range(b, NB):
                        last = pe.transpose(bank[3 + b % 2][:, P * (q - b):P * (q - b + 1)],
                                            source[:, ROW[q] + P * b:ROW[q] + P * (b + 1)], ident[:])
                    last.then_inc(s.transposed, 1)

            def weigh_mla(h):
                if h:
                    pe.wait_ge(mla.out, h)
                j = h % GH
                pe.wait_ge(unit_evac, UNIT[("v", h // GH, NB - 1)] + 1)
                for b in range(NB):
                    pe.wait_ge(mla.prob_t_lo, NB * h + b + 1)
                    a = slice(VD * j, VD * (j + 1))
                    r = slice(COLUMN[b], COLUMN[b + 1])
                    last = three(bank[5][:, P * b:S], v_hi[:, b, a], v_lo[:, b, a], prob_t_hi[:, r], prob_t_lo[:, r],
                                 b == 0, b == NB - 1)
                last.then_inc(mla.weighted, 1)

            def prepare(g, j):
                unit(("k", g, j))
                unit(("q", g, j))
                if j < 2:
                    unit(("rope", g, j))
                if j == GH - 1:
                    for b in range(NB):
                        unit(("v", g, b))

            pe.wait_ge(made, 3)
            pe.wait_ge(lat_lo_done, LC)
            pe.wait_ge(mla_evac, LC + 2 + PC)
            pe.wait_ge(rope_k_lo_done, 1)
            for j in range(GH):
                prepare(0, j)
            scores_mla(0)
            for h in range(HEADS):
                g, j = h // GH + 1, h % GH
                transposes(mla, h, prob, probs, NB * (h + 1))
                if h + 1 < HEADS:
                    scores_mla(h + 1)
                weigh_mla(h)
                if g < GROUPS:
                    prepare(g, j)
            out_product("mla_out", PC, lambda turn, j: (y_hi[:, j % RING, :], y_lo[:, j % RING, :]),
                        y_lo_done, lambda turn, j: turn * RING + (PC + j + 1),
                        free=[[(mla.out, HEADS)]] + [[]] * 7)

            n = norm["mix"]
            for u in range(8):
                if u >= 4:
                    pe.wait_ge(qk_ready, u - 3)
                projection("mix_qk", 0, u, bank[u % 4], mix_xg_hi, mix_xg_lo, n.xg_lo if u == 0 else None)
                if u == 0:
                    for i in range(2):
                        mean(n.summed, 2 * (DC - 1), mix_sqsum[:, i, :], bank[6 + i], n.mean)
                if u == 1:
                    pe.wait_ge(inv_both, 1)
                    for b in range(NB):
                        last = pe.matmul(bank[5][:, b:b + 1], inv[0:1, P * b:P * (b + 1)], ones[0:1, 0:1], start=True, stop=True)
                    last.then_inc(inv_t_sum, 1)

            def token_major(stage, first_tile, banks, free):
                for i in range(4):
                    t = TILE[stage] + first_tile + i
                    wait_tile(0, t)
                    for b in range(NB):
                        if i == 0:
                            pe.wait_ge(*free[b])
                        for c in range(2):
                            k = 2 * i + c
                            hi, lo = wblock(t, c, S)
                            a = slice(P * b, P * (b + 1))
                            last = three(banks[b][:], mix_xg_hi[:, k, a], mix_xg_lo[:, k, a], hi, lo, k == 0, k == DC - 1)
                        if i == 3 and b < NB - 1:
                            last.then_inc(token_summed, 1)
                    last.then_inc(tile_used, 1)

            token_major("mix_v", 0, bank[0:4], [(qk_ready, 5 + b) for b in range(NB)])
            pe.wait_ge(made, 5)
            pe.wait_ge(inv_t_ready, 1)
            for b in range(NB):
                for k in range(DC):
                    c = slice(FOX_HEADS * k, FOX_HEADS * (k + 1))
                    a = slice(P * b, P * (b + 1))
                    last = three(bank[5][:, 8 * b:8 * b + 8], mix_xg_hi[:, k, a], mix_xg_lo[:, k, a],
                                 w_f_hi[:, c], w_f_lo[:, c], k == 0, k == DC - 1)
            last.then_inc(f_summed, 1)
            token_major("mix_z", 0, bank[0:4], [(fv_lo_done, b + 1) for b in range(NB)])
            pe.wait_ge(log_f_ready, 1)
            for t in range(NB):
                for b in range(t + 1):
                    last = pe.matmul(bank[6][0:FOX_HEADS, P * t:P * (t + 1)], log_f[:, b, :],
                                     (upper if b == t else ones)[:], start=b == 0, stop=b == t)
            last.then_inc(c_summed, 1)
            token_major("mix_z", 4, bank[4:8], [(log_f_ready, 1), (log_f_ready, 1), (c_ready, 1), (c_ready, 1)])

            def scores_fox(h):
                pair, half = divmod(h, 2)
                rows = slice(FOX_D * half, FOX_D * (half + 1))
                r = 32 * (h % 4)
                for i, blocks in enumerate(((0, 1), (2,), (3,))):
                    if h:
                        pe.wait_ge(fox.exped, NB * (h - 1) + (2, 3, 4)[i])
                    for b in blocks:
                        n = P * (b + 1)
                        target = bank[i][:, SCORE_AT[b]:SCORE_AT[b] + n]
                        a = slice(P * b, P * (b + 1))
                        three(target, fq_hi[rows, pair, a], fq_lo[rows, pair, a], fk_hi[rows, pair, 0:n],
                              fk_lo[rows, pair, 0:n], True, False)
                        pe.matmul(target, decay_q[r:r + 4, h // 4, a], decay_k[r:r + 4, h // 4, 0:n], start=False, stop=False)
                        last = causal_mask(target, b)
                    last.then_inc(fox.scores, 1)

            def weigh_fox(h):
                if h:
                    pe.wait_ge(fox.out, h)
                a = slice(FOX_D * h, FOX_D * (h + 1))
                pe.wait_ge(fox.prob_t_lo, NB * (h + 1))
                for q in range(NB):
                    target = bank[5][:, FOX_D * q:FOX_D * (q + 1)]
                    for b in range(q + 1):
                        at = COLUMN[b] + P * (q - b)
                        last = three(target, f_prob_t_hi[:, at:at + P], f_prob_t_lo[:, at:at + P],
                                     fv_hi[:, b, a], fv_lo[:, b, a], b == 0, b == q)
                last.then_inc(fox.weighted, 1)

            pe.wait_ge(z_gelu, 2 * NB)
            pe.wait_ge(decay_in, 8 * 16)
            pe.wait_ge(qk_lo, 8)
            scores_fox(0)
            for h in range(FOX_HEADS):
                transposes(fox, h, f_prob, fox.exped, NB * (h + 1))
                if h + 1 < FOX_HEADS:
                    scores_fox(h + 1)
                weigh_fox(h)
                if h == 0:
                    pe.wait_ge(ws_lo_done, 1)
                    pe.wait_ge(zvn_lo_done, NB)
                if h >= 2:
                    pe.wait_ge(sgu_gated, h - 1)
                c = slice(SGU_D * h, SGU_D * (h + 1))
                w = slice(P * h, P * (h + 1))
                three(bank[6 + h % 2][:, 0:NB * SGU_D].rearrange("p (b d) -> p b d", b=NB), ws_hi[:, w], ws_lo[:, w],
                      zvn_hi[:, :, c], zvn_lo[:, :, c], True, True).then_inc(sgu_mixed, 1)
            for i, source in enumerate((zu, attn)):
                pe.wait_ge(branch_scaled, NB * (i + 1))
                for c in range(AC):
                    if AC * i + c >= 2:
                        pe.wait_ge(merged_lo_done, AC * i + c - 1)
                    for b in range(NB):
                        last = pe.transpose(bank[6 + c % 2][:, P * b:P * (b + 1)], source[:, b, P * c:P * (c + 1)], ident[:])
                    last.then_inc(branch_t, 1)
            out_product("mix_out", DC, lambda turn, j: (merged_hi[:, j, :], merged_lo[:, j, :]), merged_lo_done,
                        lambda turn, j: 2 * AC, free=[[]] * 8)

            n = norm["ffn"]
            for turn, j in sweep(pe, 2 * FC):
                if not starts(turn, j, 4):
                    pe.wait_ge(ffn_evac, turn * RING + (j - 3))
                projection("ffn_up", turn, j, bank[j % 4], ffn_xg_hi, ffn_xg_lo, n.xg_lo if starts(turn, j, 1) else None)
                if starts(turn, j, 1):
                    mean(n.summed, DC - 1, ffn_sqsum[:], bank[MEAN_BANK], n.mean)
            out_product("ffn_down", FC, lambda turn, j: (act_hi[:, turn * RING + j, :], act_lo[:, turn * RING + j, :]),
                        act_lo_done, lambda turn, j: turn * RING + (j + 1),
                        free=[[(ffn_evac, 2 * FC)]] + [[]] * 7)
            mean(norm["final"].summed, DC - 1, fin_sqsum[:], bank[0], norm["final"].mean)


def kernel(x, positions, pool_norm, pool_w_in, pool_w_group, pool_scale, pool_w_out, mla_norm, mla_w_in,
           mla_q_norm, mla_w_q_b, mla_kv_norm, mla_w_kv_b, mla_w_out, final_norm, mix_norm_g_2, w_in_2, b_f_2,
           sgu_ln_g_2, sgu_ln_b_2, w_s_2, b_s_2, out_norm_g_2, w_out_2, ffn_norm_g_2, w_gate_up_2, w_down_2,
           final_norm_g_2):
    import concourse.bacc as bacc
    from concourse.bass_utils import run_bass_kernel_spmd

    (x, positions, pool_norm, pool_w_in, pool_w_group, pool_scale, pool_w_out, mla_norm, mla_w_in, mla_q_norm,
     mla_w_q_b, mla_kv_norm, mla_w_kv_b, mla_w_out, mix_norm, w_in, b_f, ln_g, ln_b, w_s, b_s, out_norm, w_out,
     ffn_norm, w_gate_up, w_down) = (
        np.asarray(a)[0] for a in (
            x, positions, pool_norm, pool_w_in, pool_w_group, pool_scale, pool_w_out, mla_norm, mla_w_in,
            mla_q_norm, mla_w_q_b, mla_kv_norm, mla_w_kv_b, mla_w_out, mix_norm_g_2, w_in_2, b_f_2, sgu_ln_g_2,
            sgu_ln_b_2, w_s_2, b_s_2, out_norm_g_2, w_out_2, ffn_norm_g_2, w_gate_up_2, w_down_2))
    final_norm, final_norm_2 = np.asarray(final_norm), np.asarray(final_norm_g_2)

    stream = np.zeros((N_TILES, P, 8 * P), np.float32)

    def put(tile, at, part):
        stream[tile, :, at:at + part.shape[1]] = part

    def rows(w, k):
        return w[P * k:P * (k + 1)]

    def outputs(tile, w, at=0):
        for k in range(w.shape[0] // P):
            put(tile, at + P * k, rows(w, k))

    for n in range(2 * PC):
        outputs(TILE["pool_u"] + n, pool_w_in[:, P * n:P * (n + 1)])
    for c in range(PC):
        g, n = divmod(c, PG)
        outputs(TILE["pool_group"] + c // 2, pool_w_group[g][:, P * n:P * (n + 1)], PG * P * (c % 2))
    for name, w in (("pool_out", pool_w_out), ("mla_out", mla_w_out), ("mix_out", w_out), ("ffn_down", w_down)):
        for k in range(w.shape[0] // P):
            put(TILE[name] + k, 0, rows(w, k))
    t = TILE["mla_in"]
    for n in range(LC):
        outputs(t + n, mla_w_in[:, P * n:P * (n + 1)])
    half_1 = mla_w_in[:, LC * P:LC * P + HALF]
    half_2 = mla_w_in[:, LC * P + HALF:LC * P + ROPE]
    outputs(t + LC, np.concatenate([half_1, half_2] * 2, axis=1))
    outputs(t + LC + 1, np.concatenate([half_2, half_1] * 2, axis=1))
    for n in range(PC):
        at = LC * P + ROPE + P * n
        outputs(t + LC + 2 + n, mla_w_in[:, at:at + P])
    w_q = mla_w_q_b.reshape(QC * P, HEADS, NOPE + ROPE)
    w_kv = mla_w_kv_b.reshape(KC * P, HEADS, NOPE + VD)
    for g in range(GROUPS):
        t = TILE["heads"] + 5 * g
        group = slice(GH * g, GH * (g + 1))
        for j in range(GH):
            outputs(t + j, w_kv[:, GH * g + j, 0:NOPE])
            outputs(t + j, w_q[:, GH * g + j, 0:NOPE], KC * P)
            if j < 2:
                at = NOPE + HALF * j
                outputs(t + j, w_q[:, group, at:at + HALF].reshape(QC * P, P), (KC + QC) * P)
        w_v = w_kv[:, group, NOPE:].reshape(KC * P, S)
        for k in range(KC):
            put(t + GH, S * k, rows(w_v, k))
    for n in range(8):
        outputs(TILE["mix_qk"] + n, w_in[:, P * n:P * (n + 1)])
    gates = 3 * D_ATTN
    for name, first, at in (("mix_v", 0, 2 * D_ATTN), ("mix_z", 0, gates + FOX_HEADS), ("mix_z", 4, gates + FOX_HEADS + D_SGU)):
        for k in range(DC):
            put(TILE[name] + first + k // 2, S * (k % 2), rows(w_in, k)[:, at:at + S])
    for n in range(FC):
        outputs(TILE["ffn_up"] + 2 * n, w_gate_up[:, P * n:P * (n + 1)])
        outputs(TILE["ffn_up"] + 2 * n + 1, w_gate_up[:, FF + P * n:FF + P * (n + 1)])

    def as_columns(v):
        return v.reshape(-1, P).T

    inv_freq = (1.0 / (10000.0 ** (np.arange(0, ROPE, 2, dtype=np.float32) / np.float32(ROPE)))).astype(np.float32)
    sign = np.repeat(np.array([-1, 1, -1, 1], np.float32), HALF)
    columns = np.concatenate([as_columns(v) for v in (
        pool_norm, pool_scale, mla_norm, mla_q_norm, mla_kv_norm, final_norm, mix_norm, out_norm, ffn_norm,
        final_norm_2, b_s, np.tile(inv_freq, GH), sign)], axis=1)
    counts = np.tile((1.0 / np.arange(1, PAD + 1)).astype(np.float32), (P, 1))
    lines = np.tile(np.concatenate([b_f, ln_g, ln_b]), (P, 1))
    w_f = w_in[:, gates:gates + FOX_HEADS].reshape(DC, P, FOX_HEADS).transpose(1, 0, 2).reshape(P, -1)
    arrays = {
        "x_in": x.T.reshape(DC, P, S).transpose(1, 0, 2),
        "stream": stream,
        "columns": columns,
        "counts_in": counts,
        "positions_in": np.tile(positions, (P, 1)),
        "lines": lines,
        "w_s": w_s.transpose(2, 0, 1).reshape(P, SGU_G * P),
        "w_f": w_f,
    }
    arrays = {k: np.ascontiguousarray(v) for k, v in arrays.items()}

    nc = bacc.Bacc("TRN2", target_bir_lowering=False, num_devices=1)
    args = [nc.dram_tensor(k, v.shape, mybir.dt.from_np(v.dtype), kind="ExternalInput").ap() for k, v in arrays.items()]
    spill = nc.dram_tensor("spill", (P, DC, S), mybir.dt.float32, kind="Internal").ap()
    out = nc.dram_tensor("out", (P, DC, S), mybir.dt.float32, kind="ExternalOutput").ap()
    build(nc, *args, spill, out)
    r = run_bass_kernel_spmd(nc, [arrays], core_ids=[0])
    return r.results[0]["out"].transpose(1, 0, 2).reshape(D, S).T.reshape(1, S, D)
```

```python
from contextlib import ExitStack

import numpy as np

import concourse.bass as bass
from concourse import mybir

P = 128
S = 512
NB = S // P
D = 1024
DC = D // P
POOL_W = 2048
WINDOWS = (2, 4, 8, 16)
PAD = max(WINDOWS)
PC = POOL_W // P
PG = PC // len(WINDOWS)
HEADS, NOPE, ROPE, VD = 16, 128, 64, 128
HALF = ROPE // 2
QC, KC = 384 // P, 256 // P
LC = QC + KC
MLA_SCALE = float(NOPE + ROPE) ** -0.5
GH = P // HALF
GROUPS = HEADS // GH
FOX_HEADS, FOX_D = 8, 64
FOX_PAIRS = FOX_HEADS // 2
D_ATTN = FOX_HEADS * FOX_D
SGU_G, SGU_D = 8, 64
D_SGU = SGU_G * SGU_D
AC = D_ATTN // P
SC = D_SGU // P
SGU_HALF = 64
FF = 2816
FC = FF // P
EPS = 1e-6
MASKED = -1e30
ROW = [P * b * (b + 1) // 2 for b in range(NB + 1)]
COLUMN = [sum(S - P * c for c in range(b)) for b in range(NB + 1)]
SCORE_BANK = (0, 0, 1, 2)
SCORE_AT = (0, P, 0, 0)
TWO_PI = 6.283185307179586
TWO_PI_PARTS = (6.28125, 0.0019340515136718750, 1.2556659146e-06)
ROUNDER = 12582912.0

COLUMN_SIZES = (("pool_norm", DC), ("pool_scale", PC), ("mla_norm", DC), ("q_norm", QC), ("kv_norm", KC),
                ("final_norm", DC), ("mix_norm", DC), ("out_norm", DC), ("ffn_norm", DC),
                ("final_norm_2", DC), ("b_s", SGU_G), ("inv_freq", 1), ("rope_sign", 1))
COLUMNS = {name: sum(n for _, n in COLUMN_SIZES[:i]) for i, (name, _) in enumerate(COLUMN_SIZES)}
N_COLUMNS = sum(n for _, n in COLUMN_SIZES)

TILE_SIZES = (("pool_u", PC), ("pool_z", PC), ("pool_group", PC * PG // 8), ("pool_out", PC), ("mla_in", LC + 2 + PC),
              ("heads", 5 * GROUPS), ("mla_out", PC), ("mix_qk", 9), ("mix_v", 4), ("mix_z", 8),
              ("mix_out", DC), ("ffn_up", 2 * FC), ("ffn_down", FC))
TILE = {name: sum(n for _, n in TILE_SIZES[:i]) for i, (name, _) in enumerate(TILE_SIZES)}
N_TILES = sum(n for _, n in TILE_SIZES)
RING = 4
RAW = 2
AHEAD = RING - 1


GROUP_TILES = ((("k", 0), ("rope", 0), ("rope", 1)), (("k", 1), ("q", 0), ("q", 1)), (("k", 2), ("q", 2)),
               (("k", 3), ("q", 3)), tuple(("v", b) for b in range(NB)))
UNITS = [(kind, g, j) for g in range(GROUPS) for tile in GROUP_TILES for kind, j in tile]
UNIT = {u: i for i, u in enumerate(UNITS)}
CHUNKS_OF = {"k": KC, "q": QC, "rope": QC}


def unit_place(kind, j):
    for i, tile in enumerate(GROUP_TILES):
        if (kind, j) in tile:
            before = tile[:tile.index((kind, j))]
            return i, 0 if kind == "v" else sum(CHUNKS_OF[k] for k, _ in before)


def sweep(engine, n, tail=0, first=0):
    turn_1, turns = max(1, -(-first // RING)), (n - tail) // RING
    done = min(turn_1 * RING, n)
    for unit in range(first, done):
        yield 0, unit
    if turns > turn_1 + 1:
        with engine.Fori(turn_1, turns) as turn:
            for j in range(RING):
                yield turn, j
        done = turns * RING
    for unit in range(done, n):
        yield 0, unit


def starts(turn, j, n):
    return isinstance(turn, int) and j < n


class NormSemaphores:
    def __init__(self, sem, stage, before, common):
        self.before = before
        self.mean, self.prepared, self.inv = common
        self.x_ready = sem(f"{stage}_x_ready") if stage != "pool" else None
        self.xg_hi = sem(f"{stage}_xg_hi") if stage != "final" else None
        self.xg_lo = sem(f"{stage}_xg_lo") if stage != "final" else None
        self.squared = sem(f"{stage}_squared")
        self.summed = sem(f"{stage}_summed")


class HeadSemaphores:
    def __init__(self, sem, kind):
        self.scores = sem(f"{kind}_scores")
        self.peaks = sem(f"{kind}_peaks")
        self.exped = sem(f"{kind}_exped")
        self.transposed = sem(f"{kind}_transposed")
        self.prob_t_hi = sem(f"{kind}_prob_t_hi")
        self.prob_t_lo = sem(f"{kind}_prob_t_lo")
        self.weighted = sem(f"{kind}_weighted")
        self.out = sem(f"{kind}_out")


def build(nc, x_in, stream, columns, counts_in, positions, rows_in, w_s, spill, out):
    f32, f32r, i32 = mybir.dt.float32, mybir.dt.float32r, mybir.dt.int32
    ACT = mybir.ActivationFunctionType
    ALU = mybir.AluOpType
    X = mybir.AxisListType.X
    ctx = ExitStack()
    with ctx:
        def sem(name):
            return ctx.enter_context(nc.semaphore(name))

        def sb(name, shape, dtype=f32):
            return ctx.enter_context(nc.sbuf_tensor(name, shape, dtype))

        def place(kib, name, shape, dtype=f32):
            with ExitStack() as s:
                if kib:
                    s.enter_context(nc.sbuf_tensor(f"below_{name}", [P, int(kib * 256)], f32))
                return s.enter_context(nc.sbuf_tensor(name, shape, dtype))

        def plain(ap):
            return ap.bitcast(f32)

        raw = sb("raw", [P, RAW, 1024])
        w_hi = sb("w_hi", [P, RING, 1024], f32r)
        w_lo = sb("w_lo", [P, RING, 1024], f32r)
        cols = sb("cols", [P, N_COLUMNS])
        counts = sb("counts", [P, PAD])
        gain12 = sb("gain12", [P, DC])
        ident = sb("ident", [P, P])
        ident_r = sb("ident_r", [P, P], f32r)
        mask = sb("mask", [P, P])
        mask_r = sb("mask_r", [P, P], f32r)
        upper = sb("upper", [P, P])
        ones = sb("ones", [P, P])
        inv = sb("inv", [P, S])
        mean_sq = sb("mean_sq", [P, S])
        peak = sb("peak", [P, 2, NB])
        neg_peak = sb("neg_peak", [P, 2, NB])
        row_sum = sb("row_sum", [P, 2, NB])
        inv_sum = sb("inv_sum", [P, 2, NB])
        inv_t = sb("inv_t", [P, NB])
        b_f = sb("b_f", [P, FOX_HEADS])
        gate = sb("gate", [P, NB, FOX_HEADS])
        gate_abs = sb("gate_abs", [P, NB, FOX_HEADS])
        log_f = sb("log_f", [P, NB, FOX_HEADS])
        stats = sb("stats", [P, NB, 6])
        moments = sb("moments", [P, NB, 2])
        rstd = sb("rstd", [P, NB])
        branch_sq = sb("branch_sq", [P, NB])
        branch_inv = sb("branch_inv", [P, NB])

        x = place(0, "x", [P, DC, S])
        z = place(16, "z", [P, PC, S])
        pool_xg_hi, pool_xg_lo = (place(48 + 16 * i, f"pool_xg_{i}", [P, DC, S], f32r) for i in range(2))
        pooled_hi, pooled_lo = (place(80 + 32 * i, f"pooled_{i}", [P, PC, S], f32r) for i in range(2))
        pool_sq, pool_sqsum = place(144, "pool_sq", [P, 2, S]), place(148, "pool_sqsum", [P, S])
        u_pad = place(144, "u_pad", [P, 2, PAD + S])
        sum_a, sum_b = place(148.25, "sum_a", [P, PAD + S]), place(150.5, "sum_b", [P, PAD + S])
        pooled = place(152.75, "pooled", [P, 2, S])
        y_hi, y_lo = (place(80 + 8 * i, f"y_{i}", [P, RING, S], f32r) for i in range(2))
        lat_hi, lat_lo = (place(48 + 10 * i, f"lat_{i}", [P, LC, S], f32r) for i in range(2))
        rope_k_hi, rope_k_lo = (place(68 + 2 * i, f"rope_k_{i}", [P, S], f32r) for i in range(2))
        cos, sin = place(72, "cos", [P, S]), place(74, "sin", [P, S])
        rope_a, rope_b = place(76, "rope_a", [P, S]), place(78, "rope_b", [P, S])
        lat = place(96, "lat", [P, LC, S])
        mla_xg_hi, mla_xg_lo = (place(106 + 16 * i, f"mla_xg_{i}", [P, DC, S], f32r) for i in range(2))
        mla_sq, mla_sqsum = place(138, "mla_sq", [P, 2, S]), place(142, "mla_sqsum", [P, S])
        pos_i, angle = place(144, "pos_i", [P, S], i32), place(146, "angle", [P, S])
        turns_of, reduced = place(148, "turns_of", [P, S]), place(150, "reduced", [P, S])
        lat_sq, lat_sqsum = place(144, "lat_sq", [P, LC, S]), place(154, "lat_sqsum", [P, 2, S])
        v_hi, v_lo = (place(8 * i, f"v_{i}", [P, NB, S], f32r) for i in range(2))
        k_hi, k_lo = (place(76 + 8 * i, f"k_{i}", [P, GH, S], f32r) for i in range(2))
        q_hi, q_lo = (place(92 + 8 * i, f"q_{i}", [P, GH, S], f32r) for i in range(2))
        rope_q = place(108, "rope_q", [P, 2, GH, S], f32r)
        prob = place(124, "prob", [P, ROW[NB]])
        prob_t_hi, prob_t_lo = (place(129 + 5 * i, f"prob_t_{i}", [P, COLUMN[NB]], f32r) for i in range(2))
        turned_1, turned_2 = place(139, "turned_1", [P, S]), place(141, "turned_2", [P, S])
        rope_t = place(143, "rope_t", [P, S])
        turned_hi, turned_lo = (place(145 + 4 * i, f"turned_hl_{i}", [P, 2, S], f32r) for i in range(2))
        fq_hi, fq_lo = (place(16 + 8 * i, f"fq_{i}", [P, FOX_PAIRS, S], f32r) for i in range(2))
        fk_hi, fk_lo = (place(32 + 8 * i, f"fk_{i}", [P, FOX_PAIRS, S], f32r) for i in range(2))
        fv_hi, fv_lo = (place(48 + 8 * i, f"fv_{i}", [P, NB, D_ATTN], f32r) for i in range(2))
        decay_q = place(64, "decay_q", [P, 2, S], f32r)
        decay_k = place(68, "decay_k", [P, 2, S], f32r)
        ln_g, ln_b = place(72, "ln_g", [P, D_SGU]), place(74, "ln_b", [P, D_SGU])
        inv_1 = place(78, "inv_1", [P, S])
        zu, zv = place(80, "zu", [P, NB, D_SGU]), place(88, "zv", [P, NB, D_SGU])
        zvn_hi, zvn_lo = place(128, "zvn_hi", [P, NB, D_SGU], f32r), place(88, "zvn_lo", [P, NB, D_SGU], f32r)
        mix_xg_hi, mix_xg_lo = (place(96 + 16 * i, f"mix_xg_{i}", [P, DC, S], f32r) for i in range(2))
        mix_sq, mix_sqsum = place(128, "mix_sq", [P, 2, 2, S]), place(136, "mix_sqsum", [P, 2, S])
        c_parts = place(128, "c_parts", [FOX_HEADS, 4, S], f32r)
        ws_raw, ws_lo = place(141, "ws_raw", [P, SGU_G * P]), place(141, "ws_lo", [P, SGU_G * P], f32r)
        ws_hi = place(76, "ws_hi", [P, SGU_G * P], f32r)
        f_prob = place(136, "f_prob", [P, ROW[NB]])
        f_prob_t_hi, f_prob_t_lo = (place(145 + 5 * i, f"f_prob_t_{i}", [P, COLUMN[NB]], f32r) for i in range(2))
        qk_t, f_t = place(149, "qk_t", [P, 2, S]), place(155, "f_t", [P, S])
        junk = place(155, "junk", [P, S])
        attn = place(16, "attn", [P, FOX_PAIRS, S])
        attn_hi, attn_lo = (place(32 + 8 * i, f"attn_{i}", [P, FOX_PAIRS, S], f32r) for i in range(2))
        sgu_hi, sgu_lo = (place(48 + 8 * i, f"sgu_{i}", [P, SC, S], f32r) for i in range(2))
        attn_sq, attn_sqsum = place(64, "attn_sq", [P, FOX_PAIRS, S]), place(72, "attn_sqsum", [P, S])
        attn_inv, mixed = place(74, "attn_inv", [P, S]), place(76, "mixed", [P, 2, S])
        ffn_xg_hi, ffn_xg_lo = (place(104 + 16 * i, f"ffn_xg_{i}", [P, DC, S], f32r) for i in range(2))
        ffn_sq, ffn_sqsum = place(136, "ffn_sq", [P, 2, S]), place(140, "ffn_sqsum", [P, S])
        act_hi, act_lo = (place(16 + 44 * i, f"act_{i}", [P, FC, S], f32r) for i in range(2))
        gated, up = place(142, "gated", [P, 2, S]), place(146, "up", [P, 2, S])
        fin_sq, fin_sqsum = place(104, "fin_sq", [P, 2, S]), place(108, "fin_sqsum", [P, S])

        bank = [ctx.enter_context(nc.psum_tensor(f"bank{b}", [P, S], f32)) for b in range(8)]
        MEAN_BANK = 7

        def col(name, k=0):
            at = COLUMNS[name] + k
            return cols[:, at:at + 1]

        tile_loaded = [sem(f"tile_loaded_{i}") for i in range(RAW)]
        tile_hi, tile_lo, tile_used = sem("tile_hi"), sem("tile_lo"), sem("tile_used")
        cols_in, small_in, ln_in = sem("cols_in"), sem("small_in"), sem("ln_in")
        patterns, made = sem("patterns"), sem("made")
        x_loaded = [sem(f"x_loaded_{i}") for i in range(4)]
        common = sem("norm_mean"), sem("norm_prepared"), sem("norm_inv")
        norm = {n: NormSemaphores(sem, n, before, common)
                for n, before in (("pool", 0), ("mla", 1), ("mix", 2), ("ffn", 4), ("final", 5))}
        steps = sem("dve_steps")
        asteps = sem("act_steps")
        in_evac, pooled_ready = sem("in_evac"), sem("pooled_ready")
        pooled_hi_done, pooled_lo_done = sem("pooled_hi_done"), sem("pooled_lo_done")
        z_silu = sem("z_silu")
        half_tile = sem("half_tile")
        y_ready = sem("y_ready")
        y_hi_done, y_lo_done = sem("y_hi_done"), sem("y_lo_done")
        Y_BEFORE = {"pool_out": 0, "mla_out": PC}
        bank_done = {n: sem(f"{n}_bank_done") for n in ("pool_out", "mla_out", "ffn_down")}
        pos_in, angle_ready, table_done = sem("pos_in"), sem("angle_ready"), sem("table_done")
        mla_evac, lat_squared, lat_summed = sem("mla_evac"), sem("lat_squared"), sem("lat_summed")
        lat_mean, lat_prepared, lat_inv = sem("lat_mean"), sem("lat_prepared"), sem("lat_inv")
        lat_ready, lat_hi_done, lat_lo_done = sem("lat_ready"), sem("lat_hi_done"), sem("lat_lo_done")
        rope_k_ready, rope_k_hi_done, rope_k_lo_done = sem("rope_k_ready"), sem("rope_k_hi_done"), sem("rope_k_lo_done")
        mz_silu = sem("mz_silu")
        x_spilled, x_back = sem("x_spilled"), sem("x_back")
        unit_done, unit_hi, unit_evac = sem("unit_done"), sem("unit_hi"), sem("unit_evac")
        turned, turned_hi_done, turned_lo_done, rope_q_in = sem("turned"), sem("turned_hi_done"), sem("turned_lo_done"), sem("rope_q_in")

        mla, fox = HeadSemaphores(sem, "mla_head"), HeadSemaphores(sem, "fox_head")
        probs = sem("mla_head_probs")
        qk_ready, qk_hi, qk_lo = sem("qk_ready"), sem("qk_hi"), sem("qk_lo")
        inv_t_sum, inv_t_ready = sem("inv_t_sum"), sem("inv_t_ready")
        v_summed, fv_hi_done, fv_lo_done = sem("v_summed"), sem("fv_hi_done"), sem("fv_lo_done")
        f_summed, gate_abs_ready, gate_log, log_f_ready = sem("f_summed"), sem("gate_abs_ready"), sem("gate_log"), sem("log_f_ready")
        c_summed, c_hi_done, c_ready, decay_in = sem("c_summed"), sem("c_hi_done"), sem("c_ready"), sem("decay_in")
        f_ready, x_scaled = sem("f_ready"), sem("x_scaled")
        inv_both, decay_ones = sem("inv_both"), sem("decay_ones")
        z_gelu = sem("z_gelu")
        ln_prepared, ln_rstd, zvn_ready, zvn_hi_done, zvn_lo_done = (sem(n) for n in ("ln_prepared", "ln_rstd", "zvn_ready", "zvn_hi_done", "zvn_lo_done"))
        ws_in, ws_cut, ws_hi_done, ws_lo_done = sem("ws_in"), sem("ws_cut"), sem("ws_hi_done"), sem("ws_lo_done")
        sgu_mixed, sgu_gated = sem("sgu_mixed"), sem("sgu_gated")
        branch_squared, branch_prepared, branch_inv_done, branch_scaled = (sem(n) for n in ("branch_squared", "branch_prepared", "branch_inv_done", "branch_scaled"))
        branch_t, sgu_hi_done, sgu_lo_done = sem("branch_t"), sem("sgu_hi_done"), sem("sgu_lo_done")
        attn_hi_done, attn_lo_done = sem("attn_hi_done"), sem("attn_lo_done")
        attn_squared, attn_summed, attn_mean, attn_prepared, attn_inv_done = (sem(n) for n in ("attn_squared", "attn_summed", "attn_mean", "attn_prepared", "attn_inv_done"))
        ffn_evac, gate_silu, act_ready, act_hi_done, act_lo_done = (sem(n) for n in ("ffn_evac", "gate_silu", "act_ready", "act_hi_done", "act_lo_done"))
        out_ready, stored = sem("out_ready"), sem("stored")

        def unit_tile(u):
            return TILE["heads"] + 5 * u[1] + unit_place(u[0], u[2])[0]

        def ends_tile(u):
            return GROUP_TILES[unit_place(u[0], u[2])[0]][-1] == (u[0], u[2])

        def wait_unit(engine, u):
            if ends_tile(u):
                engine.wait_ge(tile_used, unit_tile(u) + 1)
            else:
                engine.wait_ge(unit_done, sum(not ends_tile(o) for o in UNITS[:UNIT[u] + 1]))

        def hi_units(u):
            return sum(o[0] != "rope" for o in UNITS[:UNIT[u] + 1])

        block = ctx.enter_context(nc.Block())

        @block.sync
        def _(sp):
            for i in range(4):
                sp.dma_start(x[:, 2 * i:2 * i + 2, :], x_in[:, 2 * i:2 * i + 2, :]).then_inc(x_loaded[i], 16)
                if i == 0:
                    sp.dma_start(raw[:, 0, :], stream[0]).then_inc(tile_loaded[0], 16)
                if i == 3:
                    sp.dma_start(raw[:, 1, :], stream[1]).then_inc(tile_loaded[1], 16)
            def load(turn, j):
                if not starts(turn, j, RAW):
                    sp.wait_ge(tile_lo, turn * RING + (j - RAW + 1))
                    sp.dma_start(raw[:, j % RAW, :], stream[turn * RING + j]).then_inc(tile_loaded[j % RAW], 16)

            def rope_rows(g, part):
                if part == 0:
                    sp.wait_ge(turned_hi_done, 2 * g + 2)
                else:
                    sp.wait_ge(turned_lo_done, 2 * g + 2)
                for i in range(2):
                    source, at = (turned_hi, turned_lo)[part], HALF * (2 * part + i)
                    for h in range(GH):
                        sp.dma_start(plain(rope_q[at:at + HALF, g % 2, h, :]),
                                     plain(source[HALF * h:HALF * h + HALF, i, :])).then_inc(rope_q_in, 16)

            for turn, j in sweep(sp, TILE["heads"] + 4):
                load(turn, j)
            for i in range(5 * GROUPS):
                load(0, TILE["heads"] + 4 + i)
                if i % 5 < 2:
                    rope_rows(i // 5, i % 5)
            for turn, j in sweep(sp, N_TILES, first=TILE["mla_out"] + 4):
                load(turn, j)

        @block.gpsimd
        def _(pool):
            pool.memset(ident[:], 0.0).then_inc(patterns, 1)
            pool.memset(mask[:], 0.0).then_inc(patterns, 1)
            pool.memset(upper[:], 1.0).then_inc(patterns, 1)
            pool.wait_ge(patterns, 3)
            pool.affine_select(out=ident[:], in_=ident[:], compare_op=ALU.not_equal, fill=1.0, base=0,
                               pattern=[[-1, P]], channel_multiplier=1).then_inc(patterns, 1)
            pool.affine_select(out=mask[:], in_=mask[:], compare_op=ALU.is_ge, fill=MASKED, base=0,
                               pattern=[[-1, P]], channel_multiplier=1).then_inc(patterns, 1)
            pool.affine_select(out=upper[:], in_=upper[:], compare_op=ALU.is_ge, fill=0.0, base=0,
                               pattern=[[1, P]], channel_multiplier=-1).then_inc(patterns, 1)
            for turn, j in sweep(pool, N_TILES):
                pool.wait_ge(tile_hi, turn * RING + (j + 1))
                pool.tensor_tensor(w_lo[:, j % RING, :], raw[:, j % RAW, :], plain(w_hi[:, j % RING, :]),
                                   ALU.subtract).then_inc(tile_lo, 1)

        @block.scalar
        def _(act):
            own = [0]

            def settle(instruction):
                own[0] += 1
                instruction.then_inc(asteps, 1)
                act.wait_ge(asteps, own[0])

            def split_tile(stage, turn, j):
                t = TILE[stage] + j + AHEAD
                if isinstance(turn, int) and t >= N_TILES:
                    return
                act.wait_ge(tile_loaded[t % RAW], turn * (16 * RING // RAW) + 16 * (t // RAW + 1))
                if not starts(turn, t, RING):
                    act.wait_ge(tile_used, turn * RING + (t - RING + 1))
                act.activation(w_hi[:, t % RING, :], raw[:, t % RAW, :], ACT.Copy).then_inc(tile_hi, 1)

            def norm_in_chunk(n, k, xg, sq, sqsum, gain, loaded=None):
                if loaded:
                    act.wait_ge(loaded[k // 2], 16)
                else:
                    act.wait_ge(n.x_ready, k + 1)
                act.activation(xg[:, k, :], x[:, k, :], ACT.Copy, scale=gain(k)).then_inc(n.xg_hi, 1)
                if k >= 3:
                    act.wait_ge(n.summed, k - 2)
                act.activation(sq[:, k % 2, :] if k else sqsum[:], x[:, k, :], ACT.Square).then_inc(n.squared, 1)

            def norm_in(*norm_and_memory):
                for k in range(DC):
                    norm_in_chunk(norm_and_memory[0], k, *norm_and_memory[1:])

            def norm_root(n):
                act.wait_ge(n.prepared, n.before + 1)
                act.activation(inv[:], mean_sq[:], ACT.Sqrt).then_inc(n.inv, 1)

            act.dma_start(cols[:], columns).then_inc(cols_in, 16)
            act.dma_start(counts[:], counts_in).then_inc(small_in, 16)
            act.dma_start(b_f[:], rows_in[:, 0:FOX_HEADS]).then_inc(small_in, 16)
            act.wait_ge(cols_in, 16)
            split_tile("pool_u", 0, -3)
            norm_in(norm["pool"], pool_xg_hi, pool_sq, pool_sqsum, lambda k: col("pool_norm", k), x_loaded)
            split_tile("pool_u", 0, -2)
            split_tile("pool_u", 0, -1)
            for n in range(PC):
                split_tile("pool_u", 0, n)
                if n == 0:
                    norm_root(norm["pool"])
                else:
                    act.wait_ge(pooled_ready, n)
                    act.activation(pooled_hi[:, n - 1, :], pooled[:, (n - 1) % 2, :], ACT.Copy).then_inc(pooled_hi_done, 1)
            for n in range(PC):
                split_tile("pool_z", 0, n)
                if n == 0:
                    act.wait_ge(pooled_ready, PC)
                    act.activation(pooled_hi[:, PC - 1, :], pooled[:, (PC - 1) % 2, :], ACT.Copy).then_inc(pooled_hi_done, 1)
                else:
                    act.wait_ge(in_evac, PC + n)
                    act.activation(z[:, n - 1, :], z[:, n - 1, :], ACT.Silu).then_inc(z_silu, 1)
            act.wait_ge(in_evac, 2 * PC)
            act.activation(z[:, PC - 1, :], z[:, PC - 1, :], ACT.Silu).then_inc(z_silu, 1)
            for n in range(PC * PG // 8):
                split_tile("pool_group", 0, n)

            def out_split(stage, ready, before):
                def chunk_hi(turn, k):
                    act.wait_ge(ready, turn * RING + (k + 1))
                    if not starts(turn, k, RING):
                        act.wait_ge(tile_used, turn * RING + (TILE[stage] + k - RING + 1))
                    index = turn * RING + k
                    act.activation(y_hi[:, k % RING, :], z[:, index, :], ACT.Copy).then_inc(y_hi_done, 1)

                before()
                for k in range(AHEAD):
                    chunk_hi(0, k)
                for turn, j in sweep(act, PC, tail=AHEAD):
                    split_tile(stage, turn, j)
                    if not isinstance(turn, int) or j + AHEAD < PC:
                        chunk_hi(turn, j + AHEAD)
                    if stage == "pool_out" and isinstance(turn, int) and j == 3:
                        for i, table in enumerate((sin, cos)):
                            act.wait_ge(angle_ready, i + 1)
                            act.activation(table[:], reduced[:], ACT.Sin).then_inc(table_done, 1)

            def before_pool_out():
                act.wait_ge(tile_used, TILE["pool_out"])
                act.dma_start(pos_i[:], positions).then_inc(pos_in, 16)

            out_split("pool_out", y_ready, before_pool_out)

            norm_in(norm["mla"], mla_xg_hi, mla_sq, mla_sqsum, lambda k: col("mla_norm", k))
            act.dma_start(spill, x[:]).then_inc(x_spilled, 16)
            for u in range(LC + 2 + PC):
                split_tile("mla_in", 0, u)
                if u == 0:
                    norm_root(norm["mla"])
                if 1 <= u <= LC:
                    act.wait_ge(mla_evac, u)
                    act.activation(lat_sq[:, u - 1, :], lat[:, u - 1, :], ACT.Square).then_inc(lat_squared, 1)
                if u == LC + 2:
                    for i in range(2):
                        act.wait_ge(lat_prepared, i + 1)
                        act.activation(lat_sqsum[:, i, :], lat_sqsum[:, i, :], ACT.Sqrt).then_inc(lat_inv, 1)
                    act.wait_ge(rope_k_ready, 1)
                    act.activation(rope_k_hi[:], rope_a[:], ACT.Copy).then_inc(rope_k_hi_done, 1)
                if u == LC + 4:
                    for i in range(LC):
                        act.wait_ge(lat_ready, i + 1)
                        act.activation(lat_hi[:, i, :], lat[:, i, :], ACT.Copy).then_inc(lat_hi_done, 1)
                if u > LC + 2:
                    n = u - LC - 3
                    act.wait_ge(mla_evac, LC + 2 + n + 1)
                    act.activation(z[:, n, :], z[:, n, :], ACT.Silu).then_inc(mz_silu, 1)
            act.wait_ge(mla_evac, LC + 2 + PC)
            act.activation(z[:, PC - 1, :], z[:, PC - 1, :], ACT.Silu).then_inc(mz_silu, 1)

            def unit_high(u):
                kind, g, j = u
                if kind == "v":
                    if u == ("v", 0, 0):
                        act.wait_ge(x_spilled, 16)
                    target = v_hi
                else:
                    target = k_hi if kind == "k" else q_hi
                wait_unit(act, u)
                act.activation(target[:, j, :], bank[6 + UNIT[u] % 2][:], ACT.Copy).then_inc(unit_hi, 1)

            def prepare(g, j):
                for i in (j,) if j < GH - 1 else (j, GH):
                    for n, (kind, k) in enumerate(GROUP_TILES[i]):
                        if kind != "rope":
                            unit_high((kind, g, k))
                        if n == 0:
                            split_tile("heads", 0, 5 * g + i)

            def turn_split(g):
                act.wait_ge(turned, 2 * g + 2)
                if g:
                    act.wait_ge(rope_q_in, 256 * g)
                for i, t in enumerate((turned_1, turned_2)):
                    act.activation(turned_hi[:, i, :], t[:], ACT.Copy).then_inc(turned_hi_done, 1)

            def exps(s, h, target, scale):
                for b in range(NB):
                    act.wait_ge(s.peaks, 3 * h + SCORE_BANK[b] + 1)
                    if b == 0 and h:
                        act.wait_ge(s.transposed, NB * h)
                    n = P * (b + 1)
                    act.activation(target[:, ROW[b]:ROW[b + 1]], bank[SCORE_BANK[b]][:, SCORE_AT[b]:SCORE_AT[b] + n],
                                   ACT.Exp, bias=neg_peak[:, h % 2, b:b + 1], scale=scale,
                                   accum_out=row_sum[:, h % 2, b:b + 1]).then_inc(s.exped, 1)

            def transposed_high(s, h, target):
                if h:
                    act.wait_ge(s.weighted, h)
                for b in range(NB):
                    act.wait_ge(s.transposed, NB * h + b + 1)
                    act.activation(target[:, COLUMN[b]:COLUMN[b + 1]], bank[3 + b % 2][:, 0:S - P * b],
                                   ACT.Copy).then_inc(s.prob_t_hi, 1)

            for j in range(GH):
                if j == 1:
                    turn_split(0)
                prepare(0, j)
            exps(mla, 0, prob, MLA_SCALE)
            for h in range(HEADS):
                g, j = h // GH + 1, h % GH
                transposed_high(mla, h, prob_t_hi)
                if h + 1 < HEADS:
                    exps(mla, h + 1, prob, MLA_SCALE)
                if g < GROUPS:
                    if j == 1:
                        turn_split(g)
                    prepare(g, j)

            def before_mla_out():
                act.wait_ge(mla.weighted, HEADS)
                act.dma_start(x[:], spill).then_inc(x_back, 16)

            out_split("mla_out", mla.out, before_mla_out)

            n = norm["mix"]
            act.dma_start(ln_g[:], rows_in[:, FOX_HEADS:FOX_HEADS + D_SGU]).then_inc(ln_in, 16)
            act.dma_start(ln_b[:], rows_in[:, FOX_HEADS + D_SGU:]).then_inc(ln_in, 16)
            for k in range(DC):
                act.wait_ge(n.x_ready, k + 1)
                act.activation(mix_xg_hi[:, k, :], x[:, k, :], ACT.Copy, scale=gain12[:, k:k + 1]).then_inc(n.xg_hi, 1)
                if k >= 3:
                    act.wait_ge(n.summed, 2 * (k - 2))
                act.activation(mix_sq[:, k % 2, 0, :] if k else mix_sqsum[:, 0, :], x[:, k, :], ACT.Square).then_inc(n.squared, 1)
                act.activation(mix_sq[:, k % 2, 1, :] if k else mix_sqsum[:, 1, :], x[:, k, :], ACT.Square,
                               scale=col("final_norm", k)).then_inc(n.squared, 1)
            act.wait_ge(n.summed, 2 * (DC - 1))
            act.dma_start(ws_raw[:], w_s).then_inc(ws_in, 16)
            for u in range(9):
                split_tile("mix_qk", 0, u)
                if u == 0:
                    act.wait_ge(n.prepared, n.before + 1)
                    act.activation(inv_1[:], mean_sq[:], ACT.Sqrt).then_inc(n.inv, 1)
                    act.wait_ge(n.prepared, n.before + 2)
                    act.activation(inv[:], mean_sq[:], ACT.Sqrt).then_inc(n.inv, 1)
                elif u != 5:
                    m = u if u < 5 else u - 1
                    act.wait_ge(qk_ready, m)
                    target = fq_hi if m <= 4 else fk_hi
                    act.activation(target[:, (m - 1) % 4, :], qk_t[:, (m - 1) % 2, :], ACT.Copy).then_inc(qk_hi, 1)
                if u == 7:
                    act.wait_ge(gate_abs_ready, 1)
                    settle(act.activation(gate_abs[:], gate_abs[:], ACT.Exp, scale=-1.0))
                    act.activation(gate_abs[:], gate_abs[:], ACT.Ln, bias=1.0).then_inc(gate_log, 1)
            split_tile("mix_v", 0, 0)
            act.wait_ge(qk_ready, 8)
            act.activation(fk_hi[:, 3, :], qk_t[:, 1, :], ACT.Copy).then_inc(qk_hi, 1)
            act.wait_ge(c_summed, 1)
            act.activation(c_parts[:, 0, :], bank[6][0:FOX_HEADS, :], ACT.Copy).then_inc(c_hi_done, 1)
            split_tile("mix_v", 0, 1)
            act.wait_ge(decay_ones, 1)
            act.wait_ge(c_ready, 1)
            for s in range(2):
                for part in range(2):
                    act.dma_start(plain(decay_q[part:P:32, s, :]), plain(c_parts[4 * s:4 * s + 4, part, :])).then_inc(decay_in, 16)
                    act.dma_start(plain(decay_k[2 + part:P:32, s, :]), plain(c_parts[4 * s:4 * s + 4, 2 + part, :])).then_inc(decay_in, 16)
            split_tile("mix_v", 0, 2)
            act.wait_ge(ws_cut, 1)
            act.wait_ge(x_scaled, 1)
            act.activation(ws_hi[:], ws_raw[:], ACT.Copy).then_inc(ws_hi_done, 1)
            split_tile("mix_v", 0, 3)
            act.wait_ge(inv_t_ready, 1)
            for b in range(NB):
                if b == NB - 1:
                    act.wait_ge(tile_used, TILE["mix_z"])
                else:
                    act.wait_ge(v_summed, b + 1)
                act.activation(fv_hi[:, b, :], bank[b][:], ACT.Copy, scale=inv_t[:, b:b + 1]).then_inc(fv_hi_done, 1)

            def gelu(c):
                act.wait_ge(tile_used, TILE["mix_z"] + 2 * c + 2)
                half = slice(D_SGU // 2 * (c % 2), D_SGU // 2 * (c % 2 + 1))
                for b in range(NB):
                    at = D_SGU // 2 * (b % 2)
                    act.activation((zv, zu)[c // 2][:, b, half], bank[6 + b // 2][:, at:at + D_SGU // 2], ACT.Gelu,
                                   scale=inv_t[:, b:b + 1]).then_inc(z_gelu, 1)

            def attn_high(pair):
                act.wait_ge(fox.out, 2 * pair + 2)
                act.activation(attn_hi[:, pair, :], attn[:, pair, :], ACT.Copy, scale=col("out_norm", pair)).then_inc(attn_hi_done, 1)

            def norms_high(blocks):
                for b in blocks:
                    act.wait_ge(zvn_ready, b + 1)
                    act.activation(zvn_hi[:, b, :], zv[:, b, :], ACT.Copy).then_inc(zvn_hi_done, 1)

            split_tile("mix_z", 0, 0)
            exps(fox, 0, f_prob, 1.0)
            split_tile("mix_z", 0, 1)
            gelu(0)
            for h in range(FOX_HEADS):
                transposed_high(fox, h, f_prob_t_hi)
                if h + 1 < FOX_HEADS:
                    exps(fox, h + 1, f_prob, 1.0)
                if h in (2, 4, 6):
                    gelu(h // 2)
                if h == 3:
                    act.wait_ge(decay_in, 8 * 16)
                    act.wait_ge(ln_prepared, 1)
                    act.activation(rstd[:], rstd[:], ACT.Sqrt).then_inc(ln_rstd, 1)
                if h < 6:
                    split_tile("mix_z", 0, 2 + h)
                if h == 4:
                    norms_high((0, 1))
                if h == 5:
                    norms_high((2, 3))
                if h % 2 == 0 and h:
                    attn_high(h // 2 - 1)
            attn_high(FOX_PAIRS - 1)
            split_tile("mix_out", 0, 0)
            for pair in range(FOX_PAIRS):
                act.activation(attn_sq[:, pair, :], attn[:, pair, :], ACT.Square).then_inc(attn_squared, 1)
            act.wait_ge(sgu_gated, SGU_G)
            for b in range(NB):
                if b:
                    act.wait_ge(branch_squared, b)
                act.activation(junk[:], zu[:, b, :], ACT.Square, accum_out=branch_sq[:, b:b + 1]).then_inc(branch_squared, 1)
            act.wait_ge(branch_prepared, 1)
            act.activation(branch_inv[:], branch_inv[:], ACT.Sqrt).then_inc(branch_inv_done, 1)
            act.wait_ge(attn_prepared, 1)
            act.activation(attn_inv[:], attn_inv[:], ACT.Sqrt).then_inc(attn_inv_done, 1)
            for c in range(SC):
                act.wait_ge(branch_t, c + 1)
                act.activation(sgu_hi[:, c, :], bank[6 + c % 2][:], ACT.Copy, scale=col("out_norm", AC + c)).then_inc(sgu_hi_done, 1)
            n = norm["ffn"]
            for k in range(DC):
                if k:
                    split_tile("mix_out", 0, k)
                for c in ((), (), (), (), (0, 1, 2, 3), (4,), (5,), (6, 7))[k]:
                    norm_in_chunk(n, c, ffn_xg_hi, ffn_sq, ffn_sqsum, lambda c: col("ffn_norm", c))


            def act_high(turn, n):
                index = turn * 2 + n
                act.wait_ge(act_ready, index + 1)
                act.activation(act_hi[:, index, :], up[:, n % 2, :], ACT.Copy).then_inc(act_hi_done, 1)

            for turn, j in sweep(act, 2 * FC):
                split_tile("ffn_up", turn, j)
                if starts(turn, j, 1):
                    norm_root(norm["ffn"])
                if j % 2 == 0:
                    act.wait_ge(ffn_evac, turn * RING + (j + 1))
                    act.activation(gated[:, j // 2 % 2, :], gated[:, j // 2 % 2, :], ACT.Silu).then_inc(gate_silu, 1)
                elif not starts(turn, j, 2):
                    act_high(turn, j // 2 - 1)
            act_high(0, FC - 1)
            for k in range(FC):
                split_tile("ffn_down", 0, k)
            n = norm["final"]
            for k in range(DC):
                act.wait_ge(n.x_ready, k + 1)
                if k >= 3:
                    act.wait_ge(n.summed, k - 2)
                act.activation(fin_sq[:, k % 2, :] if k else fin_sqsum[:], x[:, k, :], ACT.Square).then_inc(n.squared, 1)
            norm_root(n)
            for k in range(DC):
                act.wait_ge(out_ready, k + 1)
                act.dma_start(out[:, k, :], x[:, k, :]).then_inc(stored, 16)
            act.wait_ge(stored, 16 * DC)
            act.wait_ge(x_spilled, 16)

        @block.vector
        def _(dve):
            own = [0]

            def settle(instruction):
                own[0] += 1
                instruction.then_inc(steps, 1)
                dve.wait_ge(steps, own[0])

            def norm_chunk(n, k, xg_hi, xg_lo, gain, pairs):
                dve.wait_ge(n.xg_hi, k + 1)
                dve.scalar_tensor_tensor(xg_lo[:, k, :], x[:, k, :], gain(k), plain(xg_hi[:, k, :]),
                                         ALU.mult, ALU.subtract).then_inc(n.xg_lo, 1)
                if k:
                    dve.wait_ge(n.squared, len(pairs) * (k + 1))
                    if k >= 2:
                        dve.wait_ge(n.summed, len(pairs) * (k - 1))
                    for total, square in pairs:
                        dve.tensor_tensor(total, total, square(k), ALU.add).then_inc(n.summed, 1)

            def norm_mean(n, b, source_scale=1.0 / D):
                dve.wait_ge(n.mean, n.before + 1)
                settle(dve.tensor_scalar(mean_sq[:], b[:], source_scale, EPS, ALU.mult, ALU.add))
                dve.reciprocal(mean_sq[:], mean_sq[:]).then_inc(n.prepared, 1)

            def take_bank(stage, n, k):
                if k < DC - 1:
                    dve.wait_ge(bank_done[stage], k + 1)
                else:
                    dve.wait_ge(tile_used, TILE[stage] + dict(TILE_SIZES)[stage])
                dve.tensor_tensor(x[:, k, :], bank[k][:], x[:, k, :], ALU.add).then_inc(n.x_ready, 1)

            def residual(stage, name, xg_hi, xg_lo, sq, sqsum, gain):
                n = norm[name]
                for k in range(DC + 1):
                    if k < DC:
                        take_bank(stage, n, k)
                    if k:
                        norm_chunk(n, k - 1, xg_hi, xg_lo, gain, [(sqsum[:], lambda c: sq[:, c % 2, :])])

            def out_low(stage):
                for turn, j in sweep(dve, PC):
                    dve.wait_ge(y_hi_done, turn * RING + (Y_BEFORE[stage] + j + 1))
                    index = turn * RING + j
                    dve.tensor_tensor(y_lo[:, j % RING, :], z[:, index, :], plain(y_hi[:, j % RING, :]),
                                      ALU.subtract).then_inc(y_lo_done, 1)
                    if stage == "pool_out" and isinstance(turn, int) and j == 3:
                        rope_angles()

            def rope_angles():
                dve.wait_ge(pos_in, 16)
                settle(dve.tensor_copy(angle[:], pos_i[:]))
                settle(dve.tensor_scalar(angle[:], angle[:], col("inv_freq"), None, ALU.mult))
                for i, ahead in enumerate((0.0, 0.25)):
                    settle(dve.tensor_scalar(turns_of[:], angle[:], 1.0 / TWO_PI, ahead, ALU.mult, ALU.add))
                    settle(dve.tensor_scalar(turns_of[:], turns_of[:], ROUNDER, None, ALU.add))
                    settle(dve.tensor_scalar(turns_of[:], turns_of[:], ROUNDER, None, ALU.subtract))
                    if i:
                        dve.wait_ge(table_done, 1)
                    settle(dve.scalar_tensor_tensor(reduced[:], turns_of[:], -TWO_PI_PARTS[0], angle[:], ALU.mult, ALU.add))
                    for part in TWO_PI_PARTS[1:]:
                        settle(dve.scalar_tensor_tensor(reduced[:], turns_of[:], -part, reduced[:], ALU.mult, ALU.add))
                    if i:
                        settle(dve.tensor_scalar(reduced[:], reduced[:], TWO_PI / 4, None, ALU.add))
                    dve.tensor_scalar(reduced[:], reduced[:], 3.1415925, -3.1415925, ALU.min, ALU.max).then_inc(angle_ready, 1)

            dve.memset(ones[:], 1.0).then_inc(made, 1)
            dve.wait_ge(patterns, 6)
            dve.tensor_copy(ident_r[:], ident[:]).then_inc(made, 1)
            dve.tensor_copy(mask_r[:], mask[:]).then_inc(made, 1)
            dve.wait_ge(cols_in, 16)
            n = norm["pool"]
            for k in range(DC):
                norm_chunk(n, k, pool_xg_hi, pool_xg_lo, lambda c: col("pool_norm", c),
                           [(pool_sqsum[:], lambda c: pool_sq[:, c % 2, :])])
            norm_mean(n, bank[MEAN_BANK])
            dve.wait_ge(small_in, 32)
            dve.tensor_tensor(gain12[:], cols[:, COLUMNS["final_norm"]:COLUMNS["final_norm"] + DC],
                              cols[:, COLUMNS["mix_norm"]:COLUMNS["mix_norm"] + DC], ALU.mult).then_inc(made, 1)
            for i in range(2):
                settle(dve.memset(u_pad[:, i, 0:PAD], 0.0))
            dve.wait_ge(n.inv, n.before + 1)

            def pooled_low(c):
                dve.wait_ge(pooled_hi_done, c + 1)
                dve.tensor_tensor(pooled_lo[:, c, :], pooled[:, c % 2, :], plain(pooled_hi[:, c, :]),
                                  ALU.subtract).then_inc(pooled_lo_done, 1)

            for c in range(PC):
                window = WINDOWS[c // PG]
                u = u_pad[:, c % 2, :]
                dve.wait_ge(tile_used, TILE["pool_u"] + c + 1)
                dve.tensor_tensor(u[:, PAD:], bank[c % 4][:], inv[:], ALU.mult).then_inc(in_evac, 1)
                dve.wait_ge(in_evac, c + 1)
                total, reach, spare = u, 1, (sum_a, sum_b)
                while reach < window:
                    target = spare[0]
                    settle(dve.tensor_tensor(target[:, 2 * reach:], total[:, 2 * reach:], total[:, reach:PAD + S - reach], ALU.add))
                    total, reach, spare = target, 2 * reach, spare[::-1]
                if c >= 2:
                    pooled_low(c - 2)
                    dve.wait_ge(pooled_lo_done, c - 1)
                dst = pooled[:, c % 2, :]
                edge = window - 1
                other = spare[0]
                dve.scalar_tensor_tensor(dst[:, edge:], total[:, PAD + edge:], 1.0 / window, u[:, PAD + edge:],
                                         ALU.mult, ALU.subtract)
                settle(dve.tensor_tensor(other[:, 0:edge], total[:, PAD:PAD + edge], counts[:, 0:edge], ALU.mult))
                dve.tensor_tensor(dst[:, 0:edge], other[:, 0:edge], u[:, PAD:PAD + edge], ALU.subtract).then_inc(pooled_ready, 1)
            for c in range(PC):
                dve.wait_ge(tile_used, TILE["pool_z"] + c + 1)
                dve.tensor_tensor(z[:, c, :], bank[c % 4][:], inv[:], ALU.mult).then_inc(in_evac, 1)
                if c < 2:
                    pooled_low(PC - 2 + c)
            for c in range(PC):
                if c % 2:
                    dve.wait_ge(tile_used, TILE["pool_group"] + c // 2 + 1)
                else:
                    dve.wait_ge(half_tile, c // 2 + 1)
                dve.wait_ge(z_silu, c + 1)
                dve.scalar_tensor_tensor(z[:, c, :], bank[c % 4][:], col("pool_scale", c), z[:, c, :],
                                         ALU.mult, ALU.mult).then_inc(y_ready, 1)
            out_low("pool_out")
            residual("pool_out", "mla", mla_xg_hi, mla_xg_lo, mla_sq, mla_sqsum, lambda k: col("mla_norm", k))
            norm_mean(norm["mla"], bank[MEAN_BANK])
            dve.wait_ge(norm["mla"].inv, norm["mla"].before + 1)

            for u in range(LC + 2 + PC):
                dve.wait_ge(tile_used, TILE["mla_in"] + u + 1)
                source = bank[u % 4][:]
                if u < LC:
                    dve.tensor_tensor(lat[:, u, :], source, inv[:], ALU.mult).then_inc(mla_evac, 1)
                elif u == LC:
                    dve.wait_ge(table_done, 2)
                    dve.tensor_tensor(rope_a[:], source, cos[:], ALU.mult).then_inc(mla_evac, 1)
                elif u == LC + 1:
                    dve.scalar_tensor_tensor(rope_b[:], source, col("rope_sign"), sin[:], ALU.mult, ALU.mult).then_inc(mla_evac, 1)
                    dve.wait_ge(mla_evac, LC + 2)
                    settle(dve.tensor_tensor(rope_a[:], rope_a[:], rope_b[:], ALU.add))
                    dve.tensor_tensor(rope_a[:], rope_a[:], inv[:], ALU.mult).then_inc(rope_k_ready, 1)
                    for i, (first, last) in enumerate(((0, QC), (QC, LC))):
                        dve.wait_ge(lat_squared, last)
                        for c in range(first + 1, last):
                            t = dve.tensor_tensor(lat_sqsum[:, i, :], lat_sq[:, c, :],
                                                  lat_sq[:, first, :] if c == first + 1 else lat_sqsum[:, i, :], ALU.add)
                            if c < last - 1:
                                settle(t)
                            else:
                                t.then_inc(lat_summed, 1)
                else:
                    dve.tensor_tensor(z[:, u - LC - 2, :], source, inv[:], ALU.mult).then_inc(mla_evac, 1)
                if u == LC + 2:
                    for i, width in enumerate((QC * P, KC * P)):
                        dve.wait_ge(lat_mean, i + 1)
                        settle(dve.tensor_scalar(lat_sqsum[:, i, :], bank[6 + i][:], 1.0 / width, EPS, ALU.mult, ALU.add))
                        dve.reciprocal(lat_sqsum[:, i, :], lat_sqsum[:, i, :]).then_inc(lat_prepared, 1)
                if u == LC + 3:
                    dve.wait_ge(lat_inv, 2)
                    for c in range(LC):
                        dve.scalar_tensor_tensor(lat[:, c, :], lat[:, c, :], col("q_norm", c), lat_sqsum[:, int(c >= QC), :],
                                                 ALU.mult, ALU.mult).then_inc(lat_ready, 1)
                    dve.wait_ge(rope_k_hi_done, 1)
                    dve.tensor_tensor(rope_k_lo[:], rope_a[:], plain(rope_k_hi[:]), ALU.subtract).then_inc(rope_k_lo_done, 1)
                if u == LC + 5:
                    for c in range(LC):
                        dve.wait_ge(lat_hi_done, c + 1)
                        dve.tensor_tensor(lat_lo[:, c, :], lat[:, c, :], plain(lat_hi[:, c, :]), ALU.subtract).then_inc(lat_lo_done, 1)

            def unit_low(u):
                kind, g, j = u
                hi, lo = {"k": (k_hi, k_lo), "q": (q_hi, q_lo), "v": (v_hi, v_lo)}[kind]
                dve.wait_ge(unit_hi, hi_units(u))
                dve.tensor_tensor(lo[:, j, :], bank[6 + UNIT[u] % 2][:], plain(hi[:, j, :]), ALU.subtract).then_inc(unit_evac, 1)

            def turn_half(g, j):
                u = ("rope", g, j)
                source = bank[6 + UNIT[u] % 2][:]
                wait_unit(dve, u)
                if j == 0:
                    if g:
                        dve.wait_ge(turned_lo_done, 2 * g)
                        dve.wait_ge(turned_hi_done, 2 * g)
                    settle(dve.tensor_tensor(turned_1[:], source, cos[:], ALU.mult))
                    dve.tensor_tensor(turned_2[:], source, sin[:], ALU.mult).then_inc(unit_evac, 1)
                else:
                    settle(dve.tensor_tensor(rope_t[:], source, sin[:], ALU.mult))
                    dve.tensor_tensor(turned_1[:], turned_1[:], rope_t[:], ALU.subtract).then_inc(turned, 1)
                    dve.wait_ge(turned, 2 * g + 1)
                    dve.tensor_tensor(rope_t[:], source, cos[:], ALU.mult).then_inc(unit_evac, 1)
                    dve.wait_ge(unit_evac, UNIT[u] + 1)
                    dve.tensor_tensor(turned_2[:], turned_2[:], rope_t[:], ALU.add).then_inc(turned, 1)

            def turned_low(g):
                for i, t in enumerate((turned_1, turned_2)):
                    dve.wait_ge(turned_hi_done, 2 * g + i + 1)
                    dve.tensor_tensor(turned_lo[:, i, :], t[:], plain(turned_hi[:, i, :]), ALU.subtract).then_inc(turned_lo_done, 1)

            def peaks(s, h, scale, banks):
                for i in banks:
                    blocks = ((0, 1), (2,), (3,))[i]
                    dve.wait_ge(s.scores, 3 * h + i + 1)
                    for b in blocks:
                        t = dve.reduce_max(peak[:, h % 2, b:b + 1], bank[i][:, SCORE_AT[b]:SCORE_AT[b] + P * (b + 1)], X)
                    settle(t)
                    if h >= 2:
                        dve.wait_ge(s.exped, NB * (h - 1))
                    dve.tensor_scalar(neg_peak[:, h % 2, blocks[0]:blocks[-1] + 1], peak[:, h % 2, blocks[0]:blocks[-1] + 1],
                                      -scale, None, ALU.mult).then_inc(s.peaks, 1)

            def normalise(s, h, prob):
                dve.wait_ge(s.exped, NB * (h + 1))
                settle(dve.reciprocal(inv_sum[:, h % 2, :], row_sum[:, h % 2, :]))
                for b in range(NB):
                    dve.tensor_scalar(prob[:, ROW[b]:ROW[b + 1]], prob[:, ROW[b]:ROW[b + 1]], inv_sum[:, h % 2, b:b + 1],
                                      None, ALU.mult).then_inc(probs, 1)

            def transposed_low(s, h, hi, lo, blocks):
                for b in blocks:
                    dve.wait_ge(s.prob_t_hi, NB * h + b + 1)
                    dve.tensor_tensor(lo[:, COLUMN[b]:COLUMN[b + 1]], bank[3 + b % 2][:, 0:S - P * b],
                                      plain(hi[:, COLUMN[b]:COLUMN[b + 1]]), ALU.subtract).then_inc(s.prob_t_lo, 1)

            def prepare(g, j):
                for i in (j,) if j < GH - 1 else (j, GH):
                    for kind, k in GROUP_TILES[i]:
                        if kind == "rope":
                            turn_half(g, k)
                        else:
                            unit_low((kind, g, k))

            for j in range(GH):
                if j == 1:
                    turned_low(0)
                prepare(0, j)
            peaks(mla, 0, MLA_SCALE, (0, 1, 2))
            normalise(mla, 0, prob)
            for h in range(HEADS):
                g, j = h // GH + 1, h % GH
                transposed_low(mla, h, prob_t_hi, prob_t_lo, (0, 1))
                if h + 1 < HEADS:
                    peaks(mla, h + 1, MLA_SCALE, (0,))
                transposed_low(mla, h, prob_t_hi, prob_t_lo, (2, 3))
                if h + 1 < HEADS:
                    peaks(mla, h + 1, MLA_SCALE, (1, 2))
                    normalise(mla, h + 1, prob)
                dve.wait_ge(mla.weighted, h + 1)
                dve.wait_ge(mz_silu, h + 1)
                dve.tensor_tensor(z[:, h, :], bank[5][:], z[:, h, :], ALU.mult).then_inc(mla.out, 1)
                if g < GROUPS:
                    if j == 1:
                        turned_low(g)
                    prepare(g, j)
            out_low("mla_out")

            n = norm["mix"]
            dve.wait_ge(x_back, 16)
            pairs = [(mix_sqsum[:, i, :], lambda c, i=i: mix_sq[:, c % 2, i, :]) for i in range(2)]
            for k in range(DC + 1):
                if k < DC:
                    take_bank("mla_out", n, k)
                if k:
                    norm_chunk(n, k - 1, mix_xg_hi, mix_xg_lo, lambda c: gain12[:, c:c + 1], pairs)
            dve.wait_ge(n.mean, n.before + 1)
            settle(dve.tensor_scalar(mean_sq[:], bank[6][:], 1.0 / D, EPS, ALU.mult, ALU.add))
            dve.reciprocal(mean_sq[:], mean_sq[:]).then_inc(n.prepared, 1)
            dve.wait_ge(n.inv, n.before + 1)
            dve.wait_ge(n.mean, n.before + 2)
            settle(dve.tensor_tensor(mean_sq[:], bank[7][:], inv_1[:], ALU.mult))
            settle(dve.tensor_tensor(mean_sq[:], mean_sq[:], inv_1[:], ALU.mult))
            settle(dve.tensor_scalar(mean_sq[:], mean_sq[:], 1.0 / D, EPS, ALU.mult, ALU.add))
            dve.reciprocal(mean_sq[:], mean_sq[:]).then_inc(n.prepared, 1)
            dve.wait_ge(n.inv, n.before + 2)
            dve.tensor_tensor(inv[:], inv[:], inv_1[:], ALU.mult).then_inc(inv_both, 1)
            dve.wait_ge(inv_both, 1)

            def qk_low(u):
                hi, lo = (fq_hi, fq_lo) if u < 4 else (fk_hi, fk_lo)
                dve.wait_ge(qk_hi, u + 1)
                dve.tensor_tensor(lo[:, u % 4, :], qk_t[:, u % 2, :], plain(hi[:, u % 4, :]), ALU.subtract).then_inc(qk_lo, 1)

            for u in range(9):
                dve.wait_ge(tile_used, TILE["mix_qk"] + u + 1)
                m = u if u < 4 else u - 1
                if u == 4:
                    dve.tensor_tensor(f_t[:], bank[0][:], inv[:], ALU.mult).then_inc(f_ready, 1)
                else:
                    if m >= 2:
                        qk_low(m - 2)
                        dve.wait_ge(qk_lo, m - 1)
                    dve.scalar_tensor_tensor(qk_t[:, m % 2, :], bank[u % 4][:], FOX_D ** -0.5 if m < 4 else 1.0, inv[:],
                                             ALU.mult, ALU.mult).then_inc(qk_ready, 1)
                if u < DC:
                    scaled = dve.scalar_tensor_tensor(x[:, u, :], x[:, u, :], col("final_norm", u), inv_1[:], ALU.mult, ALU.mult)
                    if u == DC - 1:
                        scaled.then_inc(x_scaled, 1)
                if u == 1:
                    dve.wait_ge(ws_in, 16)
                    w = ws_raw[:].rearrange("p (g i) -> p g i", g=SGU_G)
                    dve.memset(w[SGU_HALF:P, :, 0:SGU_HALF], 0.0).then_inc(ws_cut, 1)
                if u == 2:
                    dve.memset(plain(decay_q[:]), 1.0)
                    dve.memset(plain(decay_k[:]), 1.0).then_inc(decay_ones, 1)
                if u == 3:
                    dve.wait_ge(inv_t_sum, 1)
                    dve.tensor_copy(inv_t[:], bank[5][:, 0:NB]).then_inc(inv_t_ready, 1)
                if u == 5:
                    dve.wait_ge(f_summed, 1)
                    for b in range(NB):
                        t = dve.tensor_tensor(gate[:, b, :], bank[5][:, 8 * b:8 * b + 8], b_f[:], ALU.add)
                    settle(t)
                    dve.scalar_tensor_tensor(gate_abs[:], gate[:], -1.0, gate[:], ALU.mult, ALU.max).then_inc(gate_abs_ready, 1)
                    settle(dve.tensor_scalar(gate[:], gate[:], 0.0, None, ALU.min))
                if u == 7:
                    dve.wait_ge(gate_log, 1)
                    dve.tensor_tensor(log_f[:], gate[:], gate_abs[:], ALU.subtract).then_inc(log_f_ready, 1)
            qk_low(6)
            qk_low(7)
            dve.wait_ge(c_hi_done, 1)
            settle(dve.tensor_tensor(c_parts[:, 1, :], bank[6][0:FOX_HEADS, :], plain(c_parts[:, 0, :]), ALU.subtract))
            dve.tensor_scalar(c_parts[:, 2:4, :], plain(c_parts[:, 0:2, :]), -1.0, None, ALU.mult).then_inc(c_ready, 1)
            dve.wait_ge(ws_hi_done, 1)
            dve.tensor_tensor(ws_lo[:], ws_raw[:], plain(ws_hi[:]), ALU.subtract).then_inc(ws_lo_done, 1)
            dve.wait_ge(inv_t_ready, 1)
            for b in range(NB):
                dve.wait_ge(fv_hi_done, b + 1)
                dve.scalar_tensor_tensor(fv_lo[:, b, :], bank[b][:], inv_t[:, b:b + 1], plain(fv_hi[:, b, :]),
                                         ALU.mult, ALU.subtract).then_inc(fv_lo_done, 1)

            def attn_low(pair):
                dve.wait_ge(attn_hi_done, pair + 1)
                dve.scalar_tensor_tensor(attn_lo[:, pair, :], attn[:, pair, :], col("out_norm", pair), plain(attn_hi[:, pair, :]),
                                         ALU.mult, ALU.subtract).then_inc(attn_lo_done, 1)

            def layer_norm(blocks):
                for b in blocks:
                    settle(dve.tensor_scalar(zv[:, b, :], zv[:, b, :], moments[:, b, 0:1], rstd[:, b:b + 1], ALU.subtract, ALU.mult))
                    settle(dve.tensor_tensor(zv[:, b, :], zv[:, b, :], ln_g[:], ALU.mult))
                    dve.tensor_tensor(zv[:, b, :], zv[:, b, :], ln_b[:], ALU.add).then_inc(zvn_ready, 1)

            def layer_norm_low(blocks):
                for b in blocks:
                    dve.wait_ge(zvn_hi_done, b + 1)
                    dve.tensor_tensor(zvn_lo[:, b, :], zv[:, b, :], plain(zvn_hi[:, b, :]), ALU.subtract).then_inc(zvn_lo_done, 1)

            def gate_groups(groups):
                for g in groups:
                    dve.wait_ge(sgu_mixed, g // 2 * 2 + 2)
                    mine = zu[:, :, SGU_D * g:SGU_D * (g + 1)]
                    at = NB * SGU_D * (g % 2)
                    dve.scalar_tensor_tensor(mine, bank[6 + g // 2 % 2][:, at:at + NB * SGU_D].rearrange("p (b d) -> p b d", b=NB),
                                             col("b_s", g), mine, ALU.add, ALU.mult).then_inc(sgu_gated, 1)

            peaks(fox, 0, 1.0, (0, 1, 2))
            normalise(fox, 0, f_prob)
            for h in range(FOX_HEADS):
                transposed_low(fox, h, f_prob_t_hi, f_prob_t_lo, (0, 1))
                if h + 1 < FOX_HEADS:
                    peaks(fox, h + 1, 1.0, (0,))
                transposed_low(fox, h, f_prob_t_hi, f_prob_t_lo, (2, 3))
                if h + 1 < FOX_HEADS:
                    peaks(fox, h + 1, 1.0, (1, 2))
                    normalise(fox, h + 1, f_prob)
                dve.wait_ge(fox.weighted, h + 1)
                rows = slice(FOX_D * (h % 2), FOX_D * (h % 2 + 1))
                dve.tensor_copy(attn[rows, h // 2, :], bank[5][rows, :]).then_inc(fox.out, 1)
                if h == 3:
                    dve.wait_ge(z_gelu, 2 * NB)
                    for b in range(NB):
                        t = dve.bn_stats(stats[:, b, :], zv[:, b, :])
                    settle(t)
                    for b in range(NB):
                        t = dve.bn_aggr(moments[:, b, :], stats[:, b:b + 1, :])
                    settle(t)
                    settle(dve.tensor_scalar(rstd[:], moments[:, :, 1], EPS, None, ALU.add))
                    dve.reciprocal(rstd[:], rstd[:]).then_inc(ln_prepared, 1)
                if h == 4:
                    dve.wait_ge(ln_rstd, 1)
                    dve.wait_ge(ln_in, 32)
                    layer_norm((0, 1))
                if h == 5:
                    layer_norm_low((0, 1))
                    layer_norm((2, 3))
                if h == 6:
                    layer_norm_low((2, 3))
                    gate_groups(range(4))
                if h % 2 == 0 and h:
                    attn_low(h // 2 - 1)
            gate_groups(range(4, SGU_G))
            attn_low(FOX_PAIRS - 1)
            for pair in range(1, FOX_PAIRS):
                dve.wait_ge(attn_squared, pair + 1)
                t = dve.tensor_tensor(attn_sqsum[:], attn_sq[:, 0, :] if pair == 1 else attn_sqsum[:], attn_sq[:, pair, :], ALU.add)
                if pair < FOX_PAIRS - 1:
                    settle(t)
            t.then_inc(attn_summed, 1)
            dve.wait_ge(branch_squared, NB)
            settle(dve.tensor_scalar(branch_inv[:], branch_sq[:], 1.0 / D_SGU, EPS, ALU.mult, ALU.add))
            dve.reciprocal(branch_inv[:], branch_inv[:]).then_inc(branch_prepared, 1)
            dve.wait_ge(branch_inv_done, 1)
            for b in range(NB):
                dve.tensor_scalar(zu[:, b, :], zu[:, b, :], branch_inv[:, b:b + 1], None, ALU.mult).then_inc(branch_scaled, 1)
            dve.wait_ge(attn_mean, 1)
            settle(dve.tensor_scalar(attn_inv[:], bank[5][:], 1.0 / D_ATTN, EPS, ALU.mult, ALU.add))
            dve.reciprocal(attn_inv[:], attn_inv[:]).then_inc(attn_prepared, 1)
            for c in range(SC):
                dve.wait_ge(sgu_hi_done, c + 1)
                dve.scalar_tensor_tensor(sgu_lo[:, c, :], bank[6 + c % 2][:], col("out_norm", AC + c), plain(sgu_hi[:, c, :]),
                                         ALU.mult, ALU.subtract).then_inc(sgu_lo_done, 1)
            dve.wait_ge(attn_inv_done, 1)
            n = norm["ffn"]
            for k in range(DC + 1):
                if k < DC:
                    dve.wait_ge(tile_used, TILE["mix_out"] + k + 1)
                    t = mixed[:, k % 2, :]
                    settle(dve.tensor_tensor(t, bank[k % 4][:], attn_inv[:], ALU.mult))
                    settle(dve.tensor_tensor(t, t, bank[4 + k % 4][:], ALU.add))
                    dve.tensor_tensor(x[:, k, :], t, x[:, k, :], ALU.add).then_inc(n.x_ready, 1)
                if k:
                    norm_chunk(n, k - 1, ffn_xg_hi, ffn_xg_lo, lambda c: col("ffn_norm", c),
                               [(ffn_sqsum[:], lambda c: ffn_sq[:, c % 2, :])])

            norm_mean(norm["ffn"], bank[MEAN_BANK])
            dve.wait_ge(norm["ffn"].inv, norm["ffn"].before + 1)

            def act_low(turn, n):
                index = turn * 2 + n
                dve.wait_ge(act_hi_done, index + 1)
                dve.tensor_tensor(act_lo[:, index, :], up[:, n % 2, :], plain(act_hi[:, index, :]), ALU.subtract).then_inc(act_lo_done, 1)

            for turn, j in sweep(dve, 2 * FC):
                dve.wait_ge(tile_used, turn * RING + (TILE["ffn_up"] + j + 1))
                n = j // 2
                if j % 2 == 0:
                    dve.tensor_tensor(gated[:, n % 2, :], bank[j % 4][:], inv[:], ALU.mult).then_inc(ffn_evac, 1)
                    if not starts(turn, j, 4):
                        act_low(turn, n - 2)
                else:
                    if not starts(turn, j, 4):
                        dve.wait_ge(act_lo_done, turn * 2 + (n - 1))
                    dve.tensor_tensor(up[:, n % 2, :], bank[j % 4][:], inv[:], ALU.mult).then_inc(ffn_evac, 1)
                    dve.wait_ge(ffn_evac, turn * RING + (j + 1))
                    dve.wait_ge(gate_silu, turn * 2 + (n + 1))
                    dve.tensor_tensor(up[:, n % 2, :], up[:, n % 2, :], gated[:, n % 2, :], ALU.mult).then_inc(act_ready, 1)
            act_low(0, FC - 2)
            act_low(0, FC - 1)
            n = norm["final"]
            for k in range(DC):
                take_bank("ffn_down", n, k)
                if k:
                    dve.wait_ge(n.squared, k + 1)
                    if k >= 2:
                        dve.wait_ge(n.summed, k - 1)
                    dve.tensor_tensor(fin_sqsum[:], fin_sqsum[:], fin_sq[:, k % 2, :], ALU.add).then_inc(n.summed, 1)
            norm_mean(n, bank[0])
            dve.wait_ge(n.inv, n.before + 1)
            for k in range(DC):
                dve.scalar_tensor_tensor(x[:, k, :], x[:, k, :], col("final_norm_2", k), inv[:], ALU.mult, ALU.mult).then_inc(out_ready, 1)

        @block.tensor
        def _(pe):
            def three(target, a_hi, a_lo, b_hi, b_lo, start, stop):
                pe.matmul(target, a_hi, b_hi, start=start, stop=False)
                pe.matmul(target, a_hi, b_lo, start=False, stop=False)
                return pe.matmul(target, a_lo, b_hi, start=False, stop=stop)

            def wblock(t, i, width=P):
                return w_hi[:, t % RING, width * i:width * (i + 1)], w_lo[:, t % RING, width * i:width * (i + 1)]

            def wait_tile(turn, t):
                pe.wait_ge(tile_lo, turn * RING + (t + 1))

            def projection(stage, turn, j, b, xg_hi, xg_lo, xg_lo_done=None):
                t = TILE[stage] + j
                wait_tile(turn, t)
                for k in range(DC):
                    if xg_lo_done is not None:
                        pe.wait_ge(xg_lo_done, k + 1)
                    last = three(b[:], *wblock(t, k), xg_hi[:, k, :], xg_lo[:, k, :], k == 0, k == DC - 1)
                last.then_inc(tile_used, 1)

            def mean(sem_in, value, total, b, sem_out):
                pe.wait_ge(sem_in, value)
                pe.matmul(b[:], ones[:], total, start=True, stop=True).then_inc(sem_out, 1)

            def out_product(stage, chunks, chunk_lo, lo_sem, lo_value, tail=1, free=()):
                for turn, j in sweep(pe, chunks, tail=tail):
                    t = TILE[stage] + j
                    wait_tile(turn, t)
                    pe.wait_ge(lo_sem, lo_value(turn, j))
                    hi, lo = chunk_lo(turn, j)
                    first, final = starts(turn, j, 1), isinstance(turn, int) and j == chunks - 1
                    for n in range(DC):
                        if first:
                            for s_, v_ in free[n]:
                                pe.wait_ge(s_, v_)
                        last = three(bank[n][:], *wblock(t, n), hi, lo, first, final)
                        if final and n < DC - 1:
                            last.then_inc(bank_done[stage], 1)
                    last.then_inc(tile_used, 1)

            n = norm["pool"]
            for turn, j in sweep(pe, PC):
                if not starts(turn, j, 4):
                    pe.wait_ge(in_evac, turn * RING + (j - 3))
                projection("pool_u", turn, j, bank[j % 4], pool_xg_hi, pool_xg_lo, n.xg_lo if starts(turn, j, 1) else None)
                if starts(turn, j, 1):
                    pe.wait_ge(made, 1)
                    mean(n.summed, DC - 1, pool_sqsum[:], bank[MEAN_BANK], n.mean)
            for turn, j in sweep(pe, PC):
                pe.wait_ge(in_evac, turn * RING + (PC + j - 3))
                projection("pool_z", turn, j, bank[j % 4], pool_xg_hi, pool_xg_lo)
            for i in range(PC * PG // 8):
                t = TILE["pool_group"] + i
                wait_tile(0, t)
                group = i // 2
                pe.wait_ge(pooled_lo_done, PG * (group + 1))
                for half in range(2):
                    c = 2 * i + half
                    if c < 4:
                        pe.wait_ge(in_evac, 2 * PC - 4 + c + 1)
                    else:
                        pe.wait_ge(y_ready, c - 3)
                    for k in range(PG):
                        last = three(bank[c % 4][:], *wblock(t, PG * half + k), pooled_hi[:, PG * group + k, :],
                                     pooled_lo[:, PG * group + k, :], k == 0, k == PG - 1)
                    last.then_inc(tile_used if half else half_tile, 1)
            out_product("pool_out", PC, lambda turn, j: (y_hi[:, j % RING, :], y_lo[:, j % RING, :]),
                        y_lo_done, lambda turn, j: turn * RING + (j + 1),
                        free=[[(y_ready, PC - 4 + b + 1)] if b < 4 else [] for b in range(8)])

            n = norm["mla"]
            for u in range(LC + 2 + PC):
                if u >= 4:
                    pe.wait_ge(mla_evac, u - 3)
                projection("mla_in", 0, u, bank[u % 4], mla_xg_hi, mla_xg_lo, n.xg_lo if u == 0 else None)
                if u == 0:
                    mean(n.summed, DC - 1, mla_sqsum[:], bank[MEAN_BANK], n.mean)
                if u == LC + 2:
                    for i in range(2):
                        mean(lat_summed, i + 1, lat_sqsum[:, i, :], bank[6 + i], lat_mean)

            def unit(u):
                kind, g, j = u
                i = UNIT[u]
                if i >= 2:
                    pe.wait_ge(unit_evac, i - 1)
                t = unit_tile(u)
                wait_tile(0, t)
                b = bank[6 + i % 2]
                if kind == "v":
                    for c in range(KC):
                        hi, lo = wblock(t, c, S)
                        a = slice(P * j, P * (j + 1))
                        last = three(b[:], lat_hi[:, QC + c, a], lat_lo[:, QC + c, a], hi, lo, c == 0, c == KC - 1)
                else:
                    first, chunks, base = QC if kind == "k" else 0, CHUNKS_OF[kind], unit_place(kind, j)[1]
                    for c in range(chunks):
                        last = three(b[:], *wblock(t, base + c), lat_hi[:, first + c, :], lat_lo[:, first + c, :],
                                     c == 0, c == chunks - 1)
                last.then_inc(tile_used if ends_tile(u) else unit_done, 1)

            def causal_mask(target, b):
                return pe.matmul(target[:, P * b:P * (b + 1)], ident_r[:], mask_r[:], start=False, stop=True)

            def scores_mla(h, blocks):
                g, j = divmod(h, GH)
                pe.wait_ge(unit_evac, UNIT[("q", g, j)] + 1)
                if j == 0:
                    pe.wait_ge(rope_q_in, 256 * (g + 1))
                for b in blocks:
                    i, at, n = SCORE_BANK[b], SCORE_AT[b], P * (b + 1)
                    if h and b != 1:
                        pe.wait_ge(mla.exped, NB * (h - 1) + (2, 3, 4)[i])
                    target = bank[i][:, at:at + n]
                    a = slice(P * b, P * (b + 1))
                    three(target, q_hi[:, j, a], q_lo[:, j, a], k_hi[:, j, 0:n], k_lo[:, j, 0:n], True, False)
                    pe.matmul(target, rope_q[:, g % 2, j, a], rope_k_hi[:, 0:n], start=False, stop=False)
                    pe.matmul(target, rope_q[:, g % 2, j, a], rope_k_lo[:, 0:n], start=False, stop=False)
                    last = causal_mask(target, b)
                    if b:
                        last.then_inc(mla.scores, 1)

            def transposes(s, h, source, ready, value, blocks):
                pe.wait_ge(ready, value)
                for b in blocks:
                    if NB * h + b >= 2:
                        pe.wait_ge(s.prob_t_lo, NB * h + b - 1)
                    for q in range(b, NB):
                        last = pe.transpose(bank[3 + b % 2][:, P * (q - b):P * (q - b + 1)],
                                            source[:, ROW[q] + P * b:ROW[q] + P * (b + 1)], ident[:])
                    last.then_inc(s.transposed, 1)

            def weigh_mla(h):
                if h:
                    pe.wait_ge(mla.out, h)
                j = h % GH
                pe.wait_ge(unit_evac, UNIT[("v", h // GH, NB - 1)] + 1)
                for b in range(NB):
                    pe.wait_ge(mla.prob_t_lo, NB * h + b + 1)
                    a = slice(VD * j, VD * (j + 1))
                    r = slice(COLUMN[b], COLUMN[b + 1])
                    last = three(bank[5][:, P * b:S], v_hi[:, b, a], v_lo[:, b, a], prob_t_hi[:, r], prob_t_lo[:, r],
                                 b == 0, b == NB - 1)
                last.then_inc(mla.weighted, 1)

            def prepare(g, j):
                for i in (j,) if j < GH - 1 else (j, GH):
                    for kind, k in GROUP_TILES[i]:
                        unit((kind, g, k))

            pe.wait_ge(made, 3)
            pe.wait_ge(lat_lo_done, LC)
            pe.wait_ge(mla_evac, LC + 2 + PC)
            pe.wait_ge(rope_k_lo_done, 1)
            for j in range(GH):
                prepare(0, j)
            scores_mla(0, range(NB))
            for h in range(HEADS):
                g, j = h // GH + 1, h % GH
                for blocks in ((0, 1), (2, 3)):
                    transposes(mla, h, prob, probs, NB * (h + 1), blocks)
                    if h + 1 < HEADS:
                        scores_mla(h + 1, blocks)
                weigh_mla(h)
                if g < GROUPS:
                    prepare(g, j)
            out_product("mla_out", PC, lambda turn, j: (y_hi[:, j % RING, :], y_lo[:, j % RING, :]),
                        y_lo_done, lambda turn, j: turn * RING + (PC + j + 1),
                        free=[[(mla.out, HEADS)]] + [[]] * 7)

            n = norm["mix"]
            for u in range(9):
                if u == 8:
                    pe.wait_ge(f_ready, 1)
                elif u >= 4:
                    pe.wait_ge(qk_ready, u - 3)
                projection("mix_qk", 0, u, bank[u % 4], mix_xg_hi, mix_xg_lo, n.xg_lo if u == 0 else None)
                if u == 0:
                    for i in range(2):
                        mean(n.summed, 2 * (DC - 1), mix_sqsum[:, i, :], bank[6 + i], n.mean)
                if u == 3:
                    pe.wait_ge(inv_both, 1)
                    for b in range(NB):
                        last = pe.matmul(bank[5][:, b:b + 1], inv[0:1, P * b:P * (b + 1)], ones[0:1, 0:1], start=True, stop=True)
                    last.then_inc(inv_t_sum, 1)
                if u == 5:
                    pe.wait_ge(f_ready, 1)
                    pe.wait_ge(inv_t_ready, 1)
                    for b in range(NB):
                        last = pe.transpose(bank[5][:, 8 * b:8 * b + 8], f_t[0:FOX_HEADS, P * b:P * (b + 1)],
                                            ident[0:FOX_HEADS, 0:FOX_HEADS])
                    last.then_inc(f_summed, 1)
                if u == 8:
                    pe.wait_ge(log_f_ready, 1)
                    for t in range(NB):
                        for b in range(t + 1):
                            last = pe.matmul(bank[6][0:FOX_HEADS, P * t:P * (t + 1)], log_f[:, b, :],
                                             (upper if b == t else ones)[:], start=b == 0, stop=b == t)
                    last.then_inc(c_summed, 1)
            for i in range(4):
                t = TILE["mix_v"] + i
                wait_tile(0, t)
                for b in range(NB):
                    if i == 0:
                        pe.wait_ge(qk_ready, (8, 5, 6, 7)[b])
                    for c in range(2):
                        k = 2 * i + c
                        a = slice(P * b, P * (b + 1))
                        last = three(bank[b][:], mix_xg_hi[:, k, a], mix_xg_lo[:, k, a], *wblock(t, c, S), k == 0, k == DC - 1)
                    if i == 3 and b < NB - 1:
                        last.then_inc(v_summed, 1)
                last.then_inc(tile_used, 1)

            def sgu_tile(i):
                t = TILE["mix_z"] + i
                wait_tile(0, t)
                if i % 2 == 0 and i:
                    pe.wait_ge(z_gelu, NB * (i // 2))
                for b in range(NB):
                    a = slice(P * b, P * (b + 1))
                    at = D_SGU // 2 * (b % 2)
                    for c in range(4):
                        k = 4 * (i % 2) + c
                        last = three(bank[6 + b // 2][:, at:at + D_SGU // 2], mix_xg_hi[:, k, a], mix_xg_lo[:, k, a],
                                     *wblock(t, c, D_SGU // 2), k == 0 and b % 2 == 0, k == DC - 1 and b % 2 == 1)
                last.then_inc(tile_used, 1)

            def sgu_mix(groups):
                for g in groups:
                    if g >= 4:
                        pe.wait_ge(sgu_gated, g // 2 * 2 - 2)
                    c = slice(SGU_D * g, SGU_D * (g + 1))
                    w = slice(P * g, P * (g + 1))
                    at = NB * SGU_D * (g % 2)
                    three(bank[6 + g // 2 % 2][:, at:at + NB * SGU_D].rearrange("p (b d) -> p b d", b=NB), ws_hi[:, w],
                          ws_lo[:, w], zvn_hi[:, :, c], zvn_lo[:, :, c], True, True).then_inc(sgu_mixed, 1)

            def scores_fox(h, banks):
                pair, half = divmod(h, 2)
                rows = slice(FOX_D * half, FOX_D * (half + 1))
                r = 32 * (h % 4)
                for i in banks:
                    blocks = ((0, 1), (2,), (3,))[i]
                    if h:
                        pe.wait_ge(fox.exped, NB * (h - 1) + (2, 3, 4)[i])
                    for b in blocks:
                        n = P * (b + 1)
                        target = bank[i][:, SCORE_AT[b]:SCORE_AT[b] + n]
                        a = slice(P * b, P * (b + 1))
                        three(target, fq_hi[rows, pair, a], fq_lo[rows, pair, a], fk_hi[rows, pair, 0:n],
                              fk_lo[rows, pair, 0:n], True, False)
                        pe.matmul(target, decay_q[r:r + 4, h // 4, a], decay_k[r:r + 4, h // 4, 0:n], start=False, stop=False)
                        last = causal_mask(target, b)
                    last.then_inc(fox.scores, 1)

            def weigh_fox(h):
                if h:
                    pe.wait_ge(fox.out, h)
                a = slice(P * (h // 2), P * (h // 2 + 1))
                for b in range(NB):
                    pe.wait_ge(fox.prob_t_lo, NB * h + b + 1)
                    r = slice(COLUMN[b], COLUMN[b + 1])
                    last = three(bank[5][:, P * b:S], fv_hi[:, b, a], fv_lo[:, b, a], f_prob_t_hi[:, r], f_prob_t_lo[:, r],
                                 b == 0, b == NB - 1)
                last.then_inc(fox.weighted, 1)

            pe.wait_ge(c_ready, 1)
            sgu_tile(0)
            pe.wait_ge(fv_lo_done, NB)
            pe.wait_ge(decay_in, 8 * 16)
            pe.wait_ge(qk_lo, 8)
            scores_fox(0, (0, 1, 2))
            sgu_tile(1)
            for h in range(FOX_HEADS):
                for blocks, banks in (((0, 1), (0,)), ((2, 3), (1, 2))):
                    transposes(fox, h, f_prob, probs, NB * (HEADS + h + 1), blocks)
                    if h + 1 < FOX_HEADS:
                        scores_fox(h + 1, banks)
                weigh_fox(h)
                if h < 6:
                    sgu_tile(2 + h)
                if h == 6:
                    pe.wait_ge(ws_lo_done, 1)
                    pe.wait_ge(zvn_lo_done, NB)
                    pe.wait_ge(z_gelu, 4 * NB)
                    sgu_mix(range(4))
            sgu_mix(range(4, SGU_G))

            for first in (0, 4):
                for n in range(first, first + 4):
                    t = TILE["mix_out"] + n
                    wait_tile(0, t)
                    if first:
                        pe.wait_ge(norm["ffn"].x_ready, n - 3)
                    for k in range(AC):
                        if n == 0:
                            pe.wait_ge(attn_lo_done, k + 1)
                        last = three(bank[n % 4][:], *wblock(t, k), attn_hi[:, k, :], attn_lo[:, k, :], k == 0, k == AC - 1)
                    if n == 1:
                        mean(attn_summed, 1, attn_sqsum[:], bank[5], attn_mean)
                if first == 0:
                    for c in range(SC):
                        if c == 0:
                            pe.wait_ge(branch_scaled, NB)
                        if c >= 2:
                            pe.wait_ge(sgu_lo_done, c - 1)
                        for b in range(NB):
                            last = pe.transpose(bank[6 + c % 2][:, P * b:P * (b + 1)], zu[:, b, P * c:P * (c + 1)], ident[:])
                        last.then_inc(branch_t, 1)
                    pe.wait_ge(attn_prepared, 1)
                for n in range(first, first + 4):
                    t = TILE["mix_out"] + n
                    for k in range(SC):
                        if n == 0:
                            pe.wait_ge(sgu_lo_done, k + 1)
                        last = three(bank[4 + n % 4][:], *wblock(t, AC + k), sgu_hi[:, k, :], sgu_lo[:, k, :], k == 0, k == SC - 1)
                    last.then_inc(tile_used, 1)

            n = norm["ffn"]
            for turn, j in sweep(pe, 2 * FC):
                if starts(turn, j, 4):
                    pe.wait_ge(n.x_ready, j + 5)
                else:
                    pe.wait_ge(ffn_evac, turn * RING + (j - 3))
                projection("ffn_up", turn, j, bank[j % 4], ffn_xg_hi, ffn_xg_lo, n.xg_lo if starts(turn, j, 1) else None)
                if starts(turn, j, 1):
                    mean(n.summed, DC - 1, ffn_sqsum[:], bank[MEAN_BANK], n.mean)
            out_product("ffn_down", FC, lambda turn, j: (act_hi[:, turn * RING + j, :], act_lo[:, turn * RING + j, :]),
                        act_lo_done, lambda turn, j: turn * RING + (j + 1),
                        free=[[(ffn_evac, 2 * FC)]] + [[]] * 7)
            mean(norm["final"].summed, DC - 1, fin_sqsum[:], bank[0], norm["final"].mean)


def kernel(x, positions, pool_norm, pool_w_in, pool_w_group, pool_scale, pool_w_out, mla_norm, mla_w_in,
           mla_q_norm, mla_w_q_b, mla_kv_norm, mla_w_kv_b, mla_w_out, final_norm, mix_norm_g_2, w_in_2, b_f_2,
           sgu_ln_g_2, sgu_ln_b_2, w_s_2, b_s_2, out_norm_g_2, w_out_2, ffn_norm_g_2, w_gate_up_2, w_down_2,
           final_norm_g_2):
    import concourse.bacc as bacc
    from concourse.bass_utils import run_bass_kernel_spmd

    (x, positions, pool_norm, pool_w_in, pool_w_group, pool_scale, pool_w_out, mla_norm, mla_w_in, mla_q_norm,
     mla_w_q_b, mla_kv_norm, mla_w_kv_b, mla_w_out, mix_norm, w_in, b_f, ln_g, ln_b, w_s, b_s, out_norm, w_out,
     ffn_norm, w_gate_up, w_down) = (
        np.asarray(a)[0] for a in (
            x, positions, pool_norm, pool_w_in, pool_w_group, pool_scale, pool_w_out, mla_norm, mla_w_in,
            mla_q_norm, mla_w_q_b, mla_kv_norm, mla_w_kv_b, mla_w_out, mix_norm_g_2, w_in_2, b_f_2, sgu_ln_g_2,
            sgu_ln_b_2, w_s_2, b_s_2, out_norm_g_2, w_out_2, ffn_norm_g_2, w_gate_up_2, w_down_2))
    final_norm, final_norm_2 = np.asarray(final_norm), np.asarray(final_norm_g_2)

    stream = np.zeros((N_TILES, P, 8 * P), np.float32)

    def put(tile, at, part):
        stream[tile, :, at:at + part.shape[1]] = part

    def rows(w, k):
        return w[P * k:P * (k + 1)]

    def outputs(tile, w, at=0):
        for k in range(w.shape[0] // P):
            put(tile, at + P * k, rows(w, k))

    for n in range(2 * PC):
        outputs(TILE["pool_u"] + n, pool_w_in[:, P * n:P * (n + 1)])
    for c in range(PC):
        g, n = divmod(c, PG)
        outputs(TILE["pool_group"] + c // 2, pool_w_group[g][:, P * n:P * (n + 1)], PG * P * (c % 2))
    for name, w in (("pool_out", pool_w_out), ("mla_out", mla_w_out), ("ffn_down", w_down)):
        for k in range(w.shape[0] // P):
            put(TILE[name] + k, 0, rows(w, k))
    t = TILE["mla_in"]
    for n in range(LC):
        outputs(t + n, mla_w_in[:, P * n:P * (n + 1)])
    half_1 = mla_w_in[:, LC * P:LC * P + HALF]
    half_2 = mla_w_in[:, LC * P + HALF:LC * P + ROPE]
    outputs(t + LC, np.concatenate([half_1, half_2] * 2, axis=1))
    outputs(t + LC + 1, np.concatenate([half_2, half_1] * 2, axis=1))
    for n in range(PC):
        at = LC * P + ROPE + P * n
        outputs(t + LC + 2 + n, mla_w_in[:, at:at + P])
    w_q = mla_w_q_b.reshape(QC * P, HEADS, NOPE + ROPE)
    w_kv = mla_w_kv_b.reshape(KC * P, HEADS, NOPE + VD)
    for g in range(GROUPS):
        t = TILE["heads"] + 5 * g
        group = slice(GH * g, GH * (g + 1))
        for tile in GROUP_TILES[:GH]:
            for kind, j in tile:
                i, block = unit_place(kind, j)
                w = {"k": lambda: w_kv[:, GH * g + j, 0:NOPE],
                     "q": lambda: w_q[:, GH * g + j, 0:NOPE],
                     "rope": lambda: w_q[:, group, NOPE + HALF * j:NOPE + HALF * (j + 1)].reshape(QC * P, P)}[kind]()
                outputs(t + i, w, P * block)
        w_v = w_kv[:, group, NOPE:].reshape(KC * P, S)
        for k in range(KC):
            put(t + GH, S * k, rows(w_v, k))
    gates = 3 * D_ATTN
    for n in range(8):
        outputs(TILE["mix_qk"] + n + (n >= 4), w_in[:, P * n:P * (n + 1)])
    for k in range(DC):
        put(TILE["mix_qk"] + 4, P * k, rows(w_in, k)[:, gates:gates + FOX_HEADS])
        put(TILE["mix_v"] + k // 2, S * (k % 2), rows(w_in, k)[:, 2 * D_ATTN:gates])
    quarter = D_SGU // 2
    for c in range(4):
        at = gates + FOX_HEADS + (D_SGU if c < 2 else 0) + quarter * (c % 2)
        for k in range(DC):
            put(TILE["mix_z"] + 2 * c + k // 4, quarter * (k % 4), rows(w_in, k)[:, at:at + quarter])
    for n in range(DC):
        outputs(TILE["mix_out"] + n, w_out[:, P * n:P * (n + 1)])
    for n in range(FC):
        outputs(TILE["ffn_up"] + 2 * n, w_gate_up[:, P * n:P * (n + 1)])
        outputs(TILE["ffn_up"] + 2 * n + 1, w_gate_up[:, FF + P * n:FF + P * (n + 1)])

    def as_columns(v):
        return v.reshape(-1, P).T

    inv_freq = (1.0 / (10000.0 ** (np.arange(0, ROPE, 2, dtype=np.float32) / np.float32(ROPE)))).astype(np.float32)
    sign = np.repeat(np.array([-1, 1, -1, 1], np.float32), HALF)
    columns = np.concatenate([as_columns(v) for v in (
        pool_norm, pool_scale, mla_norm, mla_q_norm, mla_kv_norm, final_norm, mix_norm, out_norm, ffn_norm,
        final_norm_2, b_s, np.tile(inv_freq, GH), sign)], axis=1)
    counts = np.tile((1.0 / np.arange(1, PAD + 1)).astype(np.float32), (P, 1))
    lines = np.tile(np.concatenate([b_f, ln_g, ln_b]), (P, 1))
    arrays = {
        "x_in": x.T.reshape(DC, P, S).transpose(1, 0, 2),
        "stream": stream,
        "columns": columns,
        "counts_in": counts,
        "positions_in": np.tile(positions, (P, 1)),
        "lines": lines,
        "w_s": w_s.transpose(2, 0, 1).reshape(P, SGU_G * P),
    }
    arrays = {k: np.ascontiguousarray(v) for k, v in arrays.items()}

    nc = bacc.Bacc("TRN2", target_bir_lowering=False, num_devices=1)
    args = [nc.dram_tensor(k, v.shape, mybir.dt.from_np(v.dtype), kind="ExternalInput").ap() for k, v in arrays.items()]
    spill = nc.dram_tensor("spill", (P, DC, S), mybir.dt.float32, kind="Internal").ap()
    out = nc.dram_tensor("out", (P, DC, S), mybir.dt.float32, kind="ExternalOutput").ap()
    build(nc, *args, spill, out)
    r = run_bass_kernel_spmd(nc, [arrays], core_ids=[0])
    return r.results[0]["out"].transpose(1, 0, 2).reshape(D, S).T.reshape(1, S, D)
```

```python
from contextlib import ExitStack

import numpy as np

import concourse.bass as bass
from concourse import mybir

P = 128
S = 512
NB = S // P
D = 1024
DC = D // P
POOL_W = 2048
WINDOWS = (2, 4, 8, 16)
PAD = max(WINDOWS)
PC = POOL_W // P
PG = PC // len(WINDOWS)
HEADS, NOPE, ROPE, VD = 16, 128, 64, 128
HALF = ROPE // 2
QC, KC = 384 // P, 256 // P
LC = QC + KC
MLA_SCALE = float(NOPE + ROPE) ** -0.5
GH = P // HALF
GROUPS = HEADS // GH
FOX_HEADS, FOX_D = 8, 64
FOX_PAIRS = FOX_HEADS // 2
D_ATTN = FOX_HEADS * FOX_D
SGU_G, SGU_D = 8, 64
D_SGU = SGU_G * SGU_D
AC = D_ATTN // P
SC = D_SGU // P
SGU_HALF = 64
FF = 2816
FC = FF // P
EPS = 1e-6
MASKED = -1e30
ROW = [P * b * (b + 1) // 2 for b in range(NB + 1)]
COLUMN = [sum(S - P * c for c in range(b)) for b in range(NB + 1)]
SCORE_BANK = (0, 0, 1, 2)
SCORE_AT = (0, P, 0, 0)
TWO_PI = 6.283185307179586
TWO_PI_PARTS = (6.28125, 0.0019340515136718750, 1.2556659146e-06)
ROUNDER = 12582912.0

COLUMN_SIZES = (("pool_norm", DC), ("pool_scale", PC), ("mla_norm", DC), ("q_norm", QC), ("kv_norm", KC),
                ("final_norm", DC), ("mix_norm", DC), ("out_norm", DC), ("ffn_norm", DC),
                ("final_norm_2", DC), ("b_s", SGU_G), ("inv_freq", 1), ("rope_sign", 1))
COLUMNS = {name: sum(n for _, n in COLUMN_SIZES[:i]) for i, (name, _) in enumerate(COLUMN_SIZES)}
N_COLUMNS = sum(n for _, n in COLUMN_SIZES)

TILE_SIZES = (("pool_u", PC), ("pool_z", PC), ("pool_group", PC * PG // 8), ("pool_out", PC), ("mla_in", LC + 1 + PC + 1),
              ("heads", 5 * GROUPS - 1), ("mla_out", PC), ("mix_qk", 9), ("mix_v", 4), ("mix_z", 8),
              ("mix_out", DC), ("ffn_up", 2 * FC), ("ffn_down", FC))
TILE = {name: sum(n for _, n in TILE_SIZES[:i]) for i, (name, _) in enumerate(TILE_SIZES)}
N_TILES = sum(n for _, n in TILE_SIZES)
RING = 4
RAW = 2
POOL_OUT_CHUNKS = (0, 1)
DVE_OUT_CHUNKS = tuple(range(2, DC))
OUT_ORDER = (2, 3, 0, 4, 5, 1, 6, 7)
AHEAD = RING - 1


GROUP_TILES = ((("k", 0), ("rope", 0), ("rope", 1)), (("k", 1), ("q", 0), ("q", 1)), (("k", 2), ("q", 2)),
               (("k", 3), ("q", 3)), tuple(("v", b) for b in range(NB)))
UNITS = [(kind, g, j) for g in range(GROUPS) for tile in GROUP_TILES for kind, j in tile]
UNIT = {u: i for i, u in enumerate(UNITS)}
UNIT_BANK = [(4 + i) % 8 for i in range(10)] + [6, 7, 5, 6] + [6 + i % 2 for i in range(14, len(UNITS))]
CHUNKS_OF = {"k": KC, "q": QC, "rope": QC}


def unit_place(kind, j):
    for i, tile in enumerate(GROUP_TILES):
        if (kind, j) in tile:
            before = tile[:tile.index((kind, j))]
            return i, 0 if kind == "v" else sum(CHUNKS_OF[k] for k, _ in before)


EARLY = LC + 1 + PC - 3


def group_tile(g, i):
    return TILE["mla_in"] + EARLY if (g, i) == (0, 0) else TILE["heads"] - 1 + len(GROUP_TILES) * g + i


def sweep(engine, n, tail=0, first=0):
    turn_1, turns = max(1, -(-first // RING)), (n - tail) // RING
    done = min(turn_1 * RING, n)
    for unit in range(first, done):
        yield 0, unit
    if turns > turn_1 + 1:
        with engine.Fori(turn_1, turns) as turn:
            for j in range(RING):
                yield turn, j
        done = turns * RING
    for unit in range(done, n):
        yield 0, unit


def starts(turn, j, n):
    return isinstance(turn, int) and j < n


class NormSemaphores:
    def __init__(self, sem, stage, before, common):
        self.before = before
        self.mean, self.prepared, self.inv = common
        self.x_ready = sem(f"{stage}_x_ready") if stage != "pool" else None
        self.xg_hi = sem(f"{stage}_xg_hi") if stage != "final" else None
        self.xg_lo = sem(f"{stage}_xg_lo") if stage != "final" else None
        self.squared = sem(f"{stage}_squared")
        self.summed = sem(f"{stage}_summed")


class HeadSemaphores:
    def __init__(self, sem, kind):
        self.scores = sem(f"{kind}_scores")
        self.peaks = sem(f"{kind}_peaks")
        self.exped = sem(f"{kind}_exped")
        self.transposed = sem(f"{kind}_transposed")
        self.prob_t_hi = sem(f"{kind}_prob_t_hi")
        self.prob_t_lo = sem(f"{kind}_prob_t_lo")
        self.weighted = sem(f"{kind}_weighted")
        self.out = sem(f"{kind}_out")


def build(nc, x_in, stream, columns, counts_in, positions, rows_in, w_s, spill, out):
    f32, f32r, i32 = mybir.dt.float32, mybir.dt.float32r, mybir.dt.int32
    ACT = mybir.ActivationFunctionType
    ALU = mybir.AluOpType
    X = mybir.AxisListType.X
    ctx = ExitStack()
    with ctx:
        def sem(name):
            return ctx.enter_context(nc.semaphore(name))

        def sb(name, shape, dtype=f32):
            return ctx.enter_context(nc.sbuf_tensor(name, shape, dtype))

        def place(kib, name, shape, dtype=f32):
            with ExitStack() as s:
                if kib:
                    s.enter_context(nc.sbuf_tensor(f"below_{name}", [P, int(kib * 256)], f32))
                return s.enter_context(nc.sbuf_tensor(name, shape, dtype))

        def plain(ap):
            return ap.bitcast(f32)

        raw = sb("raw", [P, RAW, 1024])
        w_hi = sb("w_hi", [P, RING, 1024], f32r)
        w_lo = sb("w_lo", [P, RING, 1024], f32r)
        cols = sb("cols", [P, N_COLUMNS])
        counts = sb("counts", [P, PAD])
        gain12 = sb("gain12", [P, DC])
        ident = sb("ident", [P, P])
        ident_r = sb("ident_r", [P, P], f32r)
        mask = sb("mask", [P, P])
        mask_r = sb("mask_r", [P, P], f32r)
        fold = sb("fold", [P, P])
        upper = sb("upper", [P, P])
        ones = sb("ones", [P, P])
        inv = sb("inv", [P, S])
        mean_sq = sb("mean_sq", [P, S])
        peak = sb("peak", [P, 2, NB])
        neg_peak = sb("neg_peak", [P, 2, NB])
        row_sum = sb("row_sum", [P, 2, NB])
        inv_sum = sb("inv_sum", [P, 2, NB])
        inv_t = sb("inv_t", [P, NB])
        b_f = sb("b_f", [P, FOX_HEADS])
        gate = sb("gate", [P, NB, FOX_HEADS])
        gate_abs = sb("gate_abs", [P, NB, FOX_HEADS])
        log_f = sb("log_f", [P, NB, FOX_HEADS])
        stats = sb("stats", [P, NB, 6])
        moments = sb("moments", [P, NB, 2])
        rstd = sb("rstd", [P, NB])
        branch_sq = sb("branch_sq", [P, NB])
        branch_inv = sb("branch_inv", [P, NB])

        x = place(0, "x", [P, DC, S])
        z = place(16, "z", [P, PC, S])
        pool_xg_hi, pool_xg_lo = (place(48 + 16 * i, f"pool_xg_{i}", [P, DC, S], f32r) for i in range(2))
        pooled_hi, pooled_lo = (place(80 + 32 * i, f"pooled_{i}", [P, PC, S], f32r) for i in range(2))
        pool_sq, pool_sqsum = place(144, "pool_sq", [P, 2, S]), place(148, "pool_sqsum", [P, S])
        u_pad = place(144, "u_pad", [P, 2, PAD + S])
        sum_a, sum_b = place(148.25, "sum_a", [P, PAD + S]), place(150.5, "sum_b", [P, PAD + S])
        pooled = place(152.75, "pooled", [P, 2, S])
        y_hi = place(48, "y_hi", [P, PC, S], f32r)
        y_lo = place(16, "y_lo", [P, PC, S], f32r)
        lat_hi, lat_lo = (place(48 + 10 * i, f"lat_{i}", [P, LC, S], f32r) for i in range(2))
        rope_k_hi, rope_k_lo = (place(68 + 2 * i, f"rope_k_{i}", [P, S], f32r) for i in range(2))
        rope_a = place(76, "rope_a", [P, S])
        cos, sin = place(154.5, "cos", [P, S]), place(156.5, "sin", [P, S])
        lat = place(126, "lat", [P, LC, S])
        mla_xg_hi, mla_xg_lo = (place(80 + 16 * i, f"mla_xg_{i}", [P, DC, S], f32r) for i in range(2))
        mla_sq, mla_sqsum = place(138, "mla_sq", [P, 2, S]), place(142, "mla_sqsum", [P, S])
        pos_i, angle = place(144, "pos_i", [P, S], i32), place(146, "angle", [P, S])
        turns_of, reduced = place(148, "turns_of", [P, S]), place(150, "reduced", [P, S])
        lat_sq, lat_sqsum = place(112, "lat_sq", [P, LC, S]), place(122, "lat_sqsum", [P, 2, S])
        v_hi, v_lo = (place(76 + 8 * i, f"v_{i}", [P, NB, S], f32r) for i in range(2))
        k_hi, k_lo = (place(8 * i, f"k_{i}", [P, GH, S], f32r) for i in range(2))
        q_hi, q_lo = (place(92 + 8 * i, f"q_{i}", [P, GH, S], f32r) for i in range(2))
        rope_q = place(112, "rope_q", [P, 2, GH, S], f32r)
        prob = place(128, "prob", [P, ROW[NB]])
        prob_t_hi, prob_t_lo = (place(133 + 5 * i, f"prob_t_{i}", [P, COLUMN[NB]], f32r) for i in range(2))
        turned_1, turned_2 = place(72, "turned_1", [P, S]), place(74, "turned_2", [P, S])
        rope_t = place(143, "rope_t", [P, S])
        turned_hi, turned_lo = (place(145 + 4 * i, f"turned_hl_{i}", [P, 2, S], f32r) for i in range(2))
        fq_hi, fq_lo = (place(16 + 8 * i, f"fq_{i}", [P, FOX_PAIRS, S], f32r) for i in range(2))
        fk_hi, fk_lo = (place(32 + 8 * i, f"fk_{i}", [P, FOX_PAIRS, S], f32r) for i in range(2))
        fv_hi, fv_lo = (place(48 + 8 * i, f"fv_{i}", [P, NB, D_ATTN], f32r) for i in range(2))
        decay_q = place(64, "decay_q", [P, 2, S], f32r)
        decay_k = place(68, "decay_k", [P, 2, S], f32r)
        ln_g, ln_b = place(72, "ln_g", [P, D_SGU]), place(74, "ln_b", [P, D_SGU])
        inv_1 = place(78, "inv_1", [P, S])
        zu, zv = place(80, "zu", [P, NB, D_SGU]), place(88, "zv", [P, NB, D_SGU])
        zvn_hi, zvn_lo = place(128, "zvn_hi", [P, NB, D_SGU], f32r), place(88, "zvn_lo", [P, NB, D_SGU], f32r)
        mix_xg_hi, mix_xg_lo = (place(96 + 16 * i, f"mix_xg_{i}", [P, DC, S], f32r) for i in range(2))
        mix_sq, mix_sqsum = place(128, "mix_sq", [P, 2, 2, S]), place(136, "mix_sqsum", [P, 2, S])
        c_parts = place(128, "c_parts", [FOX_HEADS, 4, S], f32r)
        ws_raw, ws_lo = place(141, "ws_raw", [P, SGU_G * P]), place(141, "ws_lo", [P, SGU_G * P], f32r)
        ws_hi = place(76, "ws_hi", [P, SGU_G * P], f32r)
        f_prob = place(136, "f_prob", [P, ROW[NB]])
        f_prob_t_hi, f_prob_t_lo = (place(145 + 5 * i, f"f_prob_t_{i}", [P, COLUMN[NB]], f32r) for i in range(2))
        qk_t, f_t = place(149, "qk_t", [P, 2, S]), place(155, "f_t", [P, S])
        junk = place(155, "junk", [P, S])
        attn = place(16, "attn", [P, FOX_PAIRS, S])
        attn_hi, attn_lo = (place(32 + 8 * i, f"attn_{i}", [P, FOX_PAIRS, S], f32r) for i in range(2))
        sgu_hi, sgu_lo = (place(48 + 8 * i, f"sgu_{i}", [P, SC, S], f32r) for i in range(2))
        attn_sq, attn_sqsum = place(64, "attn_sq", [P, FOX_PAIRS, S]), place(72, "attn_sqsum", [P, S])
        attn_inv, mixed = place(74, "attn_inv", [P, S]), place(76, "mixed", [P, 2, S])
        ffn_xg_hi, ffn_xg_lo = (place(104 + 16 * i, f"ffn_xg_{i}", [P, DC, S], f32r) for i in range(2))
        ffn_sq, ffn_sqsum = place(136, "ffn_sq", [P, 2, S]), place(140, "ffn_sqsum", [P, S])
        act_hi, act_lo = (place(16 + 44 * i, f"act_{i}", [P, FC, S], f32r) for i in range(2))
        gated, up = place(142, "gated", [P, 2, S]), place(146, "up", [P, 2, S])
        fin_sq, fin_sqsum = place(104, "fin_sq", [P, 2, S]), place(108, "fin_sqsum", [P, S])
        x_gained = place(110, "x_gained", [P, DC, S])

        bank = [ctx.enter_context(nc.psum_tensor(f"bank{b}", [P, S], f32)) for b in range(8)]
        MEAN_BANK = 7

        def col(name, k=0):
            at = COLUMNS[name] + k
            return cols[:, at:at + 1]

        tile_loaded = [sem(f"tile_loaded_{i}") for i in range(RAW)]
        tile_hi, tile_lo, tile_used = sem("tile_hi"), sem("tile_lo"), sem("tile_used")
        cols_in, small_in, ln_in = sem("cols_in"), sem("small_in"), sem("ln_in")
        patterns, made = sem("patterns"), sem("made")
        x_loaded = [sem(f"x_loaded_{i}") for i in range(4)]
        common = sem("norm_mean"), sem("norm_prepared"), sem("norm_inv")
        norm = {n: NormSemaphores(sem, n, before, common)
                for n, before in (("pool", 0), ("mla", 1), ("mix", 2), ("ffn", 4), ("final", 5))}
        steps = sem("dve_steps")
        asteps = sem("act_steps")
        in_evac, pooled_ready = sem("in_evac"), sem("pooled_ready")
        pooled_hi_done, pooled_lo_done = sem("pooled_hi_done"), sem("pooled_lo_done")
        z_silu = sem("z_silu")
        half_tile = sem("half_tile")
        y_ready = sem("y_ready")
        y_hi_done, y_lo_done = sem("y_hi_done"), sem("y_lo_done")
        chunk_done = sem("chunk_done")
        pos_in, angle_ready, table_done = sem("pos_in"), sem("angle_ready"), sem("table_done")
        mla_evac, lat_squared, lat_summed = sem("mla_evac"), sem("lat_squared"), sem("lat_summed")
        lat_mean, lat_prepared, lat_inv = sem("lat_mean"), sem("lat_prepared"), sem("lat_inv")
        lat_ready, lat_hi_done, lat_lo_done = sem("lat_ready"), sem("lat_hi_done"), sem("lat_lo_done")
        rope_k_summed = sem("rope_k_summed")
        rope_k_ready, rope_k_hi_done, rope_k_lo_done = sem("rope_k_ready"), sem("rope_k_hi_done"), sem("rope_k_lo_done")
        mz_silu = sem("mz_silu")
        x_spilled, x_back = sem("x_spilled"), sem("x_back")
        unit_done, unit_hi, unit_evac = sem("unit_done"), sem("unit_hi"), sem("unit_evac")
        turned, turned_hi_done, turned_lo_done, rope_q_in = sem("turned"), sem("turned_hi_done"), sem("turned_lo_done"), sem("rope_q_in")

        mla, fox = HeadSemaphores(sem, "mla_head"), HeadSemaphores(sem, "fox_head")
        probs, sum_inverted = sem("head_probs"), sem("sum_inverted")
        qk_ready, qk_hi, qk_lo = sem("qk_ready"), sem("qk_hi"), sem("qk_lo")
        inv_t_sum, inv_t_ready = sem("inv_t_sum"), sem("inv_t_ready")
        v_summed, fv_hi_done, fv_lo_done = sem("v_summed"), sem("fv_hi_done"), sem("fv_lo_done")
        f_summed, gate_abs_ready, gate_log, log_f_ready = sem("f_summed"), sem("gate_abs_ready"), sem("gate_log"), sem("log_f_ready")
        c_summed, c_hi_done, c_ready, decay_in = sem("c_summed"), sem("c_hi_done"), sem("c_ready"), sem("decay_in")
        f_ready, x_scaled = sem("f_ready"), sem("x_scaled")
        inv_both, decay_ones = sem("inv_both"), sem("decay_ones")
        z_evac, z_gelu = sem("z_evac"), sem("z_gelu")
        ln_prepared, ln_rstd, zvn_ready, zvn_hi_done, zvn_lo_done = (sem(n) for n in ("ln_prepared", "ln_rstd", "zvn_ready", "zvn_hi_done", "zvn_lo_done"))
        ln_centred, ln_gained = sem("ln_centred"), sem("ln_gained")
        ws_in, ws_cut, ws_hi_done, ws_lo_done = sem("ws_in"), sem("ws_cut"), sem("ws_hi_done"), sem("ws_lo_done")
        sgu_mixed, sgu_gated = sem("sgu_mixed"), sem("sgu_gated")
        branch_squared, branch_prepared, branch_inv_done, branch_scaled = (sem(n) for n in ("branch_squared", "branch_prepared", "branch_inv_done", "branch_scaled"))
        branch_t, sgu_hi_done, sgu_lo_done = sem("branch_t"), sem("sgu_hi_done"), sem("sgu_lo_done")
        attn_hi_done, attn_lo_done = sem("attn_hi_done"), sem("attn_lo_done")
        attn_squared, attn_summed, attn_mean, attn_prepared, attn_inv_done = (sem(n) for n in ("attn_squared", "attn_summed", "attn_mean", "attn_prepared", "attn_inv_done"))
        ffn_evac, gate_silu, act_ready, act_hi_done, act_lo_done = (sem(n) for n in ("ffn_evac", "gate_silu", "act_ready", "act_hi_done", "act_lo_done"))
        gained, pool_out_ready = sem("gained"), sem("pool_out_ready")
        out_ready, stored = sem("out_ready"), sem("stored")

        def unit_tile(u):
            return group_tile(u[1], unit_place(u[0], u[2])[0])

        def ends_tile(u):
            return GROUP_TILES[unit_place(u[0], u[2])[0]][-1] == (u[0], u[2])

        def wait_unit(engine, u):
            if ends_tile(u):
                engine.wait_ge(tile_used, unit_tile(u) + 1)
            else:
                engine.wait_ge(unit_done, sum(not ends_tile(o) for o in UNITS[:UNIT[u] + 1]))

        def hi_units(u):
            return sum(o[0] != "rope" for o in UNITS[:UNIT[u] + 1])

        def store(engine, k):
            if k in POOL_OUT_CHUNKS:
                engine.wait_ge(pool_out_ready, POOL_OUT_CHUNKS.index(k) + 1)
                engine.dma_start(out[:, k, :], x_gained[:, k, :]).then_inc(stored, 16)
            else:
                engine.wait_ge(out_ready, DVE_OUT_CHUNKS.index(k) + 1)
                engine.dma_start(out[:, k, :], x[:, k, :]).then_inc(stored, 16)

        block = ctx.enter_context(nc.Block())

        @block.sync
        def _(sp):
            sp.dma_start(raw[:, 0, :], stream[0]).then_inc(tile_loaded[0], 16)
            for i in range(4):
                sp.dma_start(x[:, 2 * i:2 * i + 2, :], x_in[:, 2 * i:2 * i + 2, :]).then_inc(x_loaded[i], 16)
            sp.dma_start(raw[:, 1, :], stream[1]).then_inc(tile_loaded[1], 16)

            def load(turn, j):
                if not starts(turn, j, RAW):
                    sp.wait_ge(tile_lo, turn * RING + (j - RAW + 1))
                    sp.dma_start(raw[:, j % RAW, :], stream[turn * RING + j]).then_inc(tile_loaded[j % RAW], 16)

            def rope_rows(g, part, halves):
                if part == 0:
                    sp.wait_ge(turned_hi_done, 2 * g + 2)
                else:
                    sp.wait_ge(turned_lo_done, 2 * g + 2)
                for i in halves:
                    source, at = (turned_hi, turned_lo)[part], HALF * (2 * part + i)
                    for h in range(GH):
                        sp.dma_start(plain(rope_q[at:at + HALF, g % 2, h, :]),
                                     plain(source[HALF * h:HALF * h + HALF, i, :])).then_inc(rope_q_in, 16)

            for turn, j in sweep(sp, TILE["heads"]):
                load(turn, j)
            for i in range(5 * GROUPS):
                load(0, TILE["heads"] + i)
                if i < 4:
                    rope_rows(0, i // 2, (i % 2,))
                elif i >= 8 and (i - 3) % 5 < 2:
                    rope_rows((i - 3) // 5, (i - 3) % 5, (0, 1))
            for turn, j in sweep(sp, N_TILES, first=TILE["heads"] + 5 * GROUPS):
                load(turn, j)
            for k in OUT_ORDER[1::2]:
                store(sp, k)
            sp.wait_ge(stored, 16 * DC)

        @block.gpsimd
        def _(pool):
            pool.memset(ident[:], 0.0).then_inc(patterns, 1)
            pool.memset(mask[:], 0.0).then_inc(patterns, 1)
            pool.memset(upper[:], 1.0).then_inc(patterns, 1)
            pool.wait_ge(patterns, 3)
            pool.affine_select(out=ident[:], in_=ident[:], compare_op=ALU.not_equal, fill=1.0, base=0,
                               pattern=[[-1, P]], channel_multiplier=1).then_inc(patterns, 1)
            pool.affine_select(out=mask[:], in_=mask[:], compare_op=ALU.is_ge, fill=MASKED, base=0,
                               pattern=[[-1, P]], channel_multiplier=1).then_inc(patterns, 1)
            pool.affine_select(out=upper[:], in_=upper[:], compare_op=ALU.is_ge, fill=0.0, base=0,
                               pattern=[[1, P]], channel_multiplier=-1).then_inc(patterns, 1)

            def low_tiles(n, first=0):
                for turn, j in sweep(pool, n, first=first):
                    pool.wait_ge(tile_hi, turn * RING + (j + 1))
                    pool.tensor_tensor(w_lo[:, j % RING, :], raw[:, j % RAW, :], plain(w_hi[:, j % RING, :]),
                                       ALU.subtract).then_inc(tile_lo, 1)

            low_tiles(TILE["mla_out"] + RING)
            for k in range(PC):
                pool.wait_ge(y_hi_done, PC + k + 1)
                pool.tensor_tensor(y_lo[:, k, :], z[:, k, :], plain(y_hi[:, k, :]), ALU.subtract).then_inc(y_lo_done, 1)
            first = TILE["mla_out"] + RING
            for step, blocks in enumerate(((0, 1), (2, 3), (0, 1), (2, 3))):
                n = TILE["mix_z"] + 8 + min(step, 2)
                if n > first:
                    low_tiles(n, first=first)
                    first = n
                for b in blocks:
                    if step < 2:
                        pool.wait_ge(ln_centred, b + 1)
                        if b == 0:
                            pool.wait_ge(ln_in, 32)
                        pool.tensor_tensor(zv[:, b, :], zv[:, b, :], ln_g[:], ALU.mult).then_inc(ln_gained, 1)
                        pool.wait_ge(ln_gained, b + 1)
                        pool.tensor_tensor(zv[:, b, :], zv[:, b, :], ln_b[:], ALU.add).then_inc(zvn_ready, 1)
                    else:
                        pool.wait_ge(zvn_hi_done, b + 1)
                        pool.tensor_tensor(zvn_lo[:, b, :], zv[:, b, :], plain(zvn_hi[:, b, :]), ALU.subtract).then_inc(zvn_lo_done, 1)
            low_tiles(N_TILES, first=first)
            pool.wait_ge(norm["final"].inv, norm["final"].before + 1)
            for k in POOL_OUT_CHUNKS:
                pool.wait_ge(gained, k + 1)
                pool.tensor_tensor(x_gained[:, k, :], x_gained[:, k, :], inv[:], ALU.mult).then_inc(pool_out_ready, 1)

        @block.scalar
        def _(act):
            own = [0]

            def settle(instruction):
                own[0] += 1
                instruction.then_inc(asteps, 1)
                act.wait_ge(asteps, own[0])

            def split_tile(stage, turn, j):
                t = TILE[stage] + j + AHEAD
                if isinstance(turn, int) and t >= N_TILES:
                    return
                act.wait_ge(tile_loaded[t % RAW], turn * (16 * RING // RAW) + 16 * (t // RAW + 1))
                if not starts(turn, t, RING):
                    act.wait_ge(tile_used, turn * RING + (t - RING + 1))
                act.activation(w_hi[:, t % RING, :], raw[:, t % RAW, :], ACT.Copy).then_inc(tile_hi, 1)

            def norm_in_chunk(n, k, xg, sq, sqsum, gain):
                act.wait_ge(n.x_ready, k + 1)
                act.activation(xg[:, k, :], x[:, k, :], ACT.Copy, scale=gain(k)).then_inc(n.xg_hi, 1)
                if k >= 3:
                    act.wait_ge(n.summed, k - 2)
                act.activation(sq[:, k % 2, :] if k else sqsum[:], x[:, k, :], ACT.Square).then_inc(n.squared, 1)

            def norm_root(n):
                act.wait_ge(n.prepared, n.before + 1)
                act.activation(inv[:], mean_sq[:], ACT.Sqrt).then_inc(n.inv, 1)

            act.dma_start(cols[:], columns).then_inc(cols_in, 16)
            act.dma_start(counts[:], counts_in).then_inc(small_in, 16)
            act.dma_start(b_f[:], rows_in[:, 0:FOX_HEADS]).then_inc(small_in, 16)
            split_tile("pool_u", 0, -3)
            act.wait_ge(cols_in, 16)
            n = norm["pool"]
            for k in range(DC):
                act.wait_ge(x_loaded[k // 2], 16)
                act.activation(pool_xg_hi[:, k, :], x[:, k, :], ACT.Copy, scale=col("pool_norm", k)).then_inc(n.xg_hi, 1)
            split_tile("pool_u", 0, -2)
            for k in range(DC):
                if k >= 3:
                    act.wait_ge(n.summed, k - 2)
                act.activation(pool_sq[:, k % 2, :] if k else pool_sqsum[:], x[:, k, :], ACT.Square).then_inc(n.squared, 1)
                if k == 3:
                    split_tile("pool_u", 0, -1)
            for n in range(PC):
                split_tile("pool_u", 0, n)
                if n == 0:
                    norm_root(norm["pool"])
                else:
                    act.wait_ge(pooled_ready, n)
                    act.activation(pooled_hi[:, n - 1, :], pooled[:, (n - 1) % 2, :], ACT.Copy).then_inc(pooled_hi_done, 1)
            for n in range(PC):
                split_tile("pool_z", 0, n)
                if n in (6, 9):
                    i = (n - 6) // 3
                    act.wait_ge(angle_ready, i + 1)
                    act.activation((sin, cos)[i][:], reduced[:], ACT.Sin).then_inc(table_done, 1)
                if n == 0:
                    act.wait_ge(pooled_ready, PC)
                    act.dma_start(pos_i[:], positions).then_inc(pos_in, 16)
                    act.activation(pooled_hi[:, PC - 1, :], pooled[:, (PC - 1) % 2, :], ACT.Copy).then_inc(pooled_hi_done, 1)
                else:
                    act.wait_ge(in_evac, PC + n)
                    act.activation(z[:, n - 1, :], z[:, n - 1, :], ACT.Silu).then_inc(z_silu, 1)
            act.wait_ge(in_evac, 2 * PC)
            act.activation(z[:, PC - 1, :], z[:, PC - 1, :], ACT.Silu).then_inc(z_silu, 1)

            def y_high(k, before=0):
                act.wait_ge(mla.out if before else y_ready, k + 1)
                act.activation(y_hi[:, k, :], z[:, k, :], ACT.Copy).then_inc(y_hi_done, 1)

            def out_stage(stage, norm_chunk, first=0):
                for k in range(first, PC):
                    split_tile(stage, 0, k)
                    if k >= 3 and k % 2:
                        norm_chunk((k - 3) // 2)
                norm_chunk(DC - 1)

            for n in range(PC * PG // 8):
                split_tile("pool_group", 0, n)
                if n:
                    y_high(2 * n - 2)
                    y_high(2 * n - 1)
            y_high(PC - 2)
            y_high(PC - 1)
            out_stage("pool_out", lambda k: norm_in_chunk(norm["mla"], k, mla_xg_hi, mla_sq, mla_sqsum, lambda c: col("mla_norm", c)))

            def unit_high(u):
                kind, g, j = u
                if u == ("k", 0, 0):
                    act.wait_ge(x_spilled, 16)
                target = {"k": k_hi, "q": q_hi, "v": v_hi}[kind]
                wait_unit(act, u)
                act.activation(target[:, j, :], bank[UNIT_BANK[UNIT[u]]][:], ACT.Copy).then_inc(unit_hi, 1)

            def prepare_tile(g, i):
                for n, (kind, k) in enumerate(GROUP_TILES[i]):
                    if kind != "rope":
                        unit_high((kind, g, k))
                    if n == 0:
                        t = group_tile(g, i)
                        stage = "mla_in" if t < TILE["heads"] else "heads"
                        split_tile(stage, 0, t - TILE[stage])

            def prepare(g, j):
                for i in (j,) if j < GH - 1 else (j, GH):
                    prepare_tile(g, i)

            def turn_split(g):
                act.wait_ge(turned, 2 * g + 2)
                if g:
                    act.wait_ge(rope_q_in, 256 * g)
                for i, t in enumerate((turned_1, turned_2)):
                    act.activation(turned_hi[:, i, :], t[:], ACT.Copy).then_inc(turned_hi_done, 1)

            act.dma_start(spill, x[:]).then_inc(x_spilled, 16)
            for u in range(LC + 1 + PC):
                if u == EARLY:
                    prepare_tile(0, 0)
                split_tile("mla_in", 0, u + int(u >= EARLY))
                if u == 0:
                    norm_root(norm["mla"])
                if 1 <= u <= LC:
                    act.wait_ge(mla_evac, u)
                    act.activation(lat_sq[:, u - 1, :], lat[:, u - 1, :], ACT.Square).then_inc(lat_squared, 1)
                if u == LC + 1:
                    for i in range(2):
                        act.wait_ge(lat_prepared, i + 1)
                        act.activation(lat_sqsum[:, i, :], lat_sqsum[:, i, :], ACT.Sqrt).then_inc(lat_inv, 1)
                    act.wait_ge(rope_k_summed, 1)
                    act.activation(rope_k_hi[:], bank[5][:], ACT.Copy).then_inc(rope_k_hi_done, 1)
                if u == LC + 3:
                    for i in range(LC):
                        act.wait_ge(lat_ready, i + 1)
                        act.activation(lat_hi[:, i, :], lat[:, i, :], ACT.Copy).then_inc(lat_hi_done, 1)
                if u > LC + 1:
                    n = u - LC - 2
                    act.wait_ge(mla_evac, LC + 1 + n + 1)
                    act.activation(z[:, n, :], z[:, n, :], ACT.Silu).then_inc(mz_silu, 1)
                if u == EARLY:
                    turn_split(0)
            act.wait_ge(mla_evac, LC + 1 + PC)
            act.activation(z[:, PC - 1, :], z[:, PC - 1, :], ACT.Silu).then_inc(mz_silu, 1)

            def exps(s, h, target, scale):
                for b in range(NB):
                    act.wait_ge(s.peaks, 3 * h + SCORE_BANK[b] + 1)
                    if b == 0 and h:
                        act.wait_ge(s.transposed, NB * h)
                    n = P * (b + 1)
                    act.activation(target[:, ROW[b]:ROW[b + 1]], bank[SCORE_BANK[b]][:, SCORE_AT[b]:SCORE_AT[b] + n],
                                   ACT.Exp, bias=neg_peak[:, h % 2, b:b + 1], scale=scale,
                                   accum_out=row_sum[:, h % 2, b:b + 1]).then_inc(s.exped, 1)

            def normalise_last(h, target, before=0):
                b = NB - 1
                act.wait_ge(sum_inverted, before + h + 1)
                act.activation(target[:, ROW[b]:ROW[b + 1]], target[:, ROW[b]:ROW[b + 1]], ACT.Copy,
                               scale=inv_sum[:, h % 2, b:b + 1]).then_inc(probs, 1)

            def transposed_high(s, h, target):
                if h:
                    act.wait_ge(s.weighted, h)
                for b in range(NB):
                    act.wait_ge(s.transposed, NB * h + b + 1)
                    act.activation(target[:, COLUMN[b]:COLUMN[b + 1]], bank[3 + b % 2][:, 0:S - P * b],
                                   ACT.Copy).then_inc(s.prob_t_hi, 1)

            for j in range(1, GH):
                prepare_tile(0, j)
            exps(mla, 0, prob, MLA_SCALE)
            normalise_last(0, prob)
            prepare_tile(0, GH)
            for h in range(HEADS):
                g, j = h // GH + 1, h % GH
                transposed_high(mla, h, prob_t_hi)
                if h + 1 < HEADS:
                    exps(mla, h + 1, prob, MLA_SCALE)
                    normalise_last(h + 1, prob)
                if g < GROUPS:
                    if j == 1:
                        turn_split(g)
                    prepare(g, j)
                elif h == 12:
                    split_tile("mla_out", 0, 0)
                for k in {12: range(0, 4), 13: range(4, 8), 14: (8, 9), 15: range(10, 14)}.get(h, ()):
                    y_high(k, PC)

            act.wait_ge(mla.weighted, HEADS)
            act.dma_start(x[:], spill).then_inc(x_back, 16)
            for k in range(14, PC):
                y_high(k, PC)

            n = norm["mix"]

            def mix_norm_chunk(k):
                act.wait_ge(n.x_ready, k + 1)
                act.activation(mix_xg_hi[:, k, :], x[:, k, :], ACT.Copy, scale=gain12[:, k:k + 1]).then_inc(n.xg_hi, 1)
                if k >= 3:
                    act.wait_ge(n.summed, 2 * (k - 2))
                act.activation(mix_sq[:, k % 2, 0, :] if k else mix_sqsum[:, 0, :], x[:, k, :], ACT.Square).then_inc(n.squared, 1)
                act.activation(mix_sq[:, k % 2, 1, :] if k else mix_sqsum[:, 1, :], x[:, k, :], ACT.Square,
                               scale=col("final_norm", k)).then_inc(n.squared, 1)

            out_stage("mla_out", mix_norm_chunk, first=1)
            act.dma_start(ln_g[:], rows_in[:, FOX_HEADS:FOX_HEADS + D_SGU]).then_inc(ln_in, 16)
            act.dma_start(ln_b[:], rows_in[:, FOX_HEADS + D_SGU:]).then_inc(ln_in, 16)
            act.wait_ge(n.summed, 2 * (DC - 1))
            act.dma_start(ws_raw[:], w_s).then_inc(ws_in, 16)
            for u in range(9):
                split_tile("mix_qk", 0, u)
                if u == 0:
                    act.wait_ge(n.prepared, n.before + 1)
                    act.activation(inv_1[:], mean_sq[:], ACT.Sqrt).then_inc(n.inv, 1)
                    act.wait_ge(n.prepared, n.before + 2)
                    act.activation(inv[:], mean_sq[:], ACT.Sqrt).then_inc(n.inv, 1)
                elif u != 5:
                    m = u if u < 5 else u - 1
                    act.wait_ge(qk_ready, m)
                    target = fq_hi if m <= 4 else fk_hi
                    act.activation(target[:, (m - 1) % 4, :], qk_t[:, (m - 1) % 2, :], ACT.Copy).then_inc(qk_hi, 1)
                if u == 7:
                    act.wait_ge(gate_abs_ready, 1)
                    settle(act.activation(gate_abs[:], gate_abs[:], ACT.Exp, scale=-1.0))
                    act.activation(gate_abs[:], gate_abs[:], ACT.Ln, bias=1.0).then_inc(gate_log, 1)
            split_tile("mix_v", 0, 0)
            act.wait_ge(qk_ready, 8)
            act.activation(fk_hi[:, 3, :], qk_t[:, 1, :], ACT.Copy).then_inc(qk_hi, 1)
            act.wait_ge(c_summed, 1)
            act.activation(c_parts[:, 0, :], bank[6][0:FOX_HEADS, :], ACT.Copy).then_inc(c_hi_done, 1)
            split_tile("mix_v", 0, 1)
            act.wait_ge(decay_ones, 1)
            act.wait_ge(c_ready, 1)
            for s in range(2):
                for part in range(2):
                    act.dma_start(plain(decay_q[part:P:32, s, :]), plain(c_parts[4 * s:4 * s + 4, part, :])).then_inc(decay_in, 16)
                    act.dma_start(plain(decay_k[2 + part:P:32, s, :]), plain(c_parts[4 * s:4 * s + 4, 2 + part, :])).then_inc(decay_in, 16)
            split_tile("mix_v", 0, 2)
            act.wait_ge(ws_cut, 1)
            act.wait_ge(x_scaled, 1)
            act.activation(ws_hi[:], ws_raw[:], ACT.Copy).then_inc(ws_hi_done, 1)
            split_tile("mix_v", 0, 3)
            act.wait_ge(inv_t_ready, 1)
            for b in range(NB):
                if b == NB - 1:
                    act.wait_ge(tile_used, TILE["mix_z"])
                else:
                    act.wait_ge(v_summed, b + 1)
                act.activation(fv_hi[:, b, :], bank[b][:], ACT.Copy, scale=inv_t[:, b:b + 1]).then_inc(fv_hi_done, 1)

            def sgu_evacuate(c):
                act.wait_ge(tile_used, TILE["mix_z"] + 2 * c + 2)
                half = slice(D_SGU // 2 * (c % 2), D_SGU // 2 * (c % 2 + 1))
                for b in range(NB):
                    at = D_SGU // 2 * (b % 2)
                    act.activation((zv, zu)[c // 2][:, b, half], bank[6 + b // 2][:, at:at + D_SGU // 2], ACT.Copy,
                                   scale=inv_t[:, b:b + 1]).then_inc(z_evac, 1)

            def gelu(i):
                act.wait_ge(z_evac, 2 * NB * (i + 1))
                act.activation((zv, zu)[i][:], (zv, zu)[i][:], ACT.Gelu).then_inc(z_gelu, 1)

            def attn_high(pair):
                act.wait_ge(fox.out, 2 * pair + 2)
                act.activation(attn_hi[:, pair, :], attn[:, pair, :], ACT.Copy, scale=col("out_norm", pair)).then_inc(attn_hi_done, 1)

            def norms_high(blocks):
                for b in blocks:
                    act.wait_ge(zvn_ready, b + 1)
                    act.activation(zvn_hi[:, b, :], zv[:, b, :], ACT.Copy).then_inc(zvn_hi_done, 1)

            split_tile("mix_z", 0, 0)
            exps(fox, 0, f_prob, 1.0)
            normalise_last(0, f_prob, HEADS)
            split_tile("mix_z", 0, 1)
            sgu_evacuate(0)
            for h in range(FOX_HEADS):
                transposed_high(fox, h, f_prob_t_hi)
                if h in (2, 4, 6):
                    sgu_evacuate(h // 2)
                if h + 1 < FOX_HEADS:
                    exps(fox, h + 1, f_prob, 1.0)
                    normalise_last(h + 1, f_prob, HEADS)
                if h < 6:
                    split_tile("mix_z", 0, 2 + h)
                if h in (2, 7):
                    gelu(h // 4)
                if h == 3:
                    act.wait_ge(decay_in, 8 * 16)
                    act.wait_ge(ln_prepared, 1)
                    act.activation(rstd[:], rstd[:], ACT.Sqrt).then_inc(ln_rstd, 1)
                if h == 5:
                    norms_high((0, 1))
                if h == 6:
                    norms_high((2, 3))
                if h % 2 == 0 and h:
                    attn_high(h // 2 - 1)
            attn_high(FOX_PAIRS - 1)
            split_tile("mix_out", 0, 0)
            for pair in range(FOX_PAIRS):
                act.activation(attn_sq[:, pair, :], attn[:, pair, :], ACT.Square).then_inc(attn_squared, 1)
            act.wait_ge(sgu_gated, SGU_G)
            for b in range(NB):
                if b:
                    act.wait_ge(branch_squared, b)
                act.activation(junk[:], zu[:, b, :], ACT.Square, accum_out=branch_sq[:, b:b + 1]).then_inc(branch_squared, 1)
            act.wait_ge(branch_prepared, 1)
            act.activation(branch_inv[:], branch_inv[:], ACT.Sqrt).then_inc(branch_inv_done, 1)
            act.wait_ge(attn_prepared, 1)
            act.activation(attn_inv[:], attn_inv[:], ACT.Sqrt).then_inc(attn_inv_done, 1)
            for c in range(SC):
                act.wait_ge(branch_t, c + 1)
                act.activation(sgu_hi[:, c, :], bank[6 + c % 2][:], ACT.Copy, scale=col("out_norm", AC + c)).then_inc(sgu_hi_done, 1)
            n = norm["ffn"]
            for k in range(DC):
                if k:
                    split_tile("mix_out", 0, k)
                for c in ((), (), (), (), (0, 1, 2, 3), (4,), (5,), (6, 7))[k]:
                    norm_in_chunk(n, c, ffn_xg_hi, ffn_sq, ffn_sqsum, lambda c: col("ffn_norm", c))


            def act_high(turn, n):
                index = turn * 2 + n
                act.wait_ge(act_ready, index + 1)
                act.activation(act_hi[:, index, :], up[:, n % 2, :], ACT.Copy).then_inc(act_hi_done, 1)

            for turn, j in sweep(act, 2 * FC):
                split_tile("ffn_up", turn, j)
                if starts(turn, j, 1):
                    norm_root(norm["ffn"])
                if j % 2 == 0:
                    act.wait_ge(ffn_evac, turn * RING + (j + 1))
                    act.activation(gated[:, j // 2 % 2, :], gated[:, j // 2 % 2, :], ACT.Silu).then_inc(gate_silu, 1)
                elif not starts(turn, j, 2):
                    act_high(turn, j // 2 - 1)
            act_high(0, FC - 1)
            n = norm["final"]

            def final_chunk(k):
                act.wait_ge(n.x_ready, k + 1)
                if k in POOL_OUT_CHUNKS:
                    act.activation(x_gained[:, k, :], x[:, k, :], ACT.Copy, scale=col("final_norm_2", k)).then_inc(gained, 1)
                if k >= 3:
                    act.wait_ge(n.summed, k - 2)
                act.activation(fin_sq[:, k % 2, :] if k else fin_sqsum[:], x[:, k, :], ACT.Square).then_inc(n.squared, 1)

            done = 0
            for k in range(FC):
                split_tile("ffn_down", 0, k)
                if done < DC and FC * (done + 1) <= 8 * (k - 1):
                    final_chunk(done)
                    done += 1
            for k in range(done, DC):
                final_chunk(k)
            norm_root(n)
            for k in OUT_ORDER[::2]:
                store(act, k)
            act.wait_ge(stored, 16 * DC)
            act.wait_ge(x_spilled, 16)

        @block.vector
        def _(dve):
            own = [0]

            def settle(instruction):
                own[0] += 1
                instruction.then_inc(steps, 1)
                dve.wait_ge(steps, own[0])

            def low_chunk(n, k, xg_hi, xg_lo, gain):
                dve.wait_ge(n.xg_hi, k + 1)
                dve.scalar_tensor_tensor(xg_lo[:, k, :], x[:, k, :], gain(k), plain(xg_hi[:, k, :]),
                                         ALU.mult, ALU.subtract).then_inc(n.xg_lo, 1)

            def sum_chunk(n, k, pairs):
                if k:
                    dve.wait_ge(n.squared, len(pairs) * (k + 1))
                    if k >= 2:
                        dve.wait_ge(n.summed, len(pairs) * (k - 1))
                    for total, square in pairs:
                        dve.tensor_tensor(total, total, square(k), ALU.add).then_inc(n.summed, 1)

            def norm_chunk(n, k, xg_hi, xg_lo, gain, pairs):
                low_chunk(n, k, xg_hi, xg_lo, gain)
                sum_chunk(n, k, pairs)

            def norm_mean(n, b, source_scale=1.0 / D):
                dve.wait_ge(n.mean, n.before + 1)
                settle(dve.tensor_scalar(mean_sq[:], b[:], source_scale, EPS, ALU.mult, ALU.add))
                dve.reciprocal(mean_sq[:], mean_sq[:]).then_inc(n.prepared, 1)

            def take_bank(stage, n, k):
                if stage != "ffn_down":
                    dve.wait_ge(tile_used, TILE[stage] + 2 * (k + 1))
                elif FC * (k + 1) % 8 == 0:
                    dve.wait_ge(tile_used, TILE[stage] + FC * (k + 1) // 8)
                else:
                    dve.wait_ge(chunk_done, sum(FC * (c + 1) % 8 != 0 for c in range(k + 1)))
                dve.tensor_tensor(x[:, k, :], bank[(k + 4) % 8][:], x[:, k, :], ALU.add).then_inc(n.x_ready, 1)

            def residual(stage, name, xg_hi, xg_lo, sq, sqsum, gain):
                n = norm[name]
                for k in range(DC + 1):
                    if k < DC:
                        take_bank(stage, n, k)
                    if k:
                        norm_chunk(n, k - 1, xg_hi, xg_lo, gain, [(sqsum[:], lambda c: sq[:, c % 2, :])])

            def rope_angles(i):
                if i == 0:
                    dve.wait_ge(pos_in, 16)
                    settle(dve.tensor_copy(angle[:], pos_i[:]))
                    settle(dve.tensor_scalar(angle[:], angle[:], col("inv_freq"), None, ALU.mult))
                settle(dve.tensor_scalar(turns_of[:], angle[:], 1.0 / TWO_PI, (0.0, 0.25)[i], ALU.mult, ALU.add))
                settle(dve.tensor_scalar(turns_of[:], turns_of[:], ROUNDER, None, ALU.add))
                settle(dve.tensor_scalar(turns_of[:], turns_of[:], ROUNDER, None, ALU.subtract))
                if i:
                    dve.wait_ge(table_done, 1)
                settle(dve.scalar_tensor_tensor(reduced[:], turns_of[:], -TWO_PI_PARTS[0], angle[:], ALU.mult, ALU.add))
                for part in TWO_PI_PARTS[1:]:
                    settle(dve.scalar_tensor_tensor(reduced[:], turns_of[:], -part, reduced[:], ALU.mult, ALU.add))
                if i:
                    settle(dve.tensor_scalar(reduced[:], reduced[:], TWO_PI / 4, None, ALU.add))
                dve.tensor_scalar(reduced[:], reduced[:], 3.1415925, -3.1415925, ALU.min, ALU.max).then_inc(angle_ready, 1)

            dve.memset(ones[:], 1.0).then_inc(made, 1)
            dve.wait_ge(patterns, 6)
            dve.tensor_copy(ident_r[:], ident[:]).then_inc(made, 1)
            dve.tensor_copy(mask_r[:], mask[:]).then_inc(made, 1)
            for i in range(2):
                dve.tensor_tensor(fold[:, ROPE * i:ROPE * (i + 1)], ident[:, 0:ROPE], ident[:, ROPE:P], ALU.add).then_inc(made, 1)
            dve.wait_ge(cols_in, 16)
            n = norm["pool"]
            for k in range(DC):
                low_chunk(n, k, pool_xg_hi, pool_xg_lo, lambda c: col("pool_norm", c))
            for k in range(DC):
                sum_chunk(n, k, [(pool_sqsum[:], lambda c: pool_sq[:, c % 2, :])])
            norm_mean(n, bank[MEAN_BANK])
            dve.wait_ge(small_in, 32)
            dve.tensor_tensor(gain12[:], cols[:, COLUMNS["final_norm"]:COLUMNS["final_norm"] + DC],
                              cols[:, COLUMNS["mix_norm"]:COLUMNS["mix_norm"] + DC], ALU.mult).then_inc(made, 1)
            for i in range(2):
                settle(dve.memset(u_pad[:, i, 0:PAD], 0.0))
            dve.wait_ge(n.inv, n.before + 1)

            def pooled_low(c):
                dve.wait_ge(pooled_hi_done, c + 1)
                dve.tensor_tensor(pooled_lo[:, c, :], pooled[:, c % 2, :], plain(pooled_hi[:, c, :]),
                                  ALU.subtract).then_inc(pooled_lo_done, 1)

            for c in range(PC):
                window = WINDOWS[c // PG]
                u = u_pad[:, c % 2, :]
                dve.wait_ge(tile_used, TILE["pool_u"] + c + 1)
                dve.tensor_tensor(u[:, PAD:], bank[c % 4][:], inv[:], ALU.mult).then_inc(in_evac, 1)
                dve.wait_ge(in_evac, c + 1)
                total, reach, spare = u, 1, (sum_a, sum_b)
                while reach < window:
                    target = spare[0]
                    settle(dve.tensor_tensor(target[:, 2 * reach:], total[:, 2 * reach:], total[:, reach:PAD + S - reach], ALU.add))
                    total, reach, spare = target, 2 * reach, spare[::-1]
                if c >= 2:
                    pooled_low(c - 2)
                    dve.wait_ge(pooled_lo_done, c - 1)
                dst = pooled[:, c % 2, :]
                edge = window - 1
                other = spare[0]
                dve.scalar_tensor_tensor(dst[:, edge:], total[:, PAD + edge:], 1.0 / window, u[:, PAD + edge:],
                                         ALU.mult, ALU.subtract)
                settle(dve.tensor_tensor(other[:, 0:edge], total[:, PAD:PAD + edge], counts[:, 0:edge], ALU.mult))
                dve.tensor_tensor(dst[:, 0:edge], other[:, 0:edge], u[:, PAD:PAD + edge], ALU.subtract).then_inc(pooled_ready, 1)
            for c in range(PC):
                dve.wait_ge(tile_used, TILE["pool_z"] + c + 1)
                dve.tensor_tensor(z[:, c, :], bank[c % 4][:], inv[:], ALU.mult).then_inc(in_evac, 1)
                if c < 2:
                    pooled_low(PC - 2 + c)
                if c in (4, 7):
                    rope_angles((c - 4) // 3)

            def y_low(c):
                dve.wait_ge(y_hi_done, c + 1)
                dve.tensor_tensor(y_lo[:, c, :], z[:, c, :], plain(y_hi[:, c, :]), ALU.subtract).then_inc(y_lo_done, 1)

            for c in range(PC):
                if c % 2:
                    dve.wait_ge(tile_used, TILE["pool_group"] + c // 2 + 1)
                else:
                    dve.wait_ge(half_tile, c // 2 + 1)
                dve.wait_ge(z_silu, c + 1)
                dve.scalar_tensor_tensor(z[:, c, :], bank[c % 4][:], col("pool_scale", c), z[:, c, :],
                                         ALU.mult, ALU.mult).then_inc(y_ready, 1)
                if c:
                    y_low(c - 1)
            y_low(PC - 1)
            residual("pool_out", "mla", mla_xg_hi, mla_xg_lo, mla_sq, mla_sqsum, lambda k: col("mla_norm", k))
            norm_mean(norm["mla"], bank[MEAN_BANK])
            dve.wait_ge(norm["mla"].inv, norm["mla"].before + 1)

            def unit_low(u):
                kind, g, j = u
                hi, lo = {"k": (k_hi, k_lo), "q": (q_hi, q_lo), "v": (v_hi, v_lo)}[kind]
                dve.wait_ge(unit_hi, hi_units(u))
                dve.tensor_tensor(lo[:, j, :], bank[UNIT_BANK[UNIT[u]]][:], plain(hi[:, j, :]), ALU.subtract).then_inc(unit_evac, 1)

            def turn_half(g, j):
                u = ("rope", g, j)
                source = bank[UNIT_BANK[UNIT[u]]][:]
                wait_unit(dve, u)
                if j == 0:
                    if g:
                        dve.wait_ge(turned_lo_done, 2 * g)
                        dve.wait_ge(turned_hi_done, 2 * g)
                    settle(dve.tensor_tensor(turned_1[:], source, cos[:], ALU.mult))
                    dve.tensor_tensor(turned_2[:], source, sin[:], ALU.mult).then_inc(unit_evac, 1)
                else:
                    settle(dve.tensor_tensor(rope_t[:], source, sin[:], ALU.mult))
                    dve.tensor_tensor(turned_1[:], turned_1[:], rope_t[:], ALU.subtract).then_inc(turned, 1)
                    dve.wait_ge(turned, 2 * g + 1)
                    dve.tensor_tensor(rope_t[:], source, cos[:], ALU.mult).then_inc(unit_evac, 1)
                    dve.wait_ge(unit_evac, UNIT[u] + 1)
                    dve.tensor_tensor(turned_2[:], turned_2[:], rope_t[:], ALU.add).then_inc(turned, 1)

            def turned_low(g):
                for i, t in enumerate((turned_1, turned_2)):
                    dve.wait_ge(turned_hi_done, 2 * g + i + 1)
                    dve.tensor_tensor(turned_lo[:, i, :], t[:], plain(turned_hi[:, i, :]), ALU.subtract).then_inc(turned_lo_done, 1)

            def prepare_tile(g, i):
                for kind, k in GROUP_TILES[i]:
                    if kind == "rope":
                        turn_half(g, k)
                    else:
                        unit_low((kind, g, k))

            for u in range(LC + 1 + PC):
                if u == EARLY:
                    prepare_tile(0, 0)
                dve.wait_ge(tile_used, TILE["mla_in"] + u + 1 + int(u >= EARLY))
                source = bank[u % 4][:]
                if u < LC:
                    dve.tensor_tensor(lat[:, u, :], source, inv[:], ALU.mult).then_inc(mla_evac, 1)
                elif u == LC:
                    dve.wait_ge(table_done, 2)
                    dve.tensor_tensor(rope_a[0:ROPE, :], bank[u % 4][0:ROPE, :], cos[0:ROPE, :], ALU.mult)
                    dve.scalar_tensor_tensor(rope_a[ROPE:P, :], bank[u % 4][ROPE:P, :], col("rope_sign")[ROPE:P, :],
                                             sin[ROPE:P, :], ALU.mult, ALU.mult).then_inc(mla_evac, 1)
                    dve.wait_ge(mla_evac, LC + 1)
                    dve.tensor_tensor(rope_a[:], rope_a[:], inv[:], ALU.mult).then_inc(rope_k_ready, 1)
                    for i, (first, last) in enumerate(((0, QC), (QC, LC))):
                        dve.wait_ge(lat_squared, last)
                        for c in range(first + 1, last):
                            t = dve.tensor_tensor(lat_sqsum[:, i, :], lat_sq[:, c, :],
                                                  lat_sq[:, first, :] if c == first + 1 else lat_sqsum[:, i, :], ALU.add)
                            if c < last - 1:
                                settle(t)
                            else:
                                t.then_inc(lat_summed, 1)
                else:
                    dve.tensor_tensor(z[:, u - LC - 1, :], source, inv[:], ALU.mult).then_inc(mla_evac, 1)
                if u == LC + 1:
                    for i, width in enumerate((QC * P, KC * P)):
                        dve.wait_ge(lat_mean, i + 1)
                        settle(dve.tensor_scalar(lat_sqsum[:, i, :], bank[6 + i][:], 1.0 / width, EPS, ALU.mult, ALU.add))
                        dve.reciprocal(lat_sqsum[:, i, :], lat_sqsum[:, i, :]).then_inc(lat_prepared, 1)
                if u == LC + 2:
                    dve.wait_ge(lat_inv, 2)
                    for c in range(LC):
                        dve.scalar_tensor_tensor(lat[:, c, :], lat[:, c, :], col("q_norm", c), lat_sqsum[:, int(c >= QC), :],
                                                 ALU.mult, ALU.mult).then_inc(lat_ready, 1)
                    dve.wait_ge(rope_k_hi_done, 1)
                    dve.tensor_tensor(rope_k_lo[:], bank[5][:], plain(rope_k_hi[:]), ALU.subtract).then_inc(rope_k_lo_done, 1)
                if u == LC + 4:
                    for c in range(LC):
                        dve.wait_ge(lat_hi_done, c + 1)
                        dve.tensor_tensor(lat_lo[:, c, :], lat[:, c, :], plain(lat_hi[:, c, :]), ALU.subtract).then_inc(lat_lo_done, 1)
                if u == EARLY:
                    turned_low(0)

            def peaks(s, h, scale, banks):
                for i in banks:
                    blocks = ((0, 1), (2,), (3,))[i]
                    dve.wait_ge(s.scores, 3 * h + i + 1)
                    for b in blocks:
                        t = dve.reduce_max(peak[:, h % 2, b:b + 1], bank[i][:, SCORE_AT[b]:SCORE_AT[b] + P * (b + 1)], X)
                    settle(t)
                    if h >= 2:
                        dve.wait_ge(s.exped, NB * (h - 1))
                    dve.tensor_scalar(neg_peak[:, h % 2, blocks[0]:blocks[-1] + 1], peak[:, h % 2, blocks[0]:blocks[-1] + 1],
                                      -scale, None, ALU.mult).then_inc(s.peaks, 1)

            def normalise(s, h, prob, before=0):
                dve.wait_ge(s.exped, NB * (h + 1))
                dve.reciprocal(inv_sum[:, h % 2, :], row_sum[:, h % 2, :]).then_inc(sum_inverted, 1)
                dve.wait_ge(sum_inverted, before + h + 1)
                for b in range(NB - 1):
                    dve.tensor_scalar(prob[:, ROW[b]:ROW[b + 1]], prob[:, ROW[b]:ROW[b + 1]], inv_sum[:, h % 2, b:b + 1],
                                      None, ALU.mult).then_inc(probs, 1)

            def transposed_low(s, h, hi, lo, blocks):
                for b in blocks:
                    dve.wait_ge(s.prob_t_hi, NB * h + b + 1)
                    dve.tensor_tensor(lo[:, COLUMN[b]:COLUMN[b + 1]], bank[3 + b % 2][:, 0:S - P * b],
                                      plain(hi[:, COLUMN[b]:COLUMN[b + 1]]), ALU.subtract).then_inc(s.prob_t_lo, 1)

            def prepare(g, j):
                for i in (j,) if j < GH - 1 else (j, GH):
                    prepare_tile(g, i)

            for j in range(1, GH):
                prepare_tile(0, j)
            peaks(mla, 0, MLA_SCALE, (0, 1, 2))
            normalise(mla, 0, prob)
            prepare_tile(0, GH)
            for h in range(HEADS):
                g, j = h // GH + 1, h % GH
                transposed_low(mla, h, prob_t_hi, prob_t_lo, (0, 1))
                if h + 1 < HEADS:
                    peaks(mla, h + 1, MLA_SCALE, (0,))
                transposed_low(mla, h, prob_t_hi, prob_t_lo, (2, 3))
                if h + 1 < HEADS:
                    peaks(mla, h + 1, MLA_SCALE, (1, 2))
                    normalise(mla, h + 1, prob)
                dve.wait_ge(mla.weighted, h + 1)
                dve.wait_ge(mz_silu, h + 1)
                dve.tensor_tensor(z[:, h, :], bank[5][:], z[:, h, :], ALU.mult).then_inc(mla.out, 1)
                if g < GROUPS:
                    if j == 1:
                        turned_low(g)
                    prepare(g, j)

            n = norm["mix"]
            dve.wait_ge(x_back, 16)
            pairs = [(mix_sqsum[:, i, :], lambda c, i=i: mix_sq[:, c % 2, i, :]) for i in range(2)]
            for k in range(DC + 1):
                if k < DC:
                    take_bank("mla_out", n, k)
                if k:
                    norm_chunk(n, k - 1, mix_xg_hi, mix_xg_lo, lambda c: gain12[:, c:c + 1], pairs)
            dve.wait_ge(n.mean, n.before + 1)
            settle(dve.tensor_scalar(mean_sq[:], bank[6][:], 1.0 / D, EPS, ALU.mult, ALU.add))
            dve.reciprocal(mean_sq[:], mean_sq[:]).then_inc(n.prepared, 1)
            dve.wait_ge(n.inv, n.before + 1)
            dve.wait_ge(n.mean, n.before + 2)
            settle(dve.tensor_tensor(mean_sq[:], bank[7][:], inv_1[:], ALU.mult))
            settle(dve.tensor_tensor(mean_sq[:], mean_sq[:], inv_1[:], ALU.mult))
            settle(dve.tensor_scalar(mean_sq[:], mean_sq[:], 1.0 / D, EPS, ALU.mult, ALU.add))
            dve.reciprocal(mean_sq[:], mean_sq[:]).then_inc(n.prepared, 1)
            dve.wait_ge(n.inv, n.before + 2)
            dve.tensor_tensor(inv[:], inv[:], inv_1[:], ALU.mult).then_inc(inv_both, 1)
            dve.wait_ge(inv_both, 1)

            def qk_low(u):
                hi, lo = (fq_hi, fq_lo) if u < 4 else (fk_hi, fk_lo)
                dve.wait_ge(qk_hi, u + 1)
                dve.tensor_tensor(lo[:, u % 4, :], qk_t[:, u % 2, :], plain(hi[:, u % 4, :]), ALU.subtract).then_inc(qk_lo, 1)

            for u in range(9):
                dve.wait_ge(tile_used, TILE["mix_qk"] + u + 1)
                m = u if u < 4 else u - 1
                if u == 4:
                    dve.tensor_tensor(f_t[:], bank[0][:], inv[:], ALU.mult).then_inc(f_ready, 1)
                else:
                    if m >= 2:
                        qk_low(m - 2)
                        dve.wait_ge(qk_lo, m - 1)
                    dve.scalar_tensor_tensor(qk_t[:, m % 2, :], bank[u % 4][:], FOX_D ** -0.5 if m < 4 else 1.0, inv[:],
                                             ALU.mult, ALU.mult).then_inc(qk_ready, 1)
                if u < DC:
                    scaled = dve.scalar_tensor_tensor(x[:, u, :], x[:, u, :], col("final_norm", u), inv_1[:], ALU.mult, ALU.mult)
                    if u == DC - 1:
                        scaled.then_inc(x_scaled, 1)
                if u == 1:
                    dve.wait_ge(ws_in, 16)
                    w = ws_raw[:].rearrange("p (g i) -> p g i", g=SGU_G)
                    dve.memset(w[SGU_HALF:P, :, 0:SGU_HALF], 0.0).then_inc(ws_cut, 1)
                if u == 2:
                    dve.memset(plain(decay_q[:]), 1.0)
                    dve.memset(plain(decay_k[:]), 1.0).then_inc(decay_ones, 1)
                if u == 3:
                    dve.wait_ge(inv_t_sum, 1)
                    dve.tensor_copy(inv_t[:], bank[5][:, 0:NB]).then_inc(inv_t_ready, 1)
                if u == 5:
                    dve.wait_ge(f_summed, 1)
                    for b in range(NB):
                        t = dve.tensor_tensor(gate[:, b, :], bank[5][:, 8 * b:8 * b + 8], b_f[:], ALU.add)
                    settle(t)
                    dve.scalar_tensor_tensor(gate_abs[:], gate[:], -1.0, gate[:], ALU.mult, ALU.max).then_inc(gate_abs_ready, 1)
                    settle(dve.tensor_scalar(gate[:], gate[:], 0.0, None, ALU.min))
                if u == 7:
                    dve.wait_ge(gate_log, 1)
                    dve.tensor_tensor(log_f[:], gate[:], gate_abs[:], ALU.subtract).then_inc(log_f_ready, 1)
            qk_low(6)
            qk_low(7)
            dve.wait_ge(c_hi_done, 1)
            settle(dve.tensor_tensor(c_parts[:, 1, :], bank[6][0:FOX_HEADS, :], plain(c_parts[:, 0, :]), ALU.subtract))
            dve.tensor_scalar(c_parts[:, 2:4, :], plain(c_parts[:, 0:2, :]), -1.0, None, ALU.mult).then_inc(c_ready, 1)
            dve.wait_ge(ws_hi_done, 1)
            dve.tensor_tensor(ws_lo[:], ws_raw[:], plain(ws_hi[:]), ALU.subtract).then_inc(ws_lo_done, 1)
            dve.wait_ge(inv_t_ready, 1)
            for b in range(NB):
                dve.wait_ge(fv_hi_done, b + 1)
                dve.scalar_tensor_tensor(fv_lo[:, b, :], bank[b][:], inv_t[:, b:b + 1], plain(fv_hi[:, b, :]),
                                         ALU.mult, ALU.subtract).then_inc(fv_lo_done, 1)

            def attn_low(pair):
                dve.wait_ge(attn_hi_done, pair + 1)
                dve.scalar_tensor_tensor(attn_lo[:, pair, :], attn[:, pair, :], col("out_norm", pair), plain(attn_hi[:, pair, :]),
                                         ALU.mult, ALU.subtract).then_inc(attn_lo_done, 1)

            def gate_groups(groups):
                dve.wait_ge(z_gelu, 2)
                for g in groups:
                    dve.wait_ge(sgu_mixed, g // 2 * 2 + 2)
                    mine = zu[:, :, SGU_D * g:SGU_D * (g + 1)]
                    at = NB * SGU_D * (g % 2)
                    dve.scalar_tensor_tensor(mine, bank[6 + g // 2 % 2][:, at:at + NB * SGU_D].rearrange("p (b d) -> p b d", b=NB),
                                             col("b_s", g), mine, ALU.add, ALU.mult).then_inc(sgu_gated, 1)

            peaks(fox, 0, 1.0, (0, 1, 2))
            normalise(fox, 0, f_prob, HEADS)
            for h in range(FOX_HEADS):
                transposed_low(fox, h, f_prob_t_hi, f_prob_t_lo, (0, 1))
                if h + 1 < FOX_HEADS:
                    peaks(fox, h + 1, 1.0, (0,))
                transposed_low(fox, h, f_prob_t_hi, f_prob_t_lo, (2, 3))
                if h + 1 < FOX_HEADS:
                    peaks(fox, h + 1, 1.0, (1, 2))
                    normalise(fox, h + 1, f_prob, HEADS)
                dve.wait_ge(fox.weighted, h + 1)
                rows = slice(FOX_D * (h % 2), FOX_D * (h % 2 + 1))
                dve.tensor_copy(attn[rows, h // 2, :], bank[5][rows, :]).then_inc(fox.out, 1)
                if h == 3:
                    dve.wait_ge(z_gelu, 1)
                    for b in range(NB):
                        t = dve.bn_stats(stats[:, b, :], zv[:, b, :])
                    settle(t)
                    for b in range(NB):
                        t = dve.bn_aggr(moments[:, b, :], stats[:, b:b + 1, :])
                    settle(t)
                    settle(dve.tensor_scalar(rstd[:], moments[:, :, 1], EPS, None, ALU.add))
                    dve.reciprocal(rstd[:], rstd[:]).then_inc(ln_prepared, 1)
                if h == 4:
                    dve.wait_ge(ln_rstd, 1)
                    for b in range(NB):
                        dve.tensor_scalar(zv[:, b, :], zv[:, b, :], moments[:, b, 0:1], rstd[:, b:b + 1],
                                          ALU.subtract, ALU.mult).then_inc(ln_centred, 1)
                if h % 2 == 0 and h:
                    attn_low(h // 2 - 1)
            gate_groups(range(SGU_G))
            attn_low(FOX_PAIRS - 1)
            for pair in range(1, FOX_PAIRS):
                dve.wait_ge(attn_squared, pair + 1)
                t = dve.tensor_tensor(attn_sqsum[:], attn_sq[:, 0, :] if pair == 1 else attn_sqsum[:], attn_sq[:, pair, :], ALU.add)
                if pair < FOX_PAIRS - 1:
                    settle(t)
            t.then_inc(attn_summed, 1)
            dve.wait_ge(branch_squared, NB)
            settle(dve.tensor_scalar(branch_inv[:], branch_sq[:], 1.0 / D_SGU, EPS, ALU.mult, ALU.add))
            dve.reciprocal(branch_inv[:], branch_inv[:]).then_inc(branch_prepared, 1)
            dve.wait_ge(branch_inv_done, 1)
            for b in range(NB):
                dve.tensor_scalar(zu[:, b, :], zu[:, b, :], branch_inv[:, b:b + 1], None, ALU.mult).then_inc(branch_scaled, 1)
            dve.wait_ge(attn_mean, 1)
            settle(dve.tensor_scalar(attn_inv[:], bank[5][:], 1.0 / D_ATTN, EPS, ALU.mult, ALU.add))
            dve.reciprocal(attn_inv[:], attn_inv[:]).then_inc(attn_prepared, 1)
            for c in range(SC):
                dve.wait_ge(sgu_hi_done, c + 1)
                dve.scalar_tensor_tensor(sgu_lo[:, c, :], bank[6 + c % 2][:], col("out_norm", AC + c), plain(sgu_hi[:, c, :]),
                                         ALU.mult, ALU.subtract).then_inc(sgu_lo_done, 1)
            dve.wait_ge(attn_inv_done, 1)
            n = norm["ffn"]
            for k in range(DC + 1):
                if k < DC:
                    dve.wait_ge(tile_used, TILE["mix_out"] + k + 1)
                    t = mixed[:, k % 2, :]
                    settle(dve.tensor_tensor(t, bank[k % 4][:], attn_inv[:], ALU.mult))
                    settle(dve.tensor_tensor(t, t, bank[4 + k % 4][:], ALU.add))
                    dve.tensor_tensor(x[:, k, :], t, x[:, k, :], ALU.add).then_inc(n.x_ready, 1)
                if k:
                    norm_chunk(n, k - 1, ffn_xg_hi, ffn_xg_lo, lambda c: col("ffn_norm", c),
                               [(ffn_sqsum[:], lambda c: ffn_sq[:, c % 2, :])])

            norm_mean(norm["ffn"], bank[MEAN_BANK])
            dve.wait_ge(norm["ffn"].inv, norm["ffn"].before + 1)

            def act_low(turn, n):
                index = turn * 2 + n
                dve.wait_ge(act_hi_done, index + 1)
                dve.tensor_tensor(act_lo[:, index, :], up[:, n % 2, :], plain(act_hi[:, index, :]), ALU.subtract).then_inc(act_lo_done, 1)

            for turn, j in sweep(dve, 2 * FC):
                dve.wait_ge(tile_used, turn * RING + (TILE["ffn_up"] + j + 1))
                n = j // 2
                if j % 2 == 0:
                    dve.tensor_tensor(gated[:, n % 2, :], bank[j % 4][:], inv[:], ALU.mult).then_inc(ffn_evac, 1)
                    if not starts(turn, j, 4):
                        act_low(turn, n - 2)
                else:
                    if not starts(turn, j, 4):
                        dve.wait_ge(act_lo_done, turn * 2 + (n - 1))
                    dve.tensor_tensor(up[:, n % 2, :], bank[j % 4][:], inv[:], ALU.mult).then_inc(ffn_evac, 1)
                    dve.wait_ge(ffn_evac, turn * RING + (j + 1))
                    dve.wait_ge(gate_silu, turn * 2 + (n + 1))
                    dve.tensor_tensor(up[:, n % 2, :], up[:, n % 2, :], gated[:, n % 2, :], ALU.mult).then_inc(act_ready, 1)
            act_low(0, FC - 2)
            act_low(0, FC - 1)
            n = norm["final"]
            for k in range(DC):
                take_bank("ffn_down", n, k)
                if k:
                    dve.wait_ge(n.squared, k + 1)
                    if k >= 2:
                        dve.wait_ge(n.summed, k - 1)
                    dve.tensor_tensor(fin_sqsum[:], fin_sqsum[:], fin_sq[:, k % 2, :], ALU.add).then_inc(n.summed, 1)
            norm_mean(n, bank[0])
            dve.wait_ge(n.inv, n.before + 1)
            for k in DVE_OUT_CHUNKS:
                dve.scalar_tensor_tensor(x[:, k, :], x[:, k, :], col("final_norm_2", k), inv[:], ALU.mult, ALU.mult).then_inc(out_ready, 1)

        @block.tensor
        def _(pe):
            def three(target, a_hi, a_lo, b_hi, b_lo, start, stop):
                pe.matmul(target, a_hi, b_hi, start=start, stop=False)
                pe.matmul(target, a_hi, b_lo, start=False, stop=False)
                return pe.matmul(target, a_lo, b_hi, start=False, stop=stop)

            def wblock(t, i, width=P):
                return w_hi[:, t % RING, width * i:width * (i + 1)], w_lo[:, t % RING, width * i:width * (i + 1)]

            def wait_tile(turn, t):
                pe.wait_ge(tile_lo, turn * RING + (t + 1))

            def projection(stage, turn, j, b, xg_hi, xg_lo, xg_lo_done=None):
                t = TILE[stage] + j
                wait_tile(turn, t)
                for k in range(DC):
                    if xg_lo_done is not None:
                        pe.wait_ge(xg_lo_done, k + 1)
                    last = three(b[:], *wblock(t, k), xg_hi[:, k, :], xg_lo[:, k, :], k == 0, k == DC - 1)
                last.then_inc(tile_used, 1)

            def mean(sem_in, value, total, b, sem_out):
                pe.wait_ge(sem_in, value)
                pe.matmul(b[:], ones[:], total, start=True, stop=True).then_inc(sem_out, 1)

            def out_product(stage, before):
                for turn, j in sweep(pe, PC, tail=PC):
                    t = TILE[stage] + j
                    wait_tile(turn, t)
                    for i in range(8):
                        k = 8 * (j % 2) + i
                        if j < 2:
                            pe.wait_ge(y_lo_done, before + k + 1)
                        last = three(bank[(j // 2 + 4) % 8][:], *wblock(t, i), y_hi[:, k, :], y_lo[:, k, :], k == 0, k == PC - 1)
                    last.then_inc(tile_used, 1)

            n = norm["pool"]
            for turn, j in sweep(pe, PC):
                if not starts(turn, j, 4):
                    pe.wait_ge(in_evac, turn * RING + (j - 3))
                projection("pool_u", turn, j, bank[j % 4], pool_xg_hi, pool_xg_lo, n.xg_lo if starts(turn, j, 1) else None)
                if starts(turn, j, 2) and j == 1:
                    pe.wait_ge(made, 1)
                    mean(n.summed, DC - 1, pool_sqsum[:], bank[MEAN_BANK], n.mean)
            for turn, j in sweep(pe, PC):
                pe.wait_ge(in_evac, turn * RING + (PC + j - 3))
                projection("pool_z", turn, j, bank[j % 4], pool_xg_hi, pool_xg_lo)
            for i in range(PC * PG // 8):
                t = TILE["pool_group"] + i
                wait_tile(0, t)
                group = i // 2
                pe.wait_ge(pooled_lo_done, PG * (group + 1))
                for half in range(2):
                    c = 2 * i + half
                    if c < 4:
                        pe.wait_ge(in_evac, 2 * PC - 4 + c + 1)
                    else:
                        pe.wait_ge(y_ready, c - 3)
                    for k in range(PG):
                        last = three(bank[c % 4][:], *wblock(t, PG * half + k), pooled_hi[:, PG * group + k, :],
                                     pooled_lo[:, PG * group + k, :], k == 0, k == PG - 1)
                    last.then_inc(tile_used if half else half_tile, 1)
            out_product("pool_out", 0)

            def unit(u):
                kind, g, j = u
                i = UNIT[u]
                before = [n for n in range(i) if UNIT_BANK[n] == UNIT_BANK[i]]
                if before:
                    pe.wait_ge(unit_evac, before[-1] + 1)
                elif i == 4:
                    pe.wait_ge(mla_evac, LC + 1 + PC)
                t = unit_tile(u)
                wait_tile(0, t)
                b = bank[UNIT_BANK[i]]
                if kind == "v":
                    for c in range(KC):
                        hi, lo = wblock(t, c, S)
                        a = slice(P * j, P * (j + 1))
                        last = three(b[:], lat_hi[:, QC + c, a], lat_lo[:, QC + c, a], hi, lo, c == 0, c == KC - 1)
                else:
                    first, chunks, base = QC if kind == "k" else 0, CHUNKS_OF[kind], unit_place(kind, j)[1]
                    for c in range(chunks):
                        last = three(b[:], *wblock(t, base + c), lat_hi[:, first + c, :], lat_lo[:, first + c, :],
                                     c == 0, c == chunks - 1)
                last.then_inc(tile_used if ends_tile(u) else unit_done, 1)

            def prepare_tile(g, i):
                for kind, k in GROUP_TILES[i]:
                    unit((kind, g, k))

            pe.wait_ge(made, 5)
            n = norm["mla"]
            for u in range(LC + 1 + PC):
                if u < 4:
                    pe.wait_ge(n.x_ready, u + 5)
                else:
                    pe.wait_ge(mla_evac, u - 3)
                if u == EARLY:
                    pe.wait_ge(lat_lo_done, LC)
                    pe.wait_ge(rope_k_lo_done, 1)
                    prepare_tile(0, 0)
                projection("mla_in", 0, u + int(u >= EARLY), bank[u % 4], mla_xg_hi, mla_xg_lo, n.xg_lo if u == 0 else None)
                if u == 0:
                    mean(n.summed, DC - 1, mla_sqsum[:], bank[MEAN_BANK], n.mean)
                if u == LC + 1:
                    pe.wait_ge(rope_k_ready, 1)
                    pe.matmul(bank[5][:], fold[:], rope_a[:], start=True, stop=True).then_inc(rope_k_summed, 1)
                    for i in range(2):
                        mean(lat_summed, i + 1, lat_sqsum[:, i, :], bank[6 + i], lat_mean)

            def causal_mask(target, b):
                return pe.matmul(target[:, P * b:P * (b + 1)], ident_r[:], mask_r[:], start=False, stop=True)

            def scores_mla(h, blocks):
                g, j = divmod(h, GH)
                pe.wait_ge(unit_evac, UNIT[("q", g, j if h else GH - 1)] + 1)
                if j == 0:
                    pe.wait_ge(rope_q_in, 256 * (g + 1))
                for b in blocks:
                    i, at, n = SCORE_BANK[b], SCORE_AT[b], P * (b + 1)
                    if h and b != 1:
                        pe.wait_ge(mla.exped, NB * (h - 1) + (2, 3, 4)[i])
                    target = bank[i][:, at:at + n]
                    a = slice(P * b, P * (b + 1))
                    three(target, q_hi[:, j, a], q_lo[:, j, a], k_hi[:, j, 0:n], k_lo[:, j, 0:n], True, False)
                    pe.matmul(target, rope_q[:, g % 2, j, a], rope_k_hi[:, 0:n], start=False, stop=False)
                    pe.matmul(target, rope_q[:, g % 2, j, a], rope_k_lo[:, 0:n], start=False, stop=False)
                    last = causal_mask(target, b)
                    if b:
                        last.then_inc(mla.scores, 1)

            def transposes(s, h, source, ready, value, blocks):
                pe.wait_ge(ready, value)
                for b in blocks:
                    if NB * h + b >= 2:
                        pe.wait_ge(s.prob_t_lo, NB * h + b - 1)
                    for q in range(b, NB):
                        last = pe.transpose(bank[3 + b % 2][:, P * (q - b):P * (q - b + 1)],
                                            source[:, ROW[q] + P * b:ROW[q] + P * (b + 1)], ident[:])
                    last.then_inc(s.transposed, 1)

            def weigh_mla(h):
                if h:
                    pe.wait_ge(mla.out, h)
                j = h % GH
                pe.wait_ge(unit_evac, UNIT[("v", h // GH, NB - 1)] + 1)
                for b in range(NB):
                    pe.wait_ge(mla.prob_t_lo, NB * h + b + 1)
                    a = slice(VD * j, VD * (j + 1))
                    r = slice(COLUMN[b], COLUMN[b + 1])
                    last = three(bank[5][:, P * b:S], v_hi[:, b, a], v_lo[:, b, a], prob_t_hi[:, r], prob_t_lo[:, r],
                                 b == 0, b == NB - 1)
                last.then_inc(mla.weighted, 1)

            def prepare(g, j):
                for i in (j,) if j < GH - 1 else (j, GH):
                    prepare_tile(g, i)

            for j in range(1, GH):
                prepare_tile(0, j)
            scores_mla(0, range(NB))
            prepare_tile(0, GH)
            for h in range(HEADS):
                g, j = h // GH + 1, h % GH
                for blocks in ((0, 1), (2, 3)):
                    transposes(mla, h, prob, probs, NB * (h + 1), blocks)
                    if h + 1 < HEADS:
                        scores_mla(h + 1, blocks)
                weigh_mla(h)
                if g < GROUPS:
                    prepare(g, j)
            out_product("mla_out", PC)

            n = norm["mix"]
            for u in range(9):
                if u == 8:
                    pe.wait_ge(f_ready, 1)
                elif u >= 4:
                    pe.wait_ge(qk_ready, u - 3)
                else:
                    pe.wait_ge(n.x_ready, u + 5)
                projection("mix_qk", 0, u, bank[u % 4], mix_xg_hi, mix_xg_lo, n.xg_lo if u == 0 else None)
                if u == 0:
                    for i in range(2):
                        mean(n.summed, 2 * (DC - 1), mix_sqsum[:, i, :], bank[6 + i], n.mean)
                if u == 3:
                    pe.wait_ge(inv_both, 1)
                    for b in range(NB):
                        last = pe.matmul(bank[5][:, b:b + 1], inv[0:1, P * b:P * (b + 1)], ones[0:1, 0:1], start=True, stop=True)
                    last.then_inc(inv_t_sum, 1)
                if u == 5:
                    pe.wait_ge(f_ready, 1)
                    pe.wait_ge(inv_t_ready, 1)
                    for b in range(NB):
                        last = pe.transpose(bank[5][:, 8 * b:8 * b + 8], f_t[0:FOX_HEADS, P * b:P * (b + 1)],
                                            ident[0:FOX_HEADS, 0:FOX_HEADS])
                    last.then_inc(f_summed, 1)
                if u == 8:
                    pe.wait_ge(log_f_ready, 1)
                    for t in range(NB):
                        for b in range(t + 1):
                            last = pe.matmul(bank[6][0:FOX_HEADS, P * t:P * (t + 1)], log_f[:, b, :],
                                             (upper if b == t else ones)[:], start=b == 0, stop=b == t)
                    last.then_inc(c_summed, 1)
            for i in range(4):
                t = TILE["mix_v"] + i
                wait_tile(0, t)
                for b in range(NB):
                    if i == 0:
                        pe.wait_ge(qk_ready, (8, 5, 6, 7)[b])
                    for c in range(2):
                        k = 2 * i + c
                        a = slice(P * b, P * (b + 1))
                        last = three(bank[b][:], mix_xg_hi[:, k, a], mix_xg_lo[:, k, a], *wblock(t, c, S), k == 0, k == DC - 1)
                    if i == 3 and b < NB - 1:
                        last.then_inc(v_summed, 1)
                last.then_inc(tile_used, 1)

            def sgu_tile(i):
                t = TILE["mix_z"] + i
                wait_tile(0, t)
                if i % 2 == 0 and i:
                    pe.wait_ge(z_evac, NB * (i // 2))
                for b in range(NB):
                    a = slice(P * b, P * (b + 1))
                    at = D_SGU // 2 * (b % 2)
                    for c in range(4):
                        k = 4 * (i % 2) + c
                        last = three(bank[6 + b // 2][:, at:at + D_SGU // 2], mix_xg_hi[:, k, a], mix_xg_lo[:, k, a],
                                     *wblock(t, c, D_SGU // 2), k == 0 and b % 2 == 0, k == DC - 1 and b % 2 == 1)
                last.then_inc(tile_used, 1)

            def sgu_mix(groups):
                for g in groups:
                    if g >= 4:
                        pe.wait_ge(sgu_gated, g // 2 * 2 - 2)
                    c = slice(SGU_D * g, SGU_D * (g + 1))
                    w = slice(P * g, P * (g + 1))
                    at = NB * SGU_D * (g % 2)
                    three(bank[6 + g // 2 % 2][:, at:at + NB * SGU_D].rearrange("p (b d) -> p b d", b=NB), ws_hi[:, w],
                          ws_lo[:, w], zvn_hi[:, :, c], zvn_lo[:, :, c], True, True).then_inc(sgu_mixed, 1)

            def scores_fox(h, banks):
                pair, half = divmod(h, 2)
                rows = slice(FOX_D * half, FOX_D * (half + 1))
                r = 32 * (h % 4)
                for i in banks:
                    blocks = ((0, 1), (2,), (3,))[i]
                    if h:
                        pe.wait_ge(fox.exped, NB * (h - 1) + (2, 3, 4)[i])
                    for b in blocks:
                        n = P * (b + 1)
                        target = bank[i][:, SCORE_AT[b]:SCORE_AT[b] + n]
                        a = slice(P * b, P * (b + 1))
                        three(target, fq_hi[rows, pair, a], fq_lo[rows, pair, a], fk_hi[rows, pair, 0:n],
                              fk_lo[rows, pair, 0:n], True, False)
                        pe.matmul(target, decay_q[r:r + 4, h // 4, a], decay_k[r:r + 4, h // 4, 0:n], start=False, stop=False)
                        last = causal_mask(target, b)
                    last.then_inc(fox.scores, 1)

            def weigh_fox(h):
                if h:
                    pe.wait_ge(fox.out, h)
                a = slice(P * (h // 2), P * (h // 2 + 1))
                for b in range(NB):
                    pe.wait_ge(fox.prob_t_lo, NB * h + b + 1)
                    r = slice(COLUMN[b], COLUMN[b + 1])
                    last = three(bank[5][:, P * b:S], fv_hi[:, b, a], fv_lo[:, b, a], f_prob_t_hi[:, r], f_prob_t_lo[:, r],
                                 b == 0, b == NB - 1)
                last.then_inc(fox.weighted, 1)

            pe.wait_ge(c_ready, 1)
            sgu_tile(0)
            pe.wait_ge(fv_lo_done, NB)
            pe.wait_ge(decay_in, 8 * 16)
            pe.wait_ge(qk_lo, 8)
            scores_fox(0, (0, 1, 2))
            sgu_tile(1)
            for h in range(FOX_HEADS):
                for blocks, banks in (((0, 1), (0,)), ((2, 3), (1, 2))):
                    transposes(fox, h, f_prob, probs, NB * (HEADS + h + 1), blocks)
                    if h + 1 < FOX_HEADS:
                        scores_fox(h + 1, banks)
                if h == FOX_HEADS - 1:
                    pe.wait_ge(ws_lo_done, 1)
                    pe.wait_ge(zvn_lo_done, NB)
                    pe.wait_ge(z_evac, 4 * NB)
                    sgu_mix(range(4))
                weigh_fox(h)
                if h < 6:
                    sgu_tile(2 + h)
            sgu_mix(range(4, SGU_G))

            for first in (0, 4):
                for n in range(first, first + 4):
                    t = TILE["mix_out"] + n
                    wait_tile(0, t)
                    if first:
                        pe.wait_ge(norm["ffn"].x_ready, n - 3)
                    for k in range(AC):
                        if n == 0:
                            pe.wait_ge(attn_lo_done, k + 1)
                        last = three(bank[n % 4][:], *wblock(t, k), attn_hi[:, k, :], attn_lo[:, k, :], k == 0, k == AC - 1)
                    if n == 1:
                        mean(attn_summed, 1, attn_sqsum[:], bank[5], attn_mean)
                if first == 0:
                    for c in range(SC):
                        if c == 0:
                            pe.wait_ge(branch_scaled, NB)
                        if c >= 2:
                            pe.wait_ge(sgu_lo_done, c - 1)
                        for b in range(NB):
                            last = pe.transpose(bank[6 + c % 2][:, P * b:P * (b + 1)], zu[:, b, P * c:P * (c + 1)], ident[:])
                        last.then_inc(branch_t, 1)
                    pe.wait_ge(attn_prepared, 1)
                for n in range(first, first + 4):
                    t = TILE["mix_out"] + n
                    for k in range(SC):
                        if n == 0:
                            pe.wait_ge(sgu_lo_done, k + 1)
                        last = three(bank[4 + n % 4][:], *wblock(t, AC + k), sgu_hi[:, k, :], sgu_lo[:, k, :], k == 0, k == SC - 1)
                    last.then_inc(tile_used, 1)

            n = norm["ffn"]
            for turn, j in sweep(pe, 2 * FC):
                if starts(turn, j, 4):
                    pe.wait_ge(n.x_ready, j + 5)
                else:
                    pe.wait_ge(ffn_evac, turn * RING + (j - 3))
                projection("ffn_up", turn, j, bank[j % 4], ffn_xg_hi, ffn_xg_lo, n.xg_lo if starts(turn, j, 1) else None)
                if starts(turn, j, 1):
                    mean(n.summed, DC - 1, ffn_sqsum[:], bank[MEAN_BANK], n.mean)
            for n in range(DC):
                for k in range(FC):
                    block_n = FC * n + k
                    t = TILE["ffn_down"] + block_n // 8
                    if block_n % 8 == 0:
                        wait_tile(0, t)
                    if n == 0:
                        pe.wait_ge(act_lo_done, k + 1)
                    last = three(bank[(n + 4) % 8][:], *wblock(t, block_n % 8), act_hi[:, k, :], act_lo[:, k, :], k == 0, k == FC - 1)
                    if block_n % 8 == 7:
                        last.then_inc(tile_used, 1)
                    elif k == FC - 1:
                        last.then_inc(chunk_done, 1)
            mean(norm["final"].summed, DC - 1, fin_sqsum[:], bank[0], norm["final"].mean)


def kernel(x, positions, pool_norm, pool_w_in, pool_w_group, pool_scale, pool_w_out, mla_norm, mla_w_in,
           mla_q_norm, mla_w_q_b, mla_kv_norm, mla_w_kv_b, mla_w_out, final_norm, mix_norm_g_2, w_in_2, b_f_2,
           sgu_ln_g_2, sgu_ln_b_2, w_s_2, b_s_2, out_norm_g_2, w_out_2, ffn_norm_g_2, w_gate_up_2, w_down_2,
           final_norm_g_2):
    import concourse.bacc as bacc
    from concourse.bass_utils import run_bass_kernel_spmd

    (x, positions, pool_norm, pool_w_in, pool_w_group, pool_scale, pool_w_out, mla_norm, mla_w_in, mla_q_norm,
     mla_w_q_b, mla_kv_norm, mla_w_kv_b, mla_w_out, mix_norm, w_in, b_f, ln_g, ln_b, w_s, b_s, out_norm, w_out,
     ffn_norm, w_gate_up, w_down) = (
        np.asarray(a)[0] for a in (
            x, positions, pool_norm, pool_w_in, pool_w_group, pool_scale, pool_w_out, mla_norm, mla_w_in,
            mla_q_norm, mla_w_q_b, mla_kv_norm, mla_w_kv_b, mla_w_out, mix_norm_g_2, w_in_2, b_f_2, sgu_ln_g_2,
            sgu_ln_b_2, w_s_2, b_s_2, out_norm_g_2, w_out_2, ffn_norm_g_2, w_gate_up_2, w_down_2))
    final_norm, final_norm_2 = np.asarray(final_norm), np.asarray(final_norm_g_2)

    stream = np.zeros((N_TILES, P, 8 * P), np.float32)

    def put(tile, at, part):
        stream[tile, :, at:at + part.shape[1]] = part

    def rows(w, k):
        return w[P * k:P * (k + 1)]

    def outputs(tile, w, at=0):
        for k in range(w.shape[0] // P):
            put(tile, at + P * k, rows(w, k))

    for n in range(2 * PC):
        outputs(TILE["pool_u"] + n, pool_w_in[:, P * n:P * (n + 1)])
    for c in range(PC):
        g, n = divmod(c, PG)
        outputs(TILE["pool_group"] + c // 2, pool_w_group[g][:, P * n:P * (n + 1)], PG * P * (c % 2))
    for name, w in (("pool_out", pool_w_out), ("mla_out", mla_w_out), ("ffn_down", w_down)):
        chunks = w.shape[0] // P
        for n in range(DC):
            for k in range(chunks):
                i = chunks * n + k
                put(TILE[name] + i // 8, P * (i % 8), rows(w, k)[:, P * n:P * (n + 1)])
    t = TILE["mla_in"]
    for n in range(LC):
        outputs(t + n, mla_w_in[:, P * n:P * (n + 1)])
    half_1 = mla_w_in[:, LC * P:LC * P + HALF]
    half_2 = mla_w_in[:, LC * P + HALF:LC * P + ROPE]
    outputs(t + LC, np.concatenate([half_1, half_2, half_2, half_1], axis=1))
    for n in range(PC):
        at = LC * P + ROPE + P * n
        outputs(t + LC + 1 + n + int(LC + 1 + n >= EARLY), mla_w_in[:, at:at + P])
    w_q = mla_w_q_b.reshape(QC * P, HEADS, NOPE + ROPE)
    w_kv = mla_w_kv_b.reshape(KC * P, HEADS, NOPE + VD)
    for g in range(GROUPS):
        group = slice(GH * g, GH * (g + 1))
        for tile in GROUP_TILES[:GH]:
            for kind, j in tile:
                i, block = unit_place(kind, j)
                w = {"k": lambda: w_kv[:, GH * g + j, 0:NOPE],
                     "q": lambda: w_q[:, GH * g + j, 0:NOPE],
                     "rope": lambda: w_q[:, group, NOPE + HALF * j:NOPE + HALF * (j + 1)].reshape(QC * P, P)}[kind]()
                outputs(group_tile(g, i), w, P * block)
        w_v = w_kv[:, group, NOPE:].reshape(KC * P, S)
        for k in range(KC):
            put(group_tile(g, GH), S * k, rows(w_v, k))
    gates = 3 * D_ATTN
    for n in range(8):
        outputs(TILE["mix_qk"] + n + (n >= 4), w_in[:, P * n:P * (n + 1)])
    for k in range(DC):
        put(TILE["mix_qk"] + 4, P * k, rows(w_in, k)[:, gates:gates + FOX_HEADS])
        put(TILE["mix_v"] + k // 2, S * (k % 2), rows(w_in, k)[:, 2 * D_ATTN:gates])
    quarter = D_SGU // 2
    for c in range(4):
        at = gates + FOX_HEADS + (D_SGU if c < 2 else 0) + quarter * (c % 2)
        for k in range(DC):
            put(TILE["mix_z"] + 2 * c + k // 4, quarter * (k % 4), rows(w_in, k)[:, at:at + quarter])
    for n in range(DC):
        outputs(TILE["mix_out"] + n, w_out[:, P * n:P * (n + 1)])
    for n in range(FC):
        outputs(TILE["ffn_up"] + 2 * n, w_gate_up[:, P * n:P * (n + 1)])
        outputs(TILE["ffn_up"] + 2 * n + 1, w_gate_up[:, FF + P * n:FF + P * (n + 1)])

    def as_columns(v):
        return v.reshape(-1, P).T

    inv_freq = (1.0 / (10000.0 ** (np.arange(0, ROPE, 2, dtype=np.float32) / np.float32(ROPE)))).astype(np.float32)
    sign = np.repeat(np.array([-1, 1, -1, 1], np.float32), HALF)
    columns = np.concatenate([as_columns(v) for v in (
        pool_norm, pool_scale, mla_norm, mla_q_norm, mla_kv_norm, final_norm, mix_norm, out_norm, ffn_norm,
        final_norm_2, b_s, np.tile(inv_freq, GH), sign)], axis=1)
    counts = np.tile((1.0 / np.arange(1, PAD + 1)).astype(np.float32), (P, 1))
    lines = np.tile(np.concatenate([b_f, ln_g, ln_b]), (P, 1))
    arrays = {
        "x_in": x.T.reshape(DC, P, S).transpose(1, 0, 2),
        "stream": stream,
        "columns": columns,
        "counts_in": counts,
        "positions_in": np.tile(positions, (P, 1)),
        "lines": lines,
        "w_s": w_s.transpose(2, 0, 1).reshape(P, SGU_G * P),
    }
    arrays = {k: np.ascontiguousarray(v) for k, v in arrays.items()}

    nc = bacc.Bacc("TRN2", target_bir_lowering=False, num_devices=1)
    args = [nc.dram_tensor(k, v.shape, mybir.dt.from_np(v.dtype), kind="ExternalInput").ap() for k, v in arrays.items()]
    spill = nc.dram_tensor("spill", (P, DC, S), mybir.dt.float32, kind="Internal").ap()
    out = nc.dram_tensor("out", (P, DC, S), mybir.dt.float32, kind="ExternalOutput").ap()
    build(nc, *args, spill, out)
    r = run_bass_kernel_spmd(nc, [arrays], core_ids=[0])
    return r.results[0]["out"].transpose(1, 0, 2).reshape(D, S).T.reshape(1, S, D)
```
